# Optimizing a Trainium2 kernel written in Bass

```python
import jax, jax.numpy as jnp
from jax import lax
import numpy as np
import math

D_MODEL = 1024
BATCH = 1
SEQ = 512
DEPTH = 2

N_A = DEPTH // 2
N_B = DEPTH - N_A
N_VRES = max(N_A - 1, 0)
HEAD_DIM = 64
N_HEADS = D_MODEL // HEAD_DIM
D_FF = 4 * D_MODEL
DECAY_LORA = 64
AAA_LORA = 64
MV_LORA = 32
GATE_LORA = 160
Q_BLOCK = 128
N_MOD = 6
NORM_EPS = 1e-6
GN_EPS = 64e-5
L2_EPS = 1e-12


def rms_norm(x, g):
    xf = x.astype(jnp.float32)
    y = xf * lax.rsqrt(jnp.mean(xf * xf, axis=-1, keepdims=True) + NORM_EPS)
    return (y * g.astype(jnp.float32)).astype(x.dtype)

def modulate(h, shift, scale):
    return h * (1.0 + scale) + shift

def token_shift(x):
    return jnp.pad(x, ((0, 0), (1, 0), (0, 0)))[:, :-1, :]

def split_heads(t):
    return t.reshape(t.shape[0], t.shape[1], N_HEADS, HEAD_DIM)

def wkv7_scan(r, decay, k, v, a_vec, b_vec):
    bsz = r.shape[0]
    xs = tuple(jnp.moveaxis(t.astype(jnp.float32), 1, 0) for t in (r, decay, k, v, a_vec, b_vec))

    def step(S, inp):
        r_t, w_t, k_t, v_t, a_t, b_t = inp
        sa = jnp.einsum('bhvk,bhk->bhv', S, a_t)
        S = S * w_t[:, :, None, :] + sa[..., :, None] * b_t[..., None, :] + v_t[..., :, None] * k_t[..., None, :]
        y = jnp.einsum('bhvk,bhk->bhv', S, r_t)
        return S, y

    S0 = jnp.zeros((bsz, N_HEADS, HEAD_DIM, HEAD_DIM), jnp.float32)
    _, ys = lax.scan(step, S0, xs)
    return jnp.moveaxis(ys, 0, 1)

def rwkv7_time_mix(h, v_first, vres, mu, wr, wk, wv, wo, w0, w1, w2, a0, a1, a2,
                   g1, g2, k_k, k_a, r_k, ln_w, ln_b):
    bsz, T, _ = h.shape
    xx = token_shift(h) - h
    xr, xw, xk, xv, xa, xg = (h + xx * mu[j] for j in range(6))
    r = xr @ wr
    w_log = -jax.nn.softplus(-(w0 + jnp.tanh(xw @ w1) @ w2)) - 0.5
    k = xk @ wk
    v = xv @ wv
    if vres is None:
        v_first = v
    else:
        v0, v1, v2 = vres
        v = v + (v_first - v) * jax.nn.sigmoid(v0 + (xv @ v1) @ v2)
    a = jax.nn.sigmoid(a0 + (xa @ a1) @ a2)
    g = jax.nn.sigmoid(xg @ g1) @ g2
    kk = split_heads(k * k_k).astype(jnp.float32)
    kk = kk / jnp.maximum(jnp.sqrt(jnp.sum(kk * kk, axis=-1, keepdims=True)), L2_EPS)
    k = k * (1.0 + (a - 1.0) * k_a)
    decay = jnp.exp(-jnp.exp(w_log.astype(jnp.float32)))
    rh, kh, vh = split_heads(r), split_heads(k), split_heads(v)
    ah = split_heads(a).astype(jnp.float32)
    y = wkv7_scan(rh, split_heads(decay), kh, vh, -kk, kk * ah)
    mean = jnp.mean(y, axis=-1, keepdims=True)
    var = jnp.mean(jnp.square(y - mean), axis=-1, keepdims=True)
    y = ((y - mean) * lax.rsqrt(var + GN_EPS)).reshape(bsz, T, D_MODEL)
    y = y * ln_w.astype(jnp.float32) + ln_b.astype(jnp.float32)
    bonus = jnp.sum((rh * kh * r_k).astype(jnp.float32), axis=-1, keepdims=True) * vh.astype(jnp.float32)
    y = (y + bonus.reshape(bsz, T, D_MODEL)).astype(h.dtype)
    return (y * g) @ wo, v_first

def shared_kv(x, shift, scale, norm_g, w_kv, f_bias, k_gain):
    h = modulate(rms_norm(x, norm_g), shift, scale)
    kvf = h @ w_kv
    k = kvf[..., :D_MODEL]
    v = kvf[..., D_MODEL:2 * D_MODEL]
    f_logit = kvf[..., 2 * D_MODEL:]
    k = rms_norm(split_heads(k), k_gain)
    log_f = jax.nn.log_sigmoid(f_logit.astype(jnp.float32) + f_bias.astype(jnp.float32))
    F = jnp.cumsum(log_f, axis=1)
    return (k.transpose(0, 2, 1, 3), split_heads(v).transpose(0, 2, 1, 3).astype(jnp.float32),
            F.transpose(0, 2, 1))

def forgetting_attention(h, k, v, F, w_qg, q_gain, w_o):
    bsz, T, _ = h.shape
    qg = h @ w_qg
    q, gate = qg[..., :D_MODEL], qg[..., D_MODEL:]
    q = rms_norm(split_heads(q), q_gain).transpose(0, 2, 1, 3)
    sm_scale = HEAD_DIM ** -0.5
    kpos = jnp.arange(T)

    def block(start):
        qb = lax.dynamic_slice_in_dim(q, start, Q_BLOCK, axis=2)
        Fq = lax.dynamic_slice_in_dim(F, start, Q_BLOCK, axis=2)
        s = jnp.einsum('bhqd,bhkd->bhqk', qb, k).astype(jnp.float32) * sm_scale
        s = s + Fq[..., :, None] - F[..., None, :]
        qpos = start + jnp.arange(Q_BLOCK)
        s = jnp.where(kpos[None, :] <= qpos[:, None], s, -jnp.inf)
        p = jax.nn.softmax(s, axis=-1)
        return jnp.einsum('bhqk,bhkd->bhqd', p, v)

    starts = jnp.arange(T // Q_BLOCK) * Q_BLOCK
    o = lax.map(block, starts)
    o = o.transpose(1, 0, 3, 2, 4).reshape(bsz, T, D_MODEL).astype(h.dtype)
    return (o * jax.nn.sigmoid(gate)) @ w_o

def sq_relu_mlp(h, w_up, w_down):
    return jnp.square(jax.nn.relu(h @ w_up)) @ w_down

def first_inputs(seed: int = 0) -> dict:
    key = jax.random.key(seed)
    keys = iter(jax.random.split(key, 48))
    f32 = jnp.float32

    def nrm(shape, scale):
        return jax.random.normal(next(keys), shape, f32) * scale

    def unif(shape, lo, hi):
        return jax.random.uniform(next(keys), shape, f32, lo, hi)

    D = D_MODEL
    return {
        'x': nrm((BATCH, SEQ, D), 1.0),
        'c': nrm((BATCH, D), 1.0),
        'mod_w': nrm((DEPTH, D, N_MOD * D), 0.2 * D ** -0.5),
        'mod_b': nrm((DEPTH, N_MOD * D), 0.01),
        'norm_mix_g': 1.0 + nrm((DEPTH, D), 0.02),
        'norm_mlp_g': 1.0 + nrm((DEPTH, D), 0.02),
        'mlp_up': nrm((DEPTH, D, D_FF), D ** -0.5),
        'mlp_down': nrm((DEPTH, D_FF, D), D_FF ** -0.5),
        'rw_mu': unif((N_A, 6, D), 0.0, 1.0),
        'rw_wr': nrm((N_A, D, D), D ** -0.5),
        'rw_wk': nrm((N_A, D, D), D ** -0.5),
        'rw_wv': nrm((N_A, D, D), D ** -0.5),
        'rw_wo': nrm((N_A, D, D), D ** -0.5),
        'rw_w0': unif((N_A, D), -6.0, 0.0),
        'rw_w1': nrm((N_A, D, DECAY_LORA), D ** -0.5),
        'rw_w2': nrm((N_A, DECAY_LORA, D), 0.1 * DECAY_LORA ** -0.5),
        'rw_a0': nrm((N_A, D), 0.1),
        'rw_a1': nrm((N_A, D, AAA_LORA), D ** -0.5),
        'rw_a2': nrm((N_A, AAA_LORA, D), 0.1 * AAA_LORA ** -0.5),
        'rw_g1': nrm((N_A, D, GATE_LORA), D ** -0.5),
        'rw_g2': nrm((N_A, GATE_LORA, D), GATE_LORA ** -0.5),
        'rw_kk': 0.85 + nrm((N_A, D), 0.02),
        'rw_ka': 1.0 + nrm((N_A, D), 0.02),
        'rw_rk': nrm((N_A, N_HEADS, HEAD_DIM), 0.1),
        'rw_lnw': 1.0 + nrm((N_A, D), 0.02),
        'rw_lnb': nrm((N_A, D), 0.01),
        'rw_v0': 1.0 + nrm((N_VRES, D), 0.02),
        'rw_v1': nrm((N_VRES, D, MV_LORA), D ** -0.5),
        'rw_v2': nrm((N_VRES, MV_LORA, D), 0.1 * MV_LORA ** -0.5),
        'kv_norm_g': 1.0 + nrm((D,), 0.02),
        'kv_mod_w': nrm((D, 2 * D), 0.2 * D ** -0.5),
        'kv_mod_b': nrm((2 * D,), 0.01),
        'kv_w': nrm((D, 2 * D + N_HEADS), D ** -0.5),
        'kv_fb': unif((N_HEADS,), 1.0, 5.0),
        'kv_kg': 1.0 + nrm((HEAD_DIM,), 0.02),
        'fx_wqg': nrm((N_B, D, 2 * D), D ** -0.5),
        'fx_qg': 1.0 + nrm((N_B, HEAD_DIM), 0.02),
        'fx_wo': nrm((N_B, D, D), D ** -0.5),
        'final_g': 1.0 + nrm((D,), 0.02),
    }

def first_block(x, c, mod_w, mod_b, norm_mix_g, norm_mlp_g, mlp_up, mlp_down,
              rw_mu, rw_wr, rw_wk, rw_wv, rw_wo, rw_w0, rw_w1, rw_w2, rw_a0, rw_a1, rw_a2,
              rw_g1, rw_g2, rw_kk, rw_ka, rw_rk, rw_lnw, rw_lnb, rw_v0, rw_v1, rw_v2,
              kv_norm_g, kv_mod_w, kv_mod_b, kv_w, kv_fb, kv_kg,
              fx_wqg, fx_qg, fx_wo, final_g):
    c_act = jax.nn.silu(c)
    v_first = None
    k_sh = v_sh = F_sh = None
    for i in range(DEPTH):
        mod = (c_act @ mod_w[i] + mod_b[i])[:, None, :]
        sh1, sc1, gt1, sh2, sc2, gt2 = jnp.split(mod, N_MOD, axis=-1)
        if i == N_A:
            kvm = (c_act @ kv_mod_w + kv_mod_b)[:, None, :]
            kv_shift, kv_scale = jnp.split(kvm, 2, axis=-1)
            k_sh, v_sh, F_sh = shared_kv(x, kv_shift, kv_scale, kv_norm_g, kv_w, kv_fb, kv_kg)
        h = modulate(rms_norm(x, norm_mix_g[i]), sh1, sc1)
        if i < N_A:
            vres = None if i == 0 else (rw_v0[i - 1], rw_v1[i - 1], rw_v2[i - 1])
            y, v_first = rwkv7_time_mix(h, v_first, vres, rw_mu[i], rw_wr[i], rw_wk[i], rw_wv[i], rw_wo[i],
                                        rw_w0[i], rw_w1[i], rw_w2[i], rw_a0[i], rw_a1[i], rw_a2[i],
                                        rw_g1[i], rw_g2[i], rw_kk[i], rw_ka[i], rw_rk[i],
                                        rw_lnw[i], rw_lnb[i])
        else:
            j = i - N_A
            y = forgetting_attention(h, k_sh, v_sh, F_sh, fx_wqg[j], fx_qg[j], fx_wo[j])
        x = x + (1.0 + gt1) * y
        h = modulate(rms_norm(x, norm_mlp_g[i]), sh2, sc2)
        x = x + (1.0 + gt2) * sq_relu_mlp(h, mlp_up[i], mlp_down[i])
    return rms_norm(x, final_g)


DEPTH_2 = 1

DN_HEADS = 8
DN_HEAD_DIM = 128
DN_WIDTH = DN_HEADS * DN_HEAD_DIM
CONV_K = 5
CHUNK = 64
MLA_HEADS = 8
Q_LORA = 512
KV_LORA = 256
NOPE_DIM = 128
ROPE_DIM = 64
V_DIM = 128
QK_DIM = NOPE_DIM + ROPE_DIM
MLA_WIDTH = MLA_HEADS * V_DIM
ROPE_THETA = 10000.0
N_EXPERTS = 16
CAPACITY_FACTOR = 2
D_EXPERT = 1024
N_BRANCHES = 2
EPS = 1e-6

IN_SPLITS = (3 * DN_WIDTH,
             DN_WIDTH,
             2 * DN_HEADS,
             2 * DN_HEADS,
             Q_LORA,
             KV_LORA,
             ROPE_DIM,
             N_BRANCHES * D_MODEL)
N_IN = sum(IN_SPLITS)


def rms_norm_2(x, g):
    xf = x.astype(jnp.float32)
    y = xf * lax.rsqrt(jnp.mean(xf * xf, axis=-1, keepdims=True) + EPS)
    return (y * g.astype(jnp.float32)).astype(x.dtype)

def l2_norm(x):
    return x * lax.rsqrt(jnp.sum(x * x, axis=-1, keepdims=True) + EPS)

def apply_rope(x, cos, sin):
    x1, x2 = jnp.split(x.astype(jnp.float32), 2, axis=-1)
    return jnp.concatenate([x1 * cos - x2 * sin, x2 * cos + x1 * sin], axis=-1).astype(x.dtype)

def centred_depthwise_conv(x, w):
    ch = x.shape[-1]
    pad = (CONV_K - 1) // 2
    return lax.conv_general_dilated(x, w[:, None, :].astype(x.dtype), window_strides=(1,),
                                    padding=[(pad, pad)], dimension_numbers=('NWC', 'WIO', 'NWC'),
                                    feature_group_count=ch)

def chunk_gated_delta_rule(q, k, v, g, beta):
    b, h, s, dk = k.shape
    dv = v.shape[-1]
    nc = s // CHUNK
    q = q * (dk ** -0.5)
    qc = q.reshape(b, h, nc, CHUNK, dk)
    kc = k.reshape(b, h, nc, CHUNK, dk)
    vc = v.reshape(b, h, nc, CHUNK, dv)
    bc = beta.reshape(b, h, nc, CHUNK)
    gc = jnp.cumsum(g.reshape(b, h, nc, CHUNK), axis=-1)
    tril = jnp.tril(jnp.ones((CHUNK, CHUNK), dtype=bool))
    strict = jnp.tril(jnp.ones((CHUNK, CHUNK), dtype=bool), -1)
    diff = gc[..., :, None] - gc[..., None, :]
    decay = jnp.where(tril, jnp.exp(jnp.where(tril, diff, 0.0)), 0.0)
    k_beta = kc * bc[..., None]
    v_beta = vc * bc[..., None]
    lower = jnp.where(strict, jnp.einsum('bhnik,bhnjk->bhnij', k_beta, kc) * decay, 0.0)
    eye = jnp.eye(CHUNK, dtype=jnp.float32)
    t_inv = lax.linalg.triangular_solve(eye + lower, jnp.broadcast_to(eye, lower.shape),
                                        left_side=True, lower=True, unit_diagonal=True)
    u = t_inv @ v_beta
    w = t_inv @ (k_beta * jnp.exp(gc)[..., None])
    intra = jnp.where(tril, jnp.einsum('bhnik,bhnjk->bhnij', qc, kc) * decay, 0.0)
    q_dec = qc * jnp.exp(gc)[..., None]
    g_last = gc[..., -1]
    k_state = kc * jnp.exp(g_last[..., None] - gc)[..., None]

    def step(state, xs):
        w_i, u_i, intra_i, qd_i, ks_i, gl_i = xs
        v_new = u_i - w_i @ state
        o_i = qd_i @ state + intra_i @ v_new
        state = state * jnp.exp(gl_i)[..., None, None] + jnp.swapaxes(ks_i, -1, -2) @ v_new
        return state, o_i

    xs = tuple(jnp.moveaxis(t, 2, 0) for t in (w, u, intra, q_dec, k_state, g_last))
    state0 = jnp.zeros((b, h, dk, dv), jnp.float32)
    _, o = lax.scan(step, state0, xs)
    return jnp.moveaxis(o, 0, 2).reshape(b, h, s, dv)

def gated_deltanet_branch(qkv, z, b_in, a_in, conv_w, a_log, dt_bias, o_gain):
    bsz, s, _ = qkv.shape
    qkv = jax.nn.silu(centred_depthwise_conv(qkv, conv_w))
    q, k, v = jnp.split(qkv, 3, axis=-1)

    def heads(t):
        return t.reshape(bsz, s, DN_HEADS, DN_HEAD_DIM).transpose(0, 2, 1, 3).astype(jnp.float32)

    q, k, v = l2_norm(heads(q)), l2_norm(heads(k)), heads(v)
    beta = jax.nn.sigmoid(b_in.astype(jnp.float32)).reshape(bsz, s, 2, DN_HEADS).transpose(2, 0, 3, 1)
    a = a_in.astype(jnp.float32).reshape(bsz, s, 2, DN_HEADS)
    g = -jnp.exp(a_log.astype(jnp.float32)) * jax.nn.softplus(a + dt_bias.astype(jnp.float32))
    g = g.transpose(2, 0, 3, 1)
    o_fwd = chunk_gated_delta_rule(q, k, v, g[0], beta[0])
    flip = lambda t: jnp.flip(t, axis=2)
    o_bwd = flip(chunk_gated_delta_rule(flip(q), flip(k), flip(v), flip(g[1]), flip(beta[1])))
    o = (o_fwd + o_bwd).transpose(0, 2, 1, 3)
    zf = z.astype(jnp.float32).reshape(bsz, s, DN_HEADS, DN_HEAD_DIM)
    o = rms_norm_2(o, o_gain) * jax.nn.silu(zf)
    return o.reshape(bsz, s, DN_WIDTH).astype(qkv.dtype)

def mla_branch(c_q, c_kv, k_r, q_gain, w_uq, kv_gain, w_ukv, cos, sin):
    bsz, s, _ = c_q.shape
    q = (rms_norm_2(c_q, q_gain) @ w_uq).reshape(bsz, s, MLA_HEADS, QK_DIM)
    q = jnp.concatenate([q[..., :NOPE_DIM],
                         apply_rope(q[..., NOPE_DIM:], cos[:, :, None], sin[:, :, None])], axis=-1)
    kv = (rms_norm_2(c_kv, kv_gain) @ w_ukv).reshape(bsz, s, MLA_HEADS, NOPE_DIM + V_DIM)
    k_nope, v = kv[..., :NOPE_DIM], kv[..., NOPE_DIM:]
    k_rope = apply_rope(k_r, cos, sin)
    k = jnp.concatenate([k_nope, jnp.broadcast_to(k_rope[:, :, None], (bsz, s, MLA_HEADS, ROPE_DIM))], axis=-1)
    qb = (q * (QK_DIM ** -0.5)).reshape(bsz, s // Q_BLOCK, Q_BLOCK, MLA_HEADS, QK_DIM).transpose(1, 0, 2, 3, 4)

    def attend(q_blk):
        scores = jnp.einsum('bqhd,bkhd->bhqk', q_blk, k, preferred_element_type=jnp.float32)
        p = jax.nn.softmax(scores, axis=-1)
        return jnp.einsum('bhqk,bkhd->bqhd', p.astype(v.dtype), v)

    o = lax.map(attend, qb)
    return o.transpose(1, 0, 2, 3, 4).reshape(bsz, s, MLA_WIDTH)

def expert_choice_ffn(h, w_router, w_gate, w_up, w_down):
    bsz, s, d = h.shape
    cap = CAPACITY_FACTOR * s // N_EXPERTS
    aff = jax.nn.softmax((h @ w_router).astype(jnp.float32), axis=-1)
    gate, idx = lax.top_k(aff.transpose(0, 2, 1), cap)
    idx_flat = idx.reshape(bsz, N_EXPERTS * cap)
    xe = jnp.take_along_axis(h, idx_flat[..., None], axis=1).reshape(bsz, N_EXPERTS, cap, d)
    hid = jax.nn.silu(jnp.einsum('becd,edf->becf', xe, w_gate)) * jnp.einsum('becd,edf->becf', xe, w_up)
    ye = jnp.einsum('becf,efd->becd', hid, w_down) * gate[..., None].astype(h.dtype)
    out = jnp.zeros_like(h).at[jnp.arange(bsz)[:, None], idx_flat].add(ye.reshape(bsz, N_EXPERTS * cap, d))
    return out

def second_inputs(seed: int = 0) -> dict:
    key = jax.random.key(seed)
    ks = jax.random.split(key, 24)
    f32 = jnp.float32

    def nrm(k, shape, fan_in):
        return jax.random.normal(k, shape, f32) * (fan_in ** -0.5)

    def gain(k, shape):
        return 1.0 + 0.05 * jax.random.normal(k, shape, f32)

    x = jax.random.normal(ks[0], (BATCH, SEQ, D_MODEL), f32)
    c = jax.random.normal(ks[1], (BATCH, D_MODEL), f32)
    positions = (jnp.cumsum(jax.random.randint(ks[2], (BATCH, SEQ), 1, 3), axis=1) - 1).astype(jnp.int32)
    w_mod = 0.5 * nrm(ks[3], (DEPTH_2, D_MODEL, N_MOD * D_MODEL), D_MODEL)
    b_mod = 0.02 * jax.random.normal(ks[4], (DEPTH_2, N_MOD * D_MODEL), f32)
    g_mix = gain(ks[5], (DEPTH_2, D_MODEL))
    w_in = nrm(ks[6], (DEPTH_2, D_MODEL, N_IN), D_MODEL)
    conv_w = nrm(ks[7], (DEPTH_2, CONV_K, 3 * DN_WIDTH), CONV_K)
    a_log = jnp.log(jax.random.uniform(ks[8], (DEPTH_2, 2, DN_HEADS), f32, 1.0, 16.0))
    dt = jnp.exp(jax.random.uniform(ks[9], (DEPTH_2, 2, DN_HEADS), f32, math.log(1e-3), math.log(1e-1)))
    dt_bias = dt + jnp.log(-jnp.expm1(-dt))
    dn_o_gain = gain(ks[10], (DEPTH_2, DN_HEAD_DIM))
    q_gain = gain(ks[11], (DEPTH_2, Q_LORA))
    w_uq = nrm(ks[12], (DEPTH_2, Q_LORA, MLA_HEADS * QK_DIM), Q_LORA)
    kv_gain = gain(ks[13], (DEPTH_2, KV_LORA))
    w_ukv = nrm(ks[14], (DEPTH_2, KV_LORA, MLA_HEADS * (NOPE_DIM + V_DIM)), KV_LORA)
    w_o_dn = nrm(ks[15], (DEPTH_2, DN_WIDTH, D_MODEL), DN_WIDTH)
    w_o_mla = nrm(ks[16], (DEPTH_2, MLA_WIDTH, D_MODEL), MLA_WIDTH)
    w_out = nrm(ks[17], (DEPTH_2, D_MODEL, D_MODEL), D_MODEL)
    g_ffn = gain(ks[18], (DEPTH_2, D_MODEL))
    w_router = nrm(ks[19], (DEPTH_2, D_MODEL, N_EXPERTS), D_MODEL)
    w_gate = nrm(ks[20], (DEPTH_2, N_EXPERTS, D_MODEL, D_EXPERT), D_MODEL)
    w_up = nrm(ks[21], (DEPTH_2, N_EXPERTS, D_MODEL, D_EXPERT), D_MODEL)
    w_down = nrm(ks[22], (DEPTH_2, N_EXPERTS, D_EXPERT, D_MODEL), D_EXPERT)
    g_final = gain(ks[23], (D_MODEL,))
    return {'x': x, 'c': c, 'positions': positions, 'w_mod': w_mod, 'b_mod': b_mod, 'g_mix': g_mix,
            'w_in': w_in, 'conv_w': conv_w, 'a_log': a_log, 'dt_bias': dt_bias, 'dn_o_gain': dn_o_gain,
            'q_gain': q_gain, 'w_uq': w_uq, 'kv_gain': kv_gain, 'w_ukv': w_ukv, 'w_o_dn': w_o_dn,
            'w_o_mla': w_o_mla, 'w_out': w_out, 'g_ffn': g_ffn, 'w_router': w_router, 'w_gate': w_gate,
            'w_up': w_up, 'w_down': w_down, 'g_final': g_final}

def second_block(x, c, positions, w_mod, b_mod, g_mix, w_in, conv_w, a_log, dt_bias, dn_o_gain,
              q_gain, w_uq, kv_gain, w_ukv, w_o_dn, w_o_mla, w_out, g_ffn, w_router, w_gate,
              w_up, w_down, g_final):
    half = ROPE_DIM // 2
    inv_freq = ROPE_THETA ** (-jnp.arange(half, dtype=jnp.float32) / half)
    ang = positions.astype(jnp.float32)[..., None] * inv_freq
    cos, sin = jnp.cos(ang), jnp.sin(ang)
    split_at = np.cumsum(IN_SPLITS)[:-1].tolist()
    for l in range(DEPTH_2):
        mod = jax.nn.silu(c) @ w_mod[l] + b_mod[l]
        sh1, sc1, gt1, sh2, sc2, gt2 = jnp.split(mod[:, None, :], N_MOD, axis=-1)
        h = rms_norm_2(x, g_mix[l]) * (1.0 + sc1) + sh1
        proj = h @ w_in[l]
        dn_qkv, dn_z, dn_b, dn_a, c_q, c_kv, k_r, gates = jnp.split(proj, split_at, axis=-1)
        y_dn = gated_deltanet_branch(dn_qkv, dn_z, dn_b, dn_a, conv_w[l], a_log[l], dt_bias[l],
                                     dn_o_gain[l]) @ w_o_dn[l]
        y_mla = mla_branch(c_q, c_kv, k_r, q_gain[l], w_uq[l], kv_gain[l], w_ukv[l], cos, sin) @ w_o_mla[l]
        g_dn, g_mla = jnp.split(jax.nn.sigmoid(gates), N_BRANCHES, axis=-1)
        merged = g_dn * y_dn + g_mla * y_mla
        x = x + gt1 * (merged @ w_out[l])
        h = rms_norm_2(x, g_ffn[l]) * (1.0 + sc2) + sh2
        x = x + gt2 * expert_choice_ffn(h, w_router[l], w_gate[l], w_up[l], w_down[l])
    return rms_norm_2(x, g_final)


def setup_inputs(seed=0):
    out = dict(first_inputs(seed))
    for name, value in second_inputs(seed + 1).items():
        if name != "x":
            out[name + "_2"] = value
    return out


def reference(
    x, c, mod_w, mod_b, norm_mix_g, norm_mlp_g, mlp_up, mlp_down, rw_mu, rw_wr, rw_wk, rw_wv,
    rw_wo, rw_w0, rw_w1, rw_w2, rw_a0, rw_a1, rw_a2, rw_g1, rw_g2, rw_kk, rw_ka, rw_rk, rw_lnw,
    rw_lnb, rw_v0, rw_v1, rw_v2, kv_norm_g, kv_mod_w, kv_mod_b, kv_w, kv_fb, kv_kg, fx_wqg,
    fx_qg, fx_wo, final_g, c_2, positions_2, w_mod_2, b_mod_2, g_mix_2, w_in_2, conv_w_2,
    a_log_2, dt_bias_2, dn_o_gain_2, q_gain_2, w_uq_2, kv_gain_2, w_ukv_2, w_o_dn_2, w_o_mla_2,
    w_out_2, g_ffn_2, w_router_2, w_gate_2, w_up_2, w_down_2, g_final_2,
):
    x = first_block(
        x, c, mod_w, mod_b, norm_mix_g, norm_mlp_g, mlp_up, mlp_down, rw_mu, rw_wr, rw_wk,
        rw_wv, rw_wo, rw_w0, rw_w1, rw_w2, rw_a0, rw_a1, rw_a2, rw_g1, rw_g2, rw_kk, rw_ka,
        rw_rk, rw_lnw, rw_lnb, rw_v0, rw_v1, rw_v2, kv_norm_g, kv_mod_w, kv_mod_b, kv_w, kv_fb,
        kv_kg, fx_wqg, fx_qg, fx_wo, final_g,
    )
    return second_block(
        x, c_2, positions_2, w_mod_2, b_mod_2, g_mix_2, w_in_2, conv_w_2, a_log_2, dt_bias_2,
        dn_o_gain_2, q_gain_2, w_uq_2, kv_gain_2, w_ukv_2, w_o_dn_2, w_o_mla_2, w_out_2,
        g_ffn_2, w_router_2, w_gate_2, w_up_2, w_down_2, g_final_2,
    )


_drawn_inputs = setup_inputs


def setup_inputs(seed=0):
    import zlib

    import numpy as np

    out = dict(_drawn_inputs(seed))
    spreads = {}
    factors = {'rw_w1': 8.0,
     'rw_w2': 8.0,
     'rw_kk': 5.01,
     'rw_ka': 4.448,
     'rw_lnw': 4.926,
     'rw_lnb': 8.0,
     'kv_norm_g': 8.0,
     'kv_mod_b': 8.0,
     'kv_kg': 8.0,
     'fx_qg': 8.0,
     'final_g': 2.766,
     'b_mod_2': 3.941,
     'g_mix_2': 5.59,
     'a_log_2': 2.767,
     'dn_o_gain_2': 7.481,
     'q_gain_2': 8.0,
     'w_uq_2': 4.487,
     'kv_gain_2': 8.0,
     'g_ffn_2': 4.936}
    for name, (base, spread) in spreads.items():
        noise = np.random.default_rng([zlib.crc32(name.encode()), seed]).standard_normal(out[name].shape)
        drawn = base * np.exp(spread * noise) if base else spread * noise
        out[name] = __import__('jax').numpy.asarray(drawn.astype(out[name].dtype))
    for name, factor in factors.items():
        out[name] = (out[name] * factor).astype(out[name].dtype)
    return out
```

```python
import numpy as np
from contextlib import ExitStack
import concourse.bass as bass
from concourse import mybir

F32 = mybir.dt.float32
I32 = mybir.dt.int32
ALU = mybir.AluOpType
ACT = mybir.ActivationFunctionType
AX = mybir.AxisListType.X
P = 128
T = 512
D = 1024
KT = 8
EXPM05 = float(np.exp(-0.5))
MUL, ADD, SUB = ALU.mult, ALU.add, ALU.subtract


class Queue:

    def __init__(self, sem, serial=False):
        self.sem, self.n, self.items, self.past, self.serial = sem, 0, [], {}, serial

    def wait(self, *marks):
        for m in marks:
            if m is None:
                continue
            if isinstance(m, list):
                self.wait(*m)
                continue
            sem, v = m
            if self.past.get(id(sem), 0) < v:
                self.past[id(sem)] = v
                self.items.append((sem, v))

    def __call__(self, fn, *marks):
        self.wait(*marks)
        if self.serial and self.n:
            self.wait((self.sem, self.n))
        self.n += 1
        sem = self.sem
        self.items.append(lambda e: fn(e).then_inc(sem, 1))
        return (sem, self.n)

    def silent(self, fn, *marks):
        self.wait(*marks)
        self.items.append(fn)

    def dma(self, sem, count, fn, *marks):
        self.wait(*marks)
        self.items.append(lambda e: fn(e).then_inc(sem, 16))
        return (sem, count)

    def play(self, eng):
        for it in self.items:
            if isinstance(it, tuple):
                eng.wait_ge(it[0], it[1])
            else:
                it(eng)


def weave(*streams):
    live = list(streams)
    while live:
        for s in list(live):
            if next(s, StopIteration) is StopIteration:
                live.remove(s)


def run(stream):
    for _ in stream:
        pass


VECS = [
    ("c", 8), ("c_2", 8), ("mod_b0", 48), ("mod_b1", 48), ("kv_mod_b", 16), ("b_mod_2", 48),
    ("norm_mix_g0", 8), ("norm_mix_g1", 8), ("norm_mlp_g0", 8), ("norm_mlp_g1", 8),
    ("rw_mu", 48), ("rw_w0", 8), ("rw_a0", 8), ("rw_kk", 8), ("rw_ka", 8), ("rw_rk", 8),
    ("rw_lnw", 8), ("rw_lnb", 8), ("kv_norm_g", 8), ("kv_kg", 1), ("fx_qg", 1), ("final_g", 8),
    ("kv_fb", 16), ("g_mix_2", 8), ("conv_w_2", 120), ("a_log_2", 16), ("dt_bias_2", 16),
    ("dn_o_gain_2", 1), ("q_gain_2", 4), ("kv_gain_2", 2), ("g_ffn_2", 8), ("g_final_2", 8),
]
COL = {}
NCOL = 0
for _n, _w in VECS:
    COL[_n] = (NCOL, _w)
    NCOL += _w


def consts():
    j = np.arange(128)[:, None]
    i = np.arange(128)[None, :]
    out = {"ident": (i == j), "incl": (j <= i), "ones": np.ones((128, 128)),
           "onesB": np.ones((128, 128)), "onesC": np.ones((128, 128)),
           "blk": (i // 64 == j // 64), "strict": (j < i),
           "strictR": (j > i), "inclR": (j >= i),
           "neg": np.where(i <= j, 0.0, -1e30)}
    for n in range(7):
        s = 1 << n
        out[f"lv{n}"] = (j // (2 * s) == i // (2 * s)) & (j % (2 * s) < s) & (i % (2 * s) >= s)
    for n in range(7):
        out[f"lvR{n}"] = out[f"lv{n}"].T
    perm = np.zeros((128, 128))
    for m in range(32):
        perm[m + 32, m] = -1.0
        perm[m, m + 32] = 1.0
    out["perm"] = perm
    freq = (np.float32(10000.0) ** (-np.arange(32, dtype=np.float32) / np.float32(32))).astype(np.float32)
    f = np.zeros((128, 128), np.float32)
    f[:, 0] = np.tile(freq, 4)
    f[:, 1] = np.arange(128) % 64
    out["misc"] = f
    out["iota"] = np.tile(np.arange(128), (128, 1))
    half = np.zeros((128, 1024))
    for pr in range(8):
        for q in range(128):
            half[2 * pr + q // 64, pr * 128 + q] = 1.0
    names = list(out)
    arr = np.concatenate([out[n].astype(np.float32) for n in names], axis=1)
    return {n: k for k, n in enumerate(names)}, arr, half[:16].astype(np.float32)


CON, _CARR, _PAIR = consts()




def program(nc, a, out):
    ctx = ExitStack()
    with ctx:
        def sb(name, cols, dt=F32):
            return ctx.enter_context(nc.sbuf_tensor(name, [P, cols], dt))

        def new_sem(name):
            return ctx.enter_context(nc.semaphore(name))

        PE, SY = Queue(new_sem("pe")), Queue(new_sem("sp"))
        DV, AC, GP = (Queue(new_sem(n), serial=True) for n in ("dve", "act", "pool"))
        BK = [ctx.enter_context(nc.psum_tensor(f"bank{i}", [P, 512], F32)) for i in range(8)]
        bfree = [[] for _ in range(8)]

        X = sb("X", 4096)
        H = sb("H", 4096)
        NS = 5
        W = sb("W", NS * 2048)
        NCON = _CARR.shape[1]
        con = sb("con", NCON)
        cols = sb("cols", NCOL)
        mods = sb("mods", 48 * 3 + 16 + 64)
        ARENA = 27456
        A = sb("A", ARENA)
        A32 = A[:, :]

        x3 = X[:, :].rearrange("p (k t) -> p k t", k=KT)
        h3 = H[:, :].rearrange("p (k t) -> p k t", k=KT)

        def C(name, n=128):
            k = CON[name] * 128
            return con[:, k:k + n]

        def col(name, k=0, n=1):
            o, w = COL[name]
            return cols[:, o + k:o + k + n]

        def now():
            return [(q.sem, q.n) for q in (PE, DV, AC, GP) if q.n]

        class Carve:
            def __init__(self):
                self.at = 0

            def __call__(self, n):
                self.at += n
                assert self.at <= ARENA, self.at
                return A[:, self.at - n:self.at]

        wsem = [new_sem(f"w{k}") for k in range(NS)]
        wcount = [0] * NS
        wfree = [[] for _ in range(NS)]
        wnext = [0]

        def load(*parts):
            k = wnext[0] % NS
            wnext[0] += 1
            views, mark = [], None
            for off, rows, shape, src in parts:
                n = 1
                for s in shape:
                    n *= s
                assert off + n <= 2048
                v = W[rows[0]:rows[1], k * 2048 + off:k * 2048 + off + n]
                if len(shape) == 2:
                    v = v.rearrange("p (a b) -> p a b", a=shape[0])
                views.append(v)
                wcount[k] += 16
                mark = SY.dma(wsem[k], wcount[k], lambda e, v=v, src=src: e.dma_start(v, src), *wfree[k])
            wfree[k] = []
            return k, views, mark

        def mms(items, *marks):
            PE.wait(*marks)
            for n, (o, l, r, s, e) in enumerate(items):
                f = lambda eng, o=o, l=l, r=r, s=s, e=e: eng.matmul(o, l, r, start=s, stop=e, skip_group_check=True)
                if n + 1 < len(items):
                    PE.silent(f)
                else:
                    return PE(f)

        def trs(items, *marks):
            PE.wait(*marks)
            for n, (o, i) in enumerate(items):
                f = lambda eng, o=o, i=i: eng.transpose(o, i, C("ident")[0:i.shape[0], 0:i.shape[0]])
                if n + 1 < len(items):
                    PE.silent(f)
                else:
                    return PE(f)

        def act(o, i, func, *marks, scale=1.0, bias=0.0, accum=None):
            if accum is not None:
                return AC(lambda e: e.activation(o, i, func, bias=bias, scale=scale, accum_out=accum), *marks)
            return AC(lambda e: e.activation(o, i, func, bias=bias, scale=scale), *marks)

        def tt(q, o, x, y, op, *marks):
            return q(lambda e: e.tensor_tensor(o, x, y, op), *marks)

        def ts(q, o, x, s1, s2, op0, op1, *marks):
            if op1 is None:
                return q(lambda e: e.tensor_scalar(o, x, s1, None, op0), *marks)
            return q(lambda e: e.tensor_scalar(o, x, s1, s2, op0, op1), *marks)

        def rroot(o, *marks):
            m = DV(lambda e: e.reciprocal(o, o), *marks)
            return act(o, o, ACT.Sqrt, m)

        def stt(o, x, s, y, op0, op1, *marks):
            return DV(lambda e: e.scalar_tensor_tensor(out=o, in0=x, scalar=s, in1=y, op0=op0, op1=op1), *marks)


        def body():
            s_in = new_sem("s_in")
            for n, (o, s) in enumerate([(con[:, :], a["const"]), (cols[:, :], a["cols"])]):
                m_in = SY.dma(s_in, 16 * (n + 1), lambda e, o=o, s=s: e.dma_start(o, s))
            ready = m_in
            xtok = A[:, 0:4096].rearrange("p (t d) -> p t d", t=4)
            s_x = new_sem("s_x")
            mx = SY.dma(s_x, 16, lambda e: e.dma_start(xtok, a["x"].rearrange("(t p) d -> p t d", p=P)))
            for q in (PE, DV, AC, GP):
                q.wait(ready)
            last = None
            for k in range(KT):
                b = k % 4
                t = trs([(BK[b][:, tk * 128:(tk + 1) * 128], xtok[:, tk, k * 128:(k + 1) * 128]) for tk in range(4)],
                        mx, *bfree[b])
                last = act(x3[:, k, :], BK[b][:, :], ACT.Copy, t)
                bfree[b] = [last]
            xdone = last

            def silu_cols(o, i, tmp):
                m = act(tmp, i, ACT.Sigmoid)
                return tt(DV, o, i, tmp, MUL, m)

            cact = sb("cact", 32)
            m_c = [silu_cols(cact[:, 0:8], col("c", 0, 8), cact[:, 16:24]),
                   silu_cols(cact[:, 8:16], col("c_2", 0, 8), cact[:, 24:32])]
            rowb = sb("rowb", 1024)
            rfree = [[], []]

            def mod_stream(o, w, n, cc, bias, banks):
                b0, b1, bc = banks
                pend = None
                m = None
                for g in range(n // 512):
                    b = (b0, b1)[g % 2]
                    mm, sl = [], []
                    for hf in range(2):
                        k, (v,), tk = load((0, (0, P), (4, 512), w[hf * 512:(hf + 1) * 512, g * 512:(g + 1) * 512].rearrange("(k p) n -> p k n", p=P)))
                        sl.append((k, v, tk))
                    for hf, (k, v, tk) in enumerate(sl):
                        m = mms([(BK[b][0:1, :], cact[:, cc + 4 * hf + j:cc + 4 * hf + j + 1], v[:, j, :],
                                  hf == 0 and j == 0, hf == 1 and j == 3) for j in range(4)], tk, m_c, *bfree[b])
                        wfree[k] = [m]
                        yield
                    r0 = 0
                    rb = rowb[0:1, (g % 2) * 512:(g % 2) * 512 + 512]
                    m = act(rb, BK[b][0:1, :], ACT.Copy, m, *rfree[g % 2])
                    bfree[b] = [m]
                    if pend:
                        pend()

                    def fin(g=g, rb=rb, m=m, r0=r0):
                        marks = [m] + (bfree[bc] if g == 0 else [])
                        mk = mms([(BK[bc][:, 4 * g + j:4 * g + j + 1], rb[:, j * 128:(j + 1) * 128], C("ones")[r0:r0 + 1, 0:1], True, True)
                                  for j in range(4)], *marks)
                        rfree[g % 2] = [mk]
                        return mk
                    pend = fin
                    yield
                mk = pend()
                m = tt(DV, o, BK[bc][:, 0:n // 128], bias, ADD, mk)
                bfree[bc] = [m]
                mod_mark.append(m)
                yield

            mod_mark = []
            mod0, mod1, mod2 = (mods[:, 48 * k:48 * k + 48] for k in range(3))
            modk = mods[:, 144:160]
            gs = mods[:, 160:168]
            g1 = mods[:, 168:176]

            def rsum_free(b):
                return bfree[b]

            sqb = sb("sqb", 1024)
            sqf = [[], []]
            rstd = sb("rstd", 512)
            rstd_r = []

            def rms_rstd(src, nk, inv_n, eps, b, *marks, o=None):
                m = None
                for k in range(nk):
                    s = sqb[:, (k % 2) * 512:(k % 2) * 512 + 512]
                    m1 = act(s, src[:, k, :], ACT.Square, *marks, *sqf[k % 2])
                    m = mms([(BK[b][:, :], C("ones"), s, k == 0, k == nk - 1)], m1, *bfree[b])
                    sqf[k % 2] = [m]
                oo = rstd[:, :] if o is None else o
                m = ts(DV, oo, BK[b][:, :], inv_n, eps, MUL, ADD, m, *rstd_r)
                bfree[b] = [m]
                return rroot(oo, m)

            def norm_mod(o3, g, sc, sh, b, *marks):
                m = rms_rstd(x3, KT, 1.0 / D, 1e-6, b, *marks)
                if sc is not None:
                    mg = ts(DV, gs, sc, 1.0, None, ADD, None, *marks)
                    mg = tt(DV, gs, gs, g, MUL, mg)
                last = []
                for k in range(KT):
                    m1 = tt(DV, o3[:, k, :], x3[:, k, :], rstd[:, :], MUL, m, *marks)
                    if sc is not None:
                        last.append(act(o3[:, k, :], o3[:, k, :], ACT.Identity, m1, mg, *marks,
                                        scale=gs[:, k:k + 1], bias=sh[:, k:k + 1]))
                    else:
                        last.append(act(o3[:, k, :], o3[:, k, :], ACT.Copy, m1, scale=g[:, k:k + 1]))
                rstd_r[:] = [m1]
                return last

            def proj(w, src3, nk, n, banks, evac, *marks, width=256):
                j = 0
                for n0 in range(0, n, width):
                    wd = min(width, n - n0)
                    k, (v,), tk = load((0, (0, P), (nk, wd), w[:, n0:n0 + wd].rearrange("(k p) n -> p k n", p=P)))
                    for c in range(0, wd, 128):
                        cw = min(128, wd - c)
                        b = banks[j % len(banks)]
                        m = mms([(BK[b][0:cw, :], v[:, kk, c:c + cw], src3[:, kk, :], kk == 0, kk == nk - 1)
                                 for kk in range(nk)], tk, *bfree[b], *marks)
                        bfree[b] = [evac(j, b, m)]
                        j += 1
                        yield
                    wfree[k] = [m]

            run(mod_stream(mod0, a["mod_w0"], 6144, 0, col("mod_b0", 0, 48), (4, 5, 6)))
            cv = Carve()
            XM = cv(3 * 4096)
            xm = [XM[:, 4096 * j:4096 * j + 4096].rearrange("p (k t) -> p k t", k=KT) for j in range(3)]
            LO = cv(512)
            ZG = cv(1024)
            XX = cv(4096)
            xx3 = XX.rearrange("p (k t) -> p k t", k=KT)
            MX = cv(1024)
            mh = norm_mod(h3, col("norm_mix_g0", 0, 8), mod0[:, 8:16], mod0[:, 0:8], 7, xdone, mod_mark[-1])
            start = now()
            xpark = nc.dram_tensor("xpark", (P, 4096), F32, kind="Internal").ap()
            s_park = new_sem("s_park")
            m_park = SY.dma(s_park, 16, lambda e: e.dma_start(xpark, X[:, :]), start)
            mxx = []
            for k in range(KT):
                m1 = tt(DV, xx3[:, k, 1:T], h3[:, k, 0:T - 1], h3[:, k, 1:T], SUB, start)
                mxx.append([m1, ts(DV, xx3[:, k, 0:1], h3[:, k, 0:1], -1.0, None, MUL, None)])

            def mix(o, j, k, *marks):
                return stt(o, xx3[:, k, :], col("rw_mu", 8 * j + k), h3[:, k, :], MUL, ADD, mxx[k], *marks)

            k1, (w1v, a1v, g1v), tk1 = load((0, (0, P), (8, 64), a["rw_w1"].rearrange("(k p) n -> p k n", p=P)),
                                            (512, (0, P), (8, 64), a["rw_a1"].rearrange("(k p) n -> p k n", p=P)),
                                            (1024, (0, P), (8, 96), a["rw_g1"][:, 0:96].rearrange("(k p) n -> p k n", p=P)))
            k2, (g1w,), tk2 = load((0, (0, P), (8, 64), a["rw_g1"][:, 96:160].rearrange("(k p) n -> p k n", p=P)))
            mfree = [[], []]
            n = 0
            for j in (1, 4, 5):
                for k in range(KT):
                    mb = MX[:, (n % 2) * 512:(n % 2) * 512 + 512]
                    m = mix(mb, j, k, *mfree[n % 2])
                    f, l = k == 0, k == KT - 1
                    if j == 1:
                        m = mms([(BK[0][0:64, :], w1v[:, k, :], mb, f, l)], m, tk1, *bfree[0])
                    elif j == 4:
                        m = mms([(BK[1][64:128, :], a1v[:, k, :], mb, f, l)], m, *bfree[1])
                    else:
                        m = mms([(BK[2][0:96, :], g1v[:, k, :], mb, f, l), (BK[3][0:64, :], g1w[:, k, :], mb, f, l)],
                                m, tk2, *bfree[2], *bfree[3])
                    mfree[n % 2] = [m]
                    n += 1
                if j == 1:
                    ml = [act(LO[0:64, :], BK[0][0:64, :], ACT.Tanh, m)]
                    bfree[0] = [ml[-1]]
                elif j == 4:
                    ml.append(act(LO[64:128, :], BK[1][64:128, :], ACT.Copy, m))
                    bfree[1] = [ml[-1]]
                else:
                    ml.append(act(ZG[0:96, 0:512], BK[2][0:96, :], ACT.Sigmoid, m))
                    ml.append(act(ZG[0:64, 512:1024], BK[3][0:64, :], ACT.Sigmoid, m))
                    bfree[2], bfree[3] = [ml[-2]], [ml[-1]]
            wfree[k1] = [m]
            wfree[k2] = [m]
            for d, j in ((0, 0), (1, 2), (2, 3)):
                for k in range(KT):
                    m = mix(xm[d][:, k, :], j, k)
                    ml.append(m)
            omka = mods[:, 176:184]
            ml.append(ts(DV, omka, col("rw_ka", 0, 8), -1.0, 1.0, MUL, ADD))
            start = now()

            cv.at = 3 * 4096 + 512 + 1024
            xa = [X[:, 512 * j:512 * j + 512] for j in range(8)]
            Rb, Kb, Lw, Ab, KKb, Lb, t0, t1 = xa
            sets = [[cv(512), cv(1024), cv(512), cv(512), cv(512), cv(512)] for _ in range(2)]
            NT, TT, TM, US, MT, AKT, RBT, RKT = [cv(512) for _ in range(8)]
            BHt, KHt, Vt, Yb = [cv(512) for _ in range(4)]
            sm = cv(64)
            XS, UU, SS, SP = [cv(64) for _ in range(4)]
            c4 = lambda v: v.rearrange("p (c t) -> p c t", c=4)
            yg = h3
            for z in (NT, AKT, RBT, RKT):
                zm = GP(lambda e, z=z: e.memset(z, 0.0), start)

            def prep(ct, since):
                G, AR, BH, KH, V, BO = sets[ct % 2]
                ar = AR.rearrange("p (c s t) -> p c s t", c=4, s=2)
                cs = slice(ct * 128, ct * 128 + 128)
                k1, (wr, wk), tk1 = load((0, (0, P), (8, 128), a["rw_wr"][:, cs].rearrange("(k p) n -> p k n", p=P)),
                                         (1024, (0, P), (8, 128), a["rw_wk"][:, cs].rearrange("(k p) n -> p k n", p=P)))
                k2, (wv, w2, a2, ga, gb), tk2 = load(
                    (0, (0, P), (8, 128), a["rw_wv"][:, cs].rearrange("(k p) n -> p k n", p=P)),
                    (1024, (0, 64), (128,), a["rw_w2"][:, cs]), (1024, (64, 128), (128,), a["rw_a2"][:, cs]),
                    (1152, (0, 96), (128,), a["rw_g2"][0:96, cs]), (1280, (0, 64), (128,), a["rw_g2"][96:160, cs]))

                def big(b, w, src, tk):
                    return mms([(BK[b][:, :], w[:, k, :], src[:, k, :], k == 0, k == 7) for k in range(8)],
                               tk, *bfree[b], *since)

                m = big(0, wk, xm[1], tk1)
                mk = act(Kb, BK[0][:, :], ACT.Copy, m, *since)
                bfree[0] = [mk]
                m1 = ts(DV, KKb, Kb, col("rw_kk", ct), None, MUL, None, mk, *since)
                m2 = act(t0, KKb, ACT.Square, m1, *since)
                yield
                m = big(1, wr, xm[0], tk1)
                wfree[k1] = [m]
                mr = act(Rb, BK[1][:, :], ACT.Copy, m, *since)
                bfree[1] = [mr]
                yield
                m = mms([(BK[2][:, :], C("blk"), t0, True, True)], m2, *bfree[2])
                m = ts(DV, t0, BK[2][:, :], 1e-24, None, ALU.max, None, m)
                bfree[2] = [m]
                m = rroot(t0, m)
                mkk = tt(DV, KKb, KKb, t0, MUL, m)
                yield
                m = mms([(BK[0][:, :], w2[:, :], LO[0:64, :], True, True)], tk2, *bfree[0])
                m1 = act(Lw, BK[0][:, :], ACT.Sigmoid, m, *since, bias=col("rw_w0", ct))
                bfree[0] = [m1]
                m = mms([(BK[2][:, :], a2[:, :], LO[64:128, :], True, True)], *bfree[2])
                ma = act(Ab, BK[2][:, :], ACT.Sigmoid, m, *since, bias=col("rw_a0", ct))
                bfree[2] = [ma]
                mlw = ts(DV, Lw, Lw, -EXPM05, None, MUL, None, m1)
                yield
                m = mms([(BK[0][:, :], ga[:, :], ZG[0:96, 0:512], True, False),
                         (BK[0][:, :], gb[:, :], ZG[0:64, 512:1024], False, True)], *bfree[0])
                mg = act(G, BK[0][:, :], ACT.Copy, m, *since)
                bfree[0] = [mg]
                yield
                for c in range(4):
                    s = slice(c * 128, c * 128 + 128)
                    mL = DV(lambda e, s=s: e.tensor_tensor_scan(Lb[:, s], C("ones"), Lw[:, s], 0.0, MUL, ADD), mlw, *since)
                m = big(1, wv, xm[2], tk2)
                wfree[k2] = [m]
                mv = act(V, BK[1][:, :], ACT.Copy, m, *since)
                bfree[1] = [mv]
                yield
                L3 = c4(Lb)
                eM, eE = sm[:, 16 * (ct % 2):16 * (ct % 2) + 4], sm[:, 16 * (ct % 2) + 4:16 * (ct % 2) + 8]
                mid = sm[:, 16 * (ct % 2) + 8:16 * (ct % 2) + 12]
                m1 = DV(lambda e: e.tensor_copy(mid, L3[:, :, 63]), mL, *since)
                m2 = tt(DV, eE, L3[:, :, 127], mid, SUB, m1)
                mE = act(eE, eE, ACT.Exp, m2)
                mM = act(eM, mid, ACT.Exp, m1)
                for c in range(4):
                    mL = ts(DV, L3[:, c, :], L3[:, c, :], mid[:, c:c + 1], None, SUB, None, m1)
                m = ts(DV, t0, Ab, col("rw_ka", ct), omka[:, ct:ct + 1], MUL, ADD, ma)
                mk2 = tt(DV, Kb, Kb, t0, MUL, m)
                yield
                m1 = act(t0, Lb, ACT.Exp, mL, mk2)
                mRh = tt(DV, ar[:, :, 1, :], c4(Rb), c4(t0), MUL, m1, mr, *since)
                m2 = tt(DV, t1, Lb, Lw, SUB, mL)
                m2 = act(t1, t1, ACT.Exp, m2)
                mAh = stt(ar[:, :, 0, :], c4(t1), -1.0, c4(KKb), MUL, MUL, m2, mkk)
                yield
                m1 = act(t0, Lb, ACT.Exp, mRh, scale=-1.0)
                mKh = tt(DV, KH, Kb, t0, MUL, m1, *since)
                m2 = tt(GP, t1, KKb, Ab, MUL, mAh, mkk)
                mBh = tt(DV, BH, t1, t0, MUL, m2, m1)
                yield
                m = stt(t1, Rb, col("rw_rk", ct), Kb, MUL, MUL, mBh)
                m = mms([(BK[2][:, :], C("blk"), t1, True, True)], m, *bfree[2])
                mbo = tt(DV, BO, BK[2][:, :], V, MUL, m, mv, *since)
                bfree[2] = [mbo]
                prepared[ct] = [mg, mRh, mAh, mKh, mBh, mbo, mv, mE, mM]
                used_tmp[ct] = now()
                yield

            def invert(NT, TT, TM, US, MT, R, banks, nb, sfree, m_nt):
                bu, bt, bm = banks
                c3 = lambda v: v.rearrange("p (c t) -> p c t", c=nb)
                bc = lambda name: C(name).unsqueeze(1).broadcast_to([P, nb, 128])
                lv = "lvR" if R else "lv"
                n3, t3, m3 = c3(NT), c3(TT), c3(TM)
                u3, k3 = c3(US), c3(MT)
                q = slice(0, nb * 128)
                m = tt(GP, k3, n3, bc(lv + "0"), MUL, m_nt, *sfree)
                mt_t = tt(GP, t3, k3, bc("ident"), ADD, m)
                m1 = mms([(BK[bu][:, c * 128:c * 128 + 128], k3[:, c, :], C("ident"), True, True) for c in range(nb)],
                         m, *bfree[bu])
                mt_m = tt(DV, m3, c3(BK[bu][:, q]), bc("ident"), ADD, m1, *sfree)
                bfree[bu] = [mt_m]
                mk_r = m1
                yield
                for lev in range(1, 7):
                    last = lev == 6
                    m = tt(GP, k3, n3, bc(lv + str(lev)), MUL, mk_r)
                    mu = mms([(BK[bu][:, c * 128:c * 128 + 128], k3[:, c, :], m3[:, c, :], True, True) for c in range(nb)],
                             m, mt_m, *bfree[bu])
                    mk_r = mu
                    me = act(US, BK[bu][:, q], ACT.Copy, mu)
                    bfree[bu] = [me]
                    yield
                    mA = mms([(BK[bt][:, c * 128:c * 128 + 128], u3[:, c, :], t3[:, c, :], True, True) for c in range(nb)],
                             me, mt_t, *bfree[bt])
                    if not last:
                        mB = mms([(BK[bm][:, c * 128:c * 128 + 128], t3[:, c, :], u3[:, c, :], True, True)
                                  for c in range(nb)], *bfree[bm])
                        mt_m = tt(DV, m3, m3, c3(BK[bm][:, q]), ADD, mB)
                        bfree[bm] = [mt_m]
                        mt_t = tt(DV, t3, t3, c3(BK[bt][:, q]), ADD, mB)
                    else:
                        mt_t = tt(DV, t3, t3, c3(BK[bt][:, q]), ADD, mA)
                    bfree[bt] = [mt_t]
                    yield
                inverse.append(mt_t)

            inverse = []
            prepared, used_tmp, chunked = {}, {}, {}

            def heads(ct, mz):
                G, AR, BH, KH, V, BO = sets[ct % 2]
                ar = AR.rearrange("p (c s t) -> p c s t", c=4, s=2)
                pm = prepared[ct]
                eM, eE = sm[:, 16 * (ct % 2):16 * (ct % 2) + 4], sm[:, 16 * (ct % 2) + 4:16 * (ct % 2) + 8]
                prev = now() if ct else []
                tok = []
                for b, src, dst in ((3, BH, BHt), (4, KH, KHt), (5, V, Vt)):
                    m = trs([(BK[b][:, c * 128:c * 128 + 128], src[:, c * 128:c * 128 + 128]) for c in range(4)],
                            pm, *bfree[b])
                    m = act(dst, BK[b][:, :], ACT.Copy, m, *prev)
                    bfree[b] = [m]
                    tok.append(m)
                yield
                for hd in range(2):
                    hp = slice(64 * hd, 64 * hd + 64)
                    before = now()
                    msc = []
                    for src, ba, dA, dR in ((BH, 3, NT, RBT), (KH, 5, AKT, RKT)):
                        for pr in range(2):
                            b = ba + pr
                            items = []
                            for cc in range(2):
                                c = 2 * pr + cc
                                o = BK[b][:, cc * 256:cc * 256 + 256].rearrange("p (s t) -> p s t", s=2)
                                items.append((o[0:64, :, :], src[hp, c * 128:c * 128 + 64], ar[hp, c, :, :], True, True))
                                items.append((o[64:128, :, 64:128], src[hp, c * 128 + 64:c * 128 + 128],
                                              ar[hp, c, :, 64:128], True, True))
                            m = mms(items, pm, *bfree[b])
                            o4 = BK[b][:, :].rearrange("p (c s t) -> p c s t", c=2, s=2)
                            for s, dst, mask in ((0, dA, "strict"), (1, dR, "incl")):
                                d3 = c4(dst)[:, 2 * pr:2 * pr + 2, :]
                                for rows, lo in ((slice(0, 64), 0), (slice(64, 128), 64)):
                                    mk = C(mask)[rows, lo:128].unsqueeze(1).broadcast_to([64, 2, 128 - lo])
                                    mm_ = tt(DV, d3[rows, :, lo:128], o4[rows, :, s, lo:128], mk, MUL, m, mz, *before)
                                msc.append(mm_)
                            bfree[b] = [mm_]
                        yield
                    yield from invert(NT, TT, TM, US, MT, False, (3, 4, 5), 4, before, msc)
                    mt = inverse[-1]
                    ms = GP(lambda e, hp=hp: e.memset(SS[hp, 0:64], 0.0), *before)
                    my = None
                    for c in range(4):
                        q = slice(c * 128, c * 128 + 128)
                        msp = ts(DV, SP[hp, :], SS[hp, :], eM[hp, c:c + 1], None, MUL, None, ms, my)
                        m = mms([(BK[6][:, 0:64], ar[hp, c, 0, :], SP[hp, :], True, False),
                                 (BK[6][:, 0:64], AKT[:, q], Vt[:, c * 128 + 64 * hd:c * 128 + 64 * hd + 64], False, True)],
                                msp, tok, msc, *bfree[6])
                        m = act(XS, BK[6][:, 0:64], ACT.Copy, m)
                        bfree[6] = [m]
                        yield
                        m = mms([(BK[7][:, 0:64], TT[:, q], XS, True, True)], m, mt, *bfree[7])
                        mu = act(UU, BK[7][:, 0:64], ACT.Copy, m)
                        bfree[7] = [mu]
                        yield
                        vt = Vt[:, c * 128 + 64 * hd:c * 128 + 64 * hd + 64]
                        m = mms([(BK[6][hp, 64:128], BHt[:, c * 128 + 64 * hd:c * 128 + 64 * hd + 64], UU, True, False),
                                 (BK[6][hp, 64:128], KHt[:, c * 128 + 64 * hd:c * 128 + 64 * hd + 64], vt, False, True)],
                                mu, *bfree[6])
                        m = tt(DV, SS[hp, :], SP[hp, :], BK[6][hp, 64:128], ADD, m)
                        bfree[6] = [m]
                        ms = ts(DV, SS[hp, :], SS[hp, :], eE[hp, c:c + 1], None, MUL, None, m)
                        my = mms([(BK[3][hp, q], SP[hp, :], ar[hp, c, 1, :], True, False),
                                  (BK[3][hp, q], UU, RBT[:, q], False, False),
                                  (BK[3][hp, q], vt, RKT[:, q], False, True)], *bfree[3])
                        yield
                    my = act(Yb[hp, :], BK[3][hp, :], ACT.Copy, my, *before)
                    bfree[3] = [my]
                m = mms([(BK[4][:, :], C("blk"), Yb, True, True)], my, *bfree[4])
                m = stt(Yb, BK[4][:, :], -1.0 / 64, Yb, MUL, ADD, m)
                bfree[4] = [m]
                m2 = act(US, Yb, ACT.Square, m)
                m2 = mms([(BK[5][:, :], C("blk"), US, True, True)], m2, *bfree[5])
                m2 = ts(DV, US, BK[5][:, :], 1.0 / 64, 64e-5, MUL, ADD, m2)
                bfree[5] = [m2]
                m2 = rroot(US, m2)
                m = tt(DV, Yb, Yb, US, MUL, m2)
                m = act(Yb, Yb, ACT.Identity, m, scale=col("rw_lnw", ct), bias=col("rw_lnb", ct))
                yield
                m = tt(DV, Yb, Yb, BO, ADD, m)
                m = tt(DV, yg[:, ct, :], Yb, G, MUL, m)
                chunked[ct] = [now(), m]
                yield

            start = [now(), m_park]
            run(prep(0, start))
            for ct in range(8):
                since = [used_tmp[ct]] + ([chunked[ct - 1]] if ct else [])
                if ct < 7:
                    weave(heads(ct, zm), prep(ct + 1, since))
                else:
                    run(heads(ct, zm))
            m_ret = SY.dma(s_park, 32, lambda e: e.dma_start(X[:, :], xpark), now())
            mg1 = ts(DV, g1, mod0[:, 16:24], 1.0, None, ADD, None)

            def residual(gate, *marks):
                def evac(j, b, m):
                    return stt(x3[:, j, :], BK[b][:, :], gate[:, j:j + 1], x3[:, j, :], MUL, ADD, m, *marks)
                return evac

            run(proj(a["rw_wo"], h3, KT, D, (0, 1), residual(g1, mg1, m_ret), now()))
            def down(w, src3, nk, n, pairs, evac, *marks):
                for g in range(n // 256):
                    bs = pairs[g % len(pairs)]
                    for kg in range(nk // 8):
                        k, (v,), tk = load((0, (0, P), (8, 256), w[kg * 1024:kg * 1024 + 1024, g * 256:g * 256 + 256].rearrange("(k p) n -> p k n", p=P)))
                        for c in range(2):
                            m = mms([(BK[bs[c]][:, :], v[:, kk, c * 128:c * 128 + 128], src3[:, kg * 8 + kk, :],
                                      kg == 0 and kk == 0, kg == nk // 8 - 1 and kk == 7) for kk in range(8)],
                                    tk, *bfree[bs[c]], *marks)
                        wfree[k] = [m]
                        yield
                    for c in range(2):
                        bfree[bs[c]] = [evac(2 * g + c, bs[c], m)]

            def mlp(l, g, mod, banks=(0, 1, 2, 3)):
                mh = norm_mod(h3, g, mod[:, 32:40], mod[:, 24:32], 7, now())
                hid = A[:, 0:16384].rearrange("p (k t) -> p k t", k=32)
                mg = ts(DV, g1, mod[:, 40:48], 1.0, None, ADD, None, now())

                def evac(j, b, m):
                    m = act(hid[:, j, :], BK[b][:, :], ACT.Relu, m)
                    hm.append(tt(GP, hid[:, j, :], hid[:, j, :], hid[:, j, :], MUL, m))
                    return m

                hm = []
                run(proj(a["mlp_up" + l], h3, KT, 4096, banks, evac, mh))
                run(down(a["mlp_down" + l], hid, 32, D, ((0, 1), (2, 3)), residual(g1, mg), hm))

            mlp("0", col("norm_mlp_g0", 0, 8), mod0)
            run(mod_stream(modk, a["kv_mod_w"], 2048, 0, col("kv_mod_b", 0, 16), (4, 5, 6)))
            run(mod_stream(mod1, a["mod_w1"], 6144, 0, col("mod_b1", 0, 48), (4, 5, 6)))

            cv = Carve()
            KK_, VV_, QQ_, GG_ = [cv(4096) for _ in range(4)]
            kT, qT, gT = [v.rearrange("p (k t) -> p k t", k=KT) for v in (KK_, QQ_, GG_)]
            vt = VV_.rearrange("p (t d) -> p t d", t=4)
            LF, FT, FA, FE = [cv(64) for _ in range(4)]
            lf3, ft3 = LF.rearrange("p (t h) -> p t h", t=4), FT.rearrange("p (t h) -> p t h", t=4)
            work = [[cv(512), cv(512), cv(2048), cv(16)] for _ in range(2)]
            nb_ = cv(512)
            start = now()

            def headnorm(dst, b, m, mask, inv_n, eps, gain, bn, o=None):
                m1 = act(dst, BK[b][:, :], ACT.Copy, m, start)
                m2 = act(nb_, dst, ACT.Square, m1, *nbf)
                m3 = mms([(BK[bn][:, :], C(mask), nb_, True, True)], m2, *bfree[bn])
                m4 = ts(DV, nb_, BK[bn][:, :], inv_n, eps, MUL, ADD, m3)
                bfree[bn] = [m4]
                m5 = rroot(nb_, m4)
                nbf[:] = [stt(dst, dst, gain, nb_, MUL, MUL, m5, m1)]
                return m1

            nbf = []
            mh = norm_mod(h3, col("kv_norm_g", 0, 8), modk[:, 8:16], modk[:, 0:8], 7, start)
            qgain = mods[:, 184:185]
            mq = ts(DV, qgain, col("fx_qg"), 0.125, None, MUL, None)
            run(proj(a["kv_w"][:, 0:1024], h3, KT, D, (0, 1, 2),
                     lambda j, b, m: headnorm(kT[:, j, :], b, m, "blk", 1.0 / 64, 1e-6, col("kv_kg"), 3), mh))

            def proj_tok(w, src3, n, banks, evac, *marks):
                for n0 in range(0, n, 512):
                    sl = [load((0, (0, P), (4, 512), w[hf * 512:hf * 512 + 512, n0:n0 + 512].rearrange("(k p) n -> p k n", p=P)))
                          for hf in range(2)]
                    for t in range(4):
                        b = banks[t % len(banks)]
                        m = mms([(BK[b][:, :], src3[:, k, t * 128:t * 128 + 128], sl[k // 4][1][0][:, k % 4, :], k == 0, k == 7)
                                 for k in range(8)], sl[0][2], sl[1][2], *bfree[b], *marks)
                        bfree[b] = [evac(t, n0, b, m)]
                        yield
                    wfree[sl[0][0]] = [m]
                    wfree[sl[1][0]] = [m]

            run(proj_tok(a["kv_w"][:, 1024:2048], h3, D, (0, 1, 2, 3),
                         lambda t, n0, b, m: act(vt[:, t, n0:n0 + 512], BK[b][:, :], ACT.Copy, m, start), mh))

            def small_tok(w, n, b, *marks):
                k, (v,), tk = load((0, (0, P), (8, n), w.rearrange("(k p) n -> p k n", p=P)))
                m = mms([(BK[b][:, t * n:t * n + n], h3[:, kk, t * 128:t * 128 + 128], v[:, kk, :], kk == 0, kk == 7)
                         for t in range(4) for kk in range(8)], tk, *bfree[b], *marks)
                wfree[k] = [m]
                return m

            def bc4(v):
                return v.unsqueeze(1).broadcast_to([P, 4, 16])

            v3 = lambda v: v.rearrange("p (t h) -> p t h", t=4)
            m = small_tok(a["kv_w"][:, 2048:2064], 16, 4, mh)
            m = tt(DV, v3(FA), v3(BK[4][:, 0:64]), bc4(col("kv_fb", 0, 16)), ADD, m, start)
            bfree[4] = [m]
            m1 = act(FE, FA, ACT.Abs, m, start)
            m1 = act(FE, FE, ACT.Exp, m1, scale=-1.0)
            m1 = act(FE, FE, ACT.Ln, m1, bias=1.0)
            m = ts(DV, FA, FA, 0.0, None, ALU.min, None, m1)
            mlf = tt(DV, LF, FA, FE, SUB, m, m1)
            m = mms([(BK[5][:, 16 * t:16 * t + 16], C("incl") if j == t else C("ones"), lf3[:, j, :], j == 0, j == t)
                     for t in range(4) for j in range(t + 1)], mlf, *bfree[5])
            mft = act(FT, BK[5][:, 0:64], ACT.Copy, m)
            bfree[5] = [mft]

            mh = norm_mod(h3, col("norm_mix_g1", 0, 8), mod1[:, 8:16], mod1[:, 0:8], 7, now())
            run(proj(a["fx_wqg"][:, 0:1024], h3, KT, D, (0, 1, 2),
                     lambda j, b, m: headnorm(qT[:, j, :], b, m, "blk", 1.0 / 64, 1e-6, qgain, 3), mh, mq))
            run(proj(a["fx_wqg"][:, 1024:2048], h3, KT, D, (0, 1, 2),
                     lambda j, b, m: act(gT[:, j, :], BK[b][:, :], ACT.Sigmoid, m), mh))
            cuml = con[:, CON["incl"] * 128:CON["incl"] * 128 + 512]

            def attention(banks, bufs, qk, causal, vcols, width, rows, evac, mr, scale=1.0, forget=None):
                bs, bt, bo = banks
                Fb, S, PT, sm_ = bufs
                p3 = PT.rearrange("p (k t) -> p k t", k=4)
                mo = None
                mF = None
                if forget is not None:
                    m = mms([(BK[bo][:, 128 * j:512], lf3[:, j, forget:forget + 1].broadcast_to([P, 128]), cuml[:, 0:512 - 128 * j],
                              j == 0, j == 3) for j in range(4)], mlf, *bfree[bo], mr)
                    mF = act(Fb, BK[bo][:, :], ACT.Copy, m, mr)
                    bfree[bo] = [mF]
                    yield
                for qt in range(4):
                    n = (qt + 1) * 128 if causal else 512
                    m = mms([(BK[bs][:, 0:n], q_(qt), k_(n), i == 0, i == len(qk) - 1) for i, (q_, k_) in enumerate(qk)],
                            *bfree[bs], mr)
                    if forget is not None:
                        m = DV(lambda e, qt=qt, n=n: e.scalar_tensor_tensor(
                            out=S[:, 0:n], in0=Fb[:, 0:n], scalar=ft3[:, qt, forget:forget + 1], in1=BK[bs][:, 0:n],
                            op0=SUB, op1=SUB, reverse1=True), m, mF, mft, mo)
                        bfree[bs] = [m]
                        m = tt(DV, S[:, n - 128:n], S[:, n - 128:n], C("neg"), ADD, m)
                        src = S
                    else:
                        src = BK[bs]
                    mx = DV(lambda e, n=n, src=src: e.tensor_reduce(sm_[:, 0:1], src[:, 0:n], AX, ALU.max), m, mo)
                    mx = ts(DV, sm_[:, 1:2], sm_[:, 0:1], -scale, None, MUL, None, mx)
                    yield
                    m = act(S[:, 0:n], src[:, 0:n], ACT.Exp, mx, mo, scale=scale, bias=sm_[:, 1:2], accum=sm_[:, 2:3])
                    if forget is None:
                        bfree[bs] = [m]
                    mr_ = DV(lambda e: e.reciprocal(sm_[:, 3:4], sm_[:, 2:3]), m)
                    m = ts(DV, S[:, 0:n], S[:, 0:n], sm_[:, 3:4], None, MUL, None, mr_)
                    yield
                    nk = n // 128
                    mo = trs([(BK[bt][:, k * 128:k * 128 + 128], S[:, k * 128:k * 128 + 128]) for k in range(nk)],
                             m, *bfree[bt])
                    m = act(p3[:, 0:nk, qt * 128:qt * 128 + 128], BK[bt][:, 0:n].rearrange("p (k t) -> p k t", k=nk),
                            ACT.Copy, mo, mr)
                    bfree[bt] = [m]
                    yield
                m = mms([(BK[bo][rows, (k * 128 if causal else 0):512], vcols(k), p3[:, k, (k * 128 if causal else 0):512],
                          k == 0, k == 3) for k in range(4)], m, *bfree[bo])
                m = evac(m)
                bfree[bo] = [m]
                yield

            def fox(par):
                for ct in range(8):
                    hd = 2 * ct + par
                    hp = slice(64 * par, 64 * par + 64)
                    bo = 4 * par + 2
                    yield from attention(
                        (4 * par, 4 * par + 1, bo), work[par],
                        [(lambda qt: qT[hp, ct, qt * 128:qt * 128 + 128], lambda n: kT[hp, ct, 0:n])], True,
                        lambda k: vt[:, k, hd * 64:hd * 64 + 64], 64, hp,
                        lambda m: tt(DV, gT[hp, ct, :], BK[bo][hp, :], gT[hp, ct, :], MUL, m), now(), forget=hd)

            weave(fox(0), fox(1))
            mg1 = ts(DV, g1, mod1[:, 16:24], 1.0, None, ADD, None)
            run(proj(a["fx_wo"], gT, KT, D, (0, 1), residual(g1, mg1), now()))
            mlp("1", col("norm_mlp_g1", 0, 8), mod1)
            norm_mod(x3, col("final_g", 0, 8), None, None, 7, now())
            run(mod_stream(mod2, a["w_mod_2"], 6144, 8, col("b_mod_2", 0, 48), (4, 5, 6)))
            cv = Carve()
            OD = cv(4096)
            od3 = OD.rearrange("p (k t) -> p k t", k=KT)
            BE, GG2, GCs, EG, NEG, EGL, EKS, BEK, NBE, TA, TB = [cv(64) for _ in range(11)]
            win = a["w_in_2"]
            start = now()
            mh = norm_mod(h3, col("g_mix_2", 0, 8), mod2[:, 8:16], mod2[:, 0:8], 7, start)
            m = small_tok(win[:, 4096:4128], 32, 4, mh)
            ba = BK[4][:, 0:128].rearrange("p (t h) -> p t h", t=4)
            m1 = act(v3(BE), ba[:, :, 0:16], ACT.Sigmoid, m, start)
            m2 = tt(DV, v3(TA), ba[:, :, 16:32], bc4(col("dt_bias_2", 0, 16)), ADD, m1, start)
            bfree[4] = [m2]
            m = act(TB, TA, ACT.Abs, m2, start)
            m = act(TB, TB, ACT.Exp, m, scale=-1.0)
            m = act(TB, TB, ACT.Ln, m, bias=1.0)
            m = stt(TA, TA, 0.0, TB, ALU.max, ADD, m)
            ea = mods[:, 185:201]
            me = act(ea, col("a_log_2", 0, 16), ACT.Exp, start)
            m = tt(DV, v3(TA), v3(TA), bc4(ea), MUL, me, m)
            mg = ts(DV, GG2, TA, -1.0, None, MUL, None, m)
            g3 = v3(GG2)
            bk5 = BK[5][:, :].rearrange("p (s t h) -> p s t h", s=8, t=4)
            m = mms([(BK[5][:, 0:32], C("incl"), g3[:, :, 0:8], True, True),
                     (BK[5][:, 32:64], C("inclR"), g3[:, :, 8:16], True, True),
                     (BK[5][:, 64:128], C("ones"), GG2, True, True)], mg, *bfree[5])
            gc3 = v3(GCs)
            m1 = act(gc3[:, :, 0:8], BK[5][:, 0:32].rearrange("p (t h) -> p t h", t=4), ACT.Copy, m, start)
            m1 = act(gc3[:, :, 8:16], BK[5][:, 32:64].rearrange("p (t h) -> p t h", t=4), ACT.Copy, m)
            m2 = act(EGL, BK[5][:, 64:128], ACT.Exp, m)
            m3 = tt(DV, EKS, BK[5][:, 64:128], GCs, SUB, m1, m2)
            bfree[5] = [m3]
            m3 = act(EKS, EKS, ACT.Exp, m3)
            m1 = act(EG, GCs, ACT.Exp)
            m = ts(DV, NEG, EG, -1.0, None, MUL, None, m1)
            m = tt(DV, BEK, BE, EKS, MUL, m3)
            mcol = [ts(DV, NBE, BE, -1.0, None, MUL, None), m3, m2]

            dsets = [[cv(512) for _ in range(9)] for _ in range(2)]
            dwork = [[cv(512) for _ in range(8)] + [cv(128) for _ in range(4)] for _ in range(2)]
            PB, t0, t1 = cv(516), cv(512), cv(512)
            start = now()
            mz = GP(lambda e: e.memset(PB[:, 0:2], 0.0), start)
            mz = GP(lambda e: e.memset(PB[:, 514:516], 0.0), start)
            dprep, dused, ddone = {}, {}, {}

            def dn_prep(hd, since):
                qT_, kT_, Z_, Kt_, Vt_, KF, KB, QF, QB = dsets[hd % 2]
                cw = col("conv_w_2", 0, 120).rearrange("p (c j) -> p c j", c=24)
                src = [win[:, b0 + hd * 128:b0 + hd * 128 + 128].rearrange("(k p) n -> p k n", p=P) for b0 in (0, 1024, 2048, 3072)]
                sl = [load((0, (0, P), (8, 128), src[2 * i]), (1024, (0, P), (8, 128), src[2 * i + 1])) for i in range(2)]
                mlast = None
                toks = []
                for i in range(4):
                    k, vs, tk = sl[i // 2]
                    b = i % 2
                    m = mms([(BK[b][:, :], vs[i % 2][:, kk, :], h3[:, kk, :], kk == 0, kk == 7) for kk in range(8)],
                            tk, *bfree[b], mh)
                    if i % 2:
                        wfree[k] = [m]
                    if i == 3:
                        mzz = act(Z_, BK[b][:, :], ACT.Silu, m, since)
                        bfree[b] = [mzz]
                        yield
                        break
                    m = act(PB[:, 2:514], BK[b][:, :], ACT.Copy, m, mlast, since)
                    bfree[b] = [m]
                    yield
                    ct = 8 * i + hd
                    m = ts(DV, t0, PB[:, 0:512], cw[:, ct, 0:1], None, MUL, None, m, mz, since)
                    for j in range(1, 5):
                        m = stt(t0, PB[:, j:j + 512], cw[:, ct, j:j + 1], t0, MUL, ADD, m)
                    mlast = m
                    yield
                    dst = (qT_, kT_, t1)[i]
                    m = act(dst, t0, ACT.Silu, m, since)
                    if i < 2:
                        m2 = act(t0, dst, ACT.Square, m)
                        m2 = mms([(BK[1 - b][:, :], C("ones"), t0, True, True)], m2, *bfree[1 - b])
                        m2 = ts(DV, t0, BK[1 - b][:, :], 1e-6, None, ADD, None, m2)
                        bfree[1 - b] = [m2]
                        m2 = rroot(t0, m2)
                        mlast = m = stt(dst, dst, (128 ** -0.5, 1.0)[i], t0, MUL, MUL, m, m2)
                    mlast = [mlast, m]
                    yield
                    if i:
                        m = trs([(BK[b][:, c * 128:c * 128 + 128], dst[:, c * 128:c * 128 + 128]) for c in range(4)],
                                m, *bfree[b])
                        m = act((None, Kt_, Vt_)[i], BK[b][:, :], ACT.Copy, m, since)
                        bfree[b] = [m]
                        toks.append(m)
                        mlast = [mlast, m]
                        yield
                q3 = lambda v: v.rearrange("p (c t) -> p c t", c=4)
                for lhs, rhs, df, db, mf, mb, b in ((kT_, kT_, KF, KB, "strict", "strictR", 0), (kT_, qT_, QF, QB, "incl", "inclR", 1)):
                    m = mms([(BK[b][:, c * 128:c * 128 + 128], lhs[:, c * 128:c * 128 + 128], rhs[:, c * 128:c * 128 + 128], True, True)
                             for c in range(4)], mlast, *bfree[b])
                    for d, mk in ((df, mf), (db, mb)):
                        m1 = tt(DV, q3(d), q3(BK[b][:, :]), C(mk).unsqueeze(1).broadcast_to([P, 4, 128]), MUL, m, since)
                    bfree[b] = [m1]
                    toks.append(m1)
                    yield
                dprep[hd] = [toks, mzz, mlast]
                dused[hd] = now()

            def dn_dir(hd, R):
                qT_, kT_, Z_, Kt_, Vt_, KF, KB, QF, QB = dsets[hd % 2]
                E_, NT, TT, TM, US, MT, RK, OO, SS, XS, VN, VS = dwork[R]
                KM, QM = (KB, QB) if R else (KF, QF)
                ba_, bb_, bc_ = (5, 6, 7) if R else (2, 3, 4)
                dh = 8 * R + hd
                c_ = lambda v, c: v3(v)[:, c, dh:dh + 1]
                q3 = lambda v: v.rearrange("p (c t) -> p c t", c=4)
                pm = [dprep[hd], mcol]
                before = [ddone[hd - 1]] if hd else [start]
                m = mms([(BK[ba_][:, c * 128:c * 128 + 128], g3[:, c, dh:dh + 1].broadcast_to([P, 128]), C("inclR" if R else "incl"), True, True)
                         for c in range(4)], pm, *bfree[ba_])
                for c in range(4):
                    m1 = ts(DV, q3(E_)[:, c, :], BK[ba_][:, c * 128:c * 128 + 128], c_(GCs, c), 0.0, SUB, ALU.min, m, before)
                bfree[ba_] = [m1]
                m = act(E_, E_, ACT.Exp, m1)
                yield
                for c in range(4):
                    mn = stt(q3(NT)[:, c, :], q3(E_)[:, c, :], c_(NBE, c), q3(KM)[:, c, :], MUL, MUL, m, before)
                mrk = tt(GP, RK, QM, E_, MUL, m, before, mn)
                yield
                yield from invert(NT, TT, TM, US, MT, R, (ba_, bb_, bc_), 4, [before], mn)
                mt = inverse[-1]
                ms = GP(lambda e: e.memset(SS, 0.0), before)
                mvs = None
                for c in (range(3, -1, -1) if R else range(4)):
                    q = slice(c * 128, c * 128 + 128)
                    m = mms([(BK[ba_][:, 0:128], kT_[:, q], SS, True, True), (BK[ba_][:, 128:256], qT_[:, q], SS, True, True)],
                            ms, *bfree[ba_])
                    m1 = stt(XS, BK[ba_][:, 0:128], c_(NEG, c), Vt_[:, q], MUL, ADD, m, mvs)
                    mq = ts(DV, OO[:, q], BK[ba_][:, 128:256], c_(EG, c), None, MUL, None, m, before)
                    bfree[ba_] = [mq]
                    yield
                    m = mms([(BK[bb_][:, 0:128], TT[:, q], XS, True, True)], m1, mt, *bfree[bb_])
                    m2 = act(VN, BK[bb_][:, 0:128], ACT.Copy, m, mvs, scale=c_(BE, c))
                    m3 = act(VS, BK[bb_][:, 0:128], ACT.Copy, m, mvs, scale=c_(BEK, c))
                    bfree[bb_] = [m3]
                    yield
                    m = mms([(BK[bc_][:, 0:128], Kt_[:, q], VS, True, True)], m3, *bfree[bc_])
                    mvs = mms([(BK[bc_][:, 128:256], RK[:, q], VN, True, True)], m2, mrk)
                    ms = stt(SS, SS, c_(EGL, c), BK[bc_][:, 0:128], MUL, ADD, mvs)
                    mo = tt(DV, OO[:, q], OO[:, q], BK[bc_][:, 128:256], ADD, mvs, mq)
                    bfree[bc_] = [mo]
                    yield
                dout.append(mo)

            dout = []

            def dn_head(hd):
                qT_, kT_, Z_, Kt_, Vt_, KF, KB, QF, QB = dsets[hd % 2]
                fs = [dn_dir(hd, False), dn_dir(hd, True)]
                while fs:
                    for f in list(fs):
                        if next(f, StopIteration) is StopIteration:
                            fs.remove(f)
                    yield
                OO, OB = dwork[0][7], dwork[1][7]
                sq, sm_ = dwork[0][0], dwork[0][8]
                m = tt(GP, OO, OO, OB, ADD, dout[-2:])
                for c in range(4):
                    m1 = act(sq[:, 0:128], OO[:, c * 128:c * 128 + 128], ACT.Square, m, accum=sm_[:, c:c + 1])
                m1 = ts(DV, sm_[:, 0:4], sm_[:, 0:4], 1.0 / 128, 1e-6, MUL, ADD, m1)
                m1 = rroot(sm_[:, 0:4], m1)
                for c in range(4):
                    m = ts(DV, OO[:, c * 128:c * 128 + 128], OO[:, c * 128:c * 128 + 128], sm_[:, c:c + 1], None, MUL, None, m1)
                yield
                m = trs([(BK[2][:, c * 128:c * 128 + 128], OO[:, c * 128:c * 128 + 128]) for c in range(4)], m, *bfree[2])
                m = stt(od3[:, hd, :], BK[2][:, :], col("dn_o_gain_2"), Z_, MUL, MUL, m)
                bfree[2] = [m]
                ddone[hd] = now()
                yield

            run(dn_prep(0, start))
            for hd in range(8):
                since = [dused[hd]] + ([ddone[hd - 1]] if hd else [])
                if hd < 7:
                    weave(dn_head(hd), dn_prep(hd + 1, since))
                else:
                    run(dn_head(hd))
            cv = Carve()
            OD, ME, GA = cv(4096), cv(4096), cv(4096)
            me3, ga3 = [v.rearrange("p (k t) -> p k t", k=KT) for v in (ME, GA)]
            start = now()
            gm = []

            def gate(j, b, m):
                m = act(ga3[:, j, :], BK[b][:, :], ACT.Sigmoid, m, start)
                gm[:] = [m]
                return m

            run(proj(win[:, 4960:5984], h3, KT, D, (0, 1), gate, mh))
            run(proj(a["w_o_dn_2"], od3, KT, D, (2, 3),
                     lambda j, b, m: tt(DV, me3[:, j, :], BK[b][:, :], ga3[:, j, :], MUL, m, gm, start), start))

            OM = OD
            om3 = OM.rearrange("p (k t) -> p k t", k=KT)
            start = now()
            CQ, CK, KR, CO, SI, R0, R1 = cv(2048), cv(1024), cv(512), cv(512), cv(512), cv(512), cv(512)
            cq3, ck3 = CQ.rearrange("p (k t) -> p k t", k=4), CK.rearrange("p (k t) -> p k t", k=2)
            lw_ = []
            for _ in range(2):
                lw_.append([cv(512) for _ in range(4)] + [None, cv(512), cv(2048), cv(16)])
            s_pos = new_sem("s_pos")
            pi = R0[0:64, :].bitcast(I32)
            mp = SY.dma(s_pos, 16, lambda e: e.dma_start(pi, a["pos"].broadcast_to([64, 512])), start)
            ang, n_ = R1[0:64, :], SI[0:64, :]
            m = DV(lambda e: e.tensor_copy(ang, pi), mp, start)
            m = ts(DV, ang, ang, C("misc")[0:64, 0:1], None, MUL, None)
            MAGIC = 12582912.0
            m = ts(DV, n_, ang, float(1 / (2 * np.pi)), MAGIC, MUL, ADD)
            m = ts(DV, n_, n_, -MAGIC, None, ADD, None)
            c1 = 6.28125
            c2 = float(np.float32(int((2 * np.pi - c1) * 2 ** 20) / 2 ** 20))
            c3 = float(np.float32(2 * np.pi - c1 - c2))
            for c in (c1, c2, c3):
                m = stt(ang, n_, -c, ang, MUL, ADD)
            m = ts(DV, ang, ang, 3.1415925, -3.1415925, ALU.min, ALU.max)
            ms = act(SI[0:64, :], ang, ACT.Sin, m)
            mc = act(CO[0:64, :], ang, ACT.Sin, m, scale=0.5)
            m = tt(DV, CO[0:64, :], CO[0:64, :], CO[0:64, :], MUL, mc)
            mcs = [ts(DV, CO[0:64, :], CO[0:64, :], -2.0, 1.0, MUL, ADD), ms]

            run(proj(win[:, 4128:4640], h3, KT, 512, (0, 1), lambda j, b, m: act(cq3[:, j, :], BK[b][:, :], ACT.Copy, m, start), mh))
            run(proj(win[:, 4640:4896], h3, KT, 256, (0, 1), lambda j, b, m: act(ck3[:, j, :], BK[b][:, :], ACT.Copy, m, start), mh))

            def rope(dst, b, m, tmp, b2, *marks):
                m1 = act(tmp[0:64, :], BK[b][0:64, :], ACT.Copy, m, *marks)
                bfree[b] = [m1]
                m2 = mms([(BK[b2][0:64, :], C("perm")[0:64, 0:64], tmp[0:64, :], True, True)], m1, *bfree[b2])
                m3 = tt(DV, dst, BK[b2][0:64, :], SI[0:64, :], MUL, m2, mcs, *marks)
                bfree[b2] = [m3]
                m4 = tt(DV, tmp[0:64, :], tmp[0:64, :], CO[0:64, :], MUL, m2, m3)
                return tt(DV, dst, dst, tmp[0:64, :], ADD, m4)

            k, (v,), tk = load((0, (0, P), (8, 64), win[:, 4896:4960].rearrange("(k p) n -> p k n", p=P)))
            m = mms([(BK[2][0:64, :], v[:, kk, :], h3[:, kk, :], kk == 0, kk == 7) for kk in range(8)], tk, mh, *bfree[2])
            wfree[k] = [m]
            mkr = rope(KR[0:64, :], 2, m, R0, 3, mp, start, now())
            for src, nk, g, inv in ((cq3, 4, "q_gain_2", 1.0 / 512), (ck3, 2, "kv_gain_2", 1.0 / 256)):
                m = rms_rstd(src, nk, inv, 1e-6, 4, now(), o=R0)
                for j in range(nk):
                    m = stt(src[:, j, :], src[:, j, :], col(g, j), R0, MUL, MUL, m)
            mlat = m
            start = now()

            def mla(par):
                Qn, Qr, Kn, Vh, _, S, PT, sm_ = lw_[par]
                b0 = 4 * par
                for hh in range(4):
                    hd = 2 * hh + par
                    since = now()
                    k, (wq, wkv), tk = load(
                        (0, (0, P), (4, 192), a["w_uq_2"][:, hd * 192:hd * 192 + 192].rearrange("(k p) n -> p k n", p=P)),
                        (768, (0, P), (2, 256), a["w_ukv_2"][:, hd * 256:hd * 256 + 256].rearrange("(k p) n -> p k n", p=P)))
                    m = mms([(BK[b0][0:64, :], wq[:, kk, 128:192], cq3[:, kk, :], kk == 0, kk == 3) for kk in range(4)],
                            tk, mlat, *bfree[b0], start)
                    mr = rope(Qr[0:64, :], b0, m, S, b0 + 1, since)
                    yield
                    m = mms([(BK[b0 + 2][:, :], wq[:, kk, 0:128], cq3[:, kk, :], kk == 0, kk == 3) for kk in range(4)],
                            *bfree[b0 + 2])
                    m1 = act(Qn, BK[b0 + 2][:, :], ACT.Copy, m, since)
                    bfree[b0 + 2] = [m1]
                    yield
                    m = mms([(BK[b0 + 3][:, :], wkv[:, kk, 0:128], ck3[:, kk, :], kk == 0, kk == 1) for kk in range(2)],
                            *bfree[b0 + 3])
                    m2 = act(Kn, BK[b0 + 3][:, :], ACT.Copy, m, since)
                    bfree[b0 + 3] = [m2]
                    yield
                    m = mms([(BK[b0][:, t * 128:t * 128 + 128], ck3[:, kk, t * 128:t * 128 + 128], wkv[:, kk, 128:256], kk == 0, kk == 1)
                             for t in range(4) for kk in range(2)], *bfree[b0])
                    wfree[k] = [m]
                    m3 = act(Vh, BK[b0][:, :], ACT.Copy, m, since)
                    bfree[b0] = [m3]
                    yield
                    yield from attention(
                        (b0, b0 + 1, b0 + 2), (None, S, PT, sm_),
                        [(lambda qt: Qn[:, qt * 128:qt * 128 + 128], lambda n: Kn[:, 0:n]),
                         (lambda qt: Qr[0:64, qt * 128:qt * 128 + 128], lambda n: KR[0:64, 0:n])], False,
                        lambda kt: Vh[:, kt * 128:kt * 128 + 128], 128, slice(0, P),
                        lambda m: act(om3[:, hd, :], BK[b0 + 2][:, :], ACT.Copy, m), [mr, m1, m2, m3, mkr, since],
                        scale=192 ** -0.5)

            weave(mla(0), mla(1))
            start = now()
            run(proj(win[:, 5984:7008], h3, KT, D, (0, 1), gate, mh))
            TG = lw_[0][6]
            tgf = [[], []]

            def merge(j, b, m):
                t_ = TG[:, 512 * (j % 2):512 * (j % 2) + 512]
                m1 = tt(DV, t_, BK[b][:, :], ga3[:, j, :], MUL, m, gm, start, *tgf[j % 2])
                tgf[j % 2] = [tt(GP, me3[:, j, :], me3[:, j, :], t_, ADD, m1)]
                return m1

            run(proj(a["w_o_mla_2"], om3, KT, D, (2, 3), merge, start))
            run(proj(a["w_out_2"], me3, KT, D, (0, 1), residual(mod2[:, 16:24]), now()))
            cv = Carve()
            HT, SEL, XE, YE = cv(4096), cv(4096), cv(8192), cv(8192)
            RKs, AFT = cv(512), cv(512)
            AF, RT, s4, s8 = cv(64), cv(64), cv(16), cv(16)
            ht3 = HT.rearrange("p (t d) -> p t d", t=4)
            sel3 = SEL.rearrange("p (t s) -> p t s", t=4)
            xe3 = XE.rearrange("p (k s) -> p k s", k=KT)
            ye3 = YE.rearrange("p (e d) -> p e d", e=8)
            start = now()
            mh = norm_mod(h3, col("g_ffn_2", 0, 8), mod2[:, 32:40], mod2[:, 24:32], 7, start)
            WKb, SMb, PAIR = YE[0:16, 0:512], YE[0:16, 512:1024], YE[0:16, 1024:2048]
            s_pair = new_sem("s_pair")
            mpair = SY.dma(s_pair, 16, lambda e: e.dma_start(PAIR, a["pair"]), start)
            m = small_tok(a["w_router_2"], 16, 0, mh)
            lg, af3 = v3(BK[0][:, 0:64]), v3(AF)
            b16 = lambda v: v.unsqueeze(2).broadcast_to([P, 4, 16])
            m = DV(lambda e: e.tensor_reduce(s4[:, 0:4], lg, AX, ALU.max), m, start)
            m = tt(DV, af3, lg, b16(s4[:, 0:4]), SUB)
            bfree[0] = [m]
            m = act(AF, AF, ACT.Exp, m)
            m = DV(lambda e: e.tensor_reduce(s4[:, 4:8], af3, AX, ADD), m)
            m = DV(lambda e: e.reciprocal(s4[:, 4:8], s4[:, 4:8]))
            m = tt(DV, af3, af3, b16(s4[:, 4:8]), MUL)
            m = trs([(BK[1][0:16, t * 128:t * 128 + 128], af3[:, t, :]) for t in range(4)], m, *bfree[1])
            ma = act(AFT[0:16, :], BK[1][0:16, :], ACT.Copy, m, start)
            bfree[1] = [ma]
            m = act(WKb, AFT[0:16, :], ACT.Copy)
            DV.wait(m)
            for _ in range(8):
                DV(lambda e: e.max(s8[0:16, 0:8], WKb))
                m = DV(lambda e: e.match_replace(WKb, s8[0:16, 0:8], WKb, -1.0))
            ts(DV, SMb, WKb, 0.0, None, ALU.is_lt, None)
            DV(lambda e: e.tensor_tensor_scan(WKb, SMb, SMb, 0.0, ADD, ALU.max))
            tt(DV, WKb, WKb, SMb, MUL)
            mr = ts(DV, RKs[0:16, :], WKb, -1.0, None, ADD, None)
            m = trs([(BK[2][:, 16 * t:16 * t + 16], RKs[0:16, t * 128:t * 128 + 128]) for t in range(4)], mr, *bfree[2])
            m = act(RT, BK[2][:, 0:64], ACT.Copy, m, start)
            bfree[2] = [m]
            for t in range(4):
                ms = DV(lambda e, t=t: e.tensor_tensor(
                    sel3[:, t, :].rearrange("p (e s) -> p e s", e=16),
                    v3(RT)[:, t, :].unsqueeze(2).broadcast_to([P, 16, 64]),
                    C("iota", 64).unsqueeze(1).broadcast_to([P, 16, 64]), ALU.is_equal), m, start)
            for k in range(KT):
                for hf in range(2):
                    pass
                b = 3 + k % 2
                m = trs([(BK[b][:, t * 128:t * 128 + 128], h3[:, k, t * 128:t * 128 + 128]) for t in range(4)], mh, *bfree[b])
                mt = act(ht3[:, :, k * 128:k * 128 + 128], BK[b][:, :].rearrange("p (t d) -> p t d", t=4), ACT.Copy, m, start)
                bfree[b] = [mt]
            mx = []
            for k in range(KT):
                for hf in range(2):
                    b = (2 * k + hf) % 4
                    m = mms([(BK[b][:, :], ht3[:, t, k * 128:k * 128 + 128], sel3[:, t, hf * 512:hf * 512 + 512], t == 0, t == 3)
                             for t in range(4)], ms, mt, *bfree[b])
                    m = act(xe3[:, k, hf * 512:hf * 512 + 512], BK[b][:, :], ACT.Copy, m, start)
                    bfree[b] = [m]
                    mx.append(m)
            dist = SEL.rearrange("p (e t) -> p e t", e=8)
            AB = HT[:, 0:1024]
            mdist = []
            gathered = now()
            for pr in range(8):
                m = mms([(BK[4][:, :], PAIR[:, pr * 128:pr * 128 + 128], RKs[0:16, :], True, True)], mr, mpair, *bfree[4])
                m1 = mms([(BK[5][:, :], PAIR[:, pr * 128:pr * 128 + 128], AFT[0:16, :], True, True)], ma, *bfree[5])
                ab = AB[:, 512 * (pr % 2):512 * (pr % 2) + 512]
                m1 = act(ab, BK[5][:, :], ACT.Copy, m1, gathered, mdist[-2:])
                bfree[5] = [m1]
                m = stt(dist[:, pr, :], BK[4][:, :], C("misc")[:, 1:2], ab, ALU.is_equal, MUL, m, m1, gathered)
                bfree[4] = [m]
                mdist.append(m)
            ready_e = now()
            SG, HI, HIT = HT[:, 0:1024], HT[:, 1024:2048], HT[:, 2048:4096]
            st = {}

            def ffn(name, pr, banks, lhs, *marks):
                for e in range(2):
                    rows = slice(64 * e, 64 * e + 64)
                    for g in range(4):
                        k, (v,), tk = load((0, (0, P), (2, 1024), a[name][2 * pr + e, g * 256:g * 256 + 256, :].rearrange("(k p) n -> p k n", p=P)))
                        m = mms([(BK[banks[hf]][rows, :], lhs(2 * g + j, e), v[:, j, hf * 512:hf * 512 + 512],
                                  g == 0 and j == 0, g == 3 and j == 1) for j in range(2) for hf in range(2)],
                                tk, *bfree[banks[0]], *bfree[banks[1]], *marks)
                        wfree[k] = [m]
                return m

            def gate_of(pr):
                m = ffn("w_gate_2", pr, (0, 1), lambda k, e: xe3[:, k, (2 * pr + e) * 64:(2 * pr + e) * 64 + 64], mx)
                for hf in range(2):
                    m1 = act(SG[:, hf * 512:hf * 512 + 512], BK[hf][:, :], ACT.Silu, m, ready_e, st.get("hi"))
                    bfree[hf] = [m1]
                st["sg"] = m1

            def up_of(pr):
                m = ffn("w_up_2", pr, (2, 3), lambda k, e: xe3[:, k, (2 * pr + e) * 64:(2 * pr + e) * 64 + 64], mx)
                for hf in range(2):
                    m1 = tt(DV, HI[:, hf * 512:hf * 512 + 512], BK[2 + hf][:, :], SG[:, hf * 512:hf * 512 + 512], MUL,
                            m, st["sg"], ready_e, st.get("tr"))
                    bfree[2 + hf] = [m1]
                st["hi"] = m1

            def down_of(pr):
                hit = HIT[:, 0:1024].rearrange("p (f s) -> p f s", f=8)
                mm_ = []
                for hf in range(2):
                    b = 6 + hf
                    m = trs([(BK[b][:, f * 128:f * 128 + 128], HI[:, hf * 512 + f * 128:hf * 512 + f * 128 + 128]) for f in range(4)],
                            st["hi"], *bfree[b])
                    m1 = act(hit[:, 4 * hf:4 * hf + 4, :], BK[b][:, :].rearrange("p (f s) -> p f s", f=4), ACT.Copy, m, st.get("dn"))
                    bfree[b] = [m1]
                    mm_.append(m1)
                st["tr"] = m
                m = ffn("w_down_2", pr, (4, 5), lambda f, e: hit[:, f, 64 * e:64 * e + 64], mm_)
                st["dn"] = m
                for hf in range(2):
                    m1 = act(ye3[:, pr, hf * 512:hf * 512 + 512], BK[4 + hf][:, :], ACT.Copy, m)
                    bfree[4 + hf] = [m1]
                st["ye"] = m1

            gate_of(0)
            up_of(0)
            for pr in range(8):
                if pr < 7:
                    gate_of(pr + 1)
                down_of(pr)
                if pr < 7:
                    up_of(pr + 1)
            evac = residual(mod2[:, 40:48])
            for k in range(KT):
                b = k % 4
                m = mms([(BK[b][:, :], ye3[:, pr, k * 128:k * 128 + 128], dist[:, pr, :], pr == 0, pr == 7) for pr in range(8)],
                        st["ye"], mdist, *bfree[b])
                bfree[b] = [evac(k, b, m)]
            mf = norm_mod(x3, col("g_final_2", 0, 8), None, None, 7, now())
            ot = A[:, 0:4096].rearrange("p (t d) -> p t d", t=4)
            mo = now()
            for k in range(KT):
                b = k % 4
                m = trs([(BK[b][:, t * 128:t * 128 + 128], x3[:, k, t * 128:t * 128 + 128]) for t in range(4)], mf[k], *bfree[b])
                m = act(ot[:, :, k * 128:k * 128 + 128], BK[b][:, :].rearrange("p (t d) -> p t d", t=4), ACT.Copy, m, mo)
                bfree[b] = [m]
            s_out = new_sem("s_out")
            m = SY.dma(s_out, 16, lambda e: e.dma_start(out.rearrange("(t p) d -> p t d", p=P), ot), m)
            SY.wait(m)

        body()
        block = ctx.enter_context(nc.Block())

        @block.sync
        def _(eng):
            SY.play(eng)

        @block.scalar
        def _(eng):
            AC.play(eng)

        @block.vector
        def _(eng):
            DV.play(eng)

        @block.gpsimd
        def _(eng):
            GP.play(eng)

        @block.tensor
        def _(eng):
            PE.play(eng)


_WHOLE = ["kv_mod_w", "kv_w"]
_FIRST = ["rw_wr", "rw_wk", "rw_wv", "rw_wo", "rw_w1", "rw_w2", "rw_a1", "rw_a2", "rw_g1", "rw_g2", "fx_wqg", "fx_wo",
          "w_mod_2", "w_in_2", "w_uq_2", "w_ukv_2", "w_o_dn_2", "w_o_mla_2", "w_out_2", "w_router_2",
          "w_gate_2", "w_up_2", "w_down_2"]
_LAYERS = ["mod_w", "mlp_up", "mlp_down"]


def _columns(inputs):
    g = {k: np.asarray(v) for k, v in inputs.items()}

    def by128(v):
        return v.reshape(-1, 128).T

    def tiled(v, n):
        return np.tile(v.reshape(-1), n).reshape(-1, 128).T

    def rows(v):
        return np.tile(v.reshape(1, -1), (128, 1))

    out = []
    for name, w in VECS:
        if name in ("mod_b0", "mod_b1", "norm_mix_g0", "norm_mix_g1", "norm_mlp_g0", "norm_mlp_g1"):
            v = by128(g[name[:-1]][int(name[-1])])
        elif name == "conv_w_2":
            v = g[name][0].reshape(5, 24, 128).transpose(2, 1, 0).reshape(128, 120)
        elif name in ("kv_kg", "fx_qg"):
            v = tiled(g[name], 2)
        elif name in ("kv_fb", "a_log_2", "dt_bias_2"):
            v = rows(g[name])
        else:
            v = by128(g[name])
        assert v.shape == (128, w), (name, v.shape)
        out.append(v)
    return np.ascontiguousarray(np.concatenate(out, axis=1))


def arrays_of(inputs):
    g = {k: np.asarray(v) for k, v in inputs.items()}
    arr = {"x": g["x"][0], "pos": g["positions_2"], "const": _CARR, "pair": _PAIR, "cols": _columns(inputs)}
    for n in _WHOLE:
        arr[n] = g[n]
    for n in _FIRST:
        arr[n] = g[n][0]
    for n in _LAYERS:
        arr[n + "0"], arr[n + "1"] = g[n][0], g[n][1]
    return {f"in_{n}": np.ascontiguousarray(v) for n, v in arr.items()}


def kernel(**inputs):
    import concourse.bacc as _bacc
    from concourse.bass_utils import run_bass_kernel_spmd as _run

    nc = _bacc.Bacc("TRN2", target_bir_lowering=False, num_devices=1)
    arrays = arrays_of(inputs)
    a = {n[3:]: nc.dram_tensor(n, v.shape, mybir.dt.from_np(v.dtype), kind="ExternalInput").ap()
         for n, v in arrays.items()}
    out = nc.dram_tensor("out_0", (T, D), F32, kind="ExternalOutput").ap()
    program(nc, a, out)
    r = _run(nc, [arrays], core_ids=[0])
    return r.results[0]["out_0"].reshape(1, T, D)
```

```python
import numpy as np
from contextlib import ExitStack
import concourse.bass as bass
from concourse import mybir

F32 = mybir.dt.float32
I32 = mybir.dt.int32
ALU = mybir.AluOpType
ACT = mybir.ActivationFunctionType
AX = mybir.AxisListType.X
P = 128
T = 512
D = 1024
KT = 8
EXPM05 = float(np.exp(-0.5))
MUL, ADD, SUB = ALU.mult, ALU.add, ALU.subtract


class Queue:

    def __init__(self, sem, serial=False):
        self.sem, self.n, self.items, self.past, self.serial = sem, 0, [], {}, serial

    def wait(self, *marks):
        for m in marks:
            if m is None:
                continue
            if isinstance(m, list):
                self.wait(*m)
                continue
            sem, v = m
            if self.past.get(id(sem), 0) < v:
                self.past[id(sem)] = v
                self.items.append((sem, v))

    def __call__(self, fn, *marks):
        self.wait(*marks)
        if self.serial and self.n:
            self.wait((self.sem, self.n))
        self.n += 1
        sem = self.sem
        self.items.append(lambda e: fn(e).then_inc(sem, 1))
        return (sem, self.n)

    def silent(self, fn, *marks):
        self.wait(*marks)
        self.items.append(fn)

    def dma(self, sem, count, fn, *marks):
        self.wait(*marks)
        self.items.append(lambda e: fn(e).then_inc(sem, 16))
        return (sem, count)

    def play(self, eng):
        for it in self.items:
            if isinstance(it, tuple):
                eng.wait_ge(it[0], it[1])
            else:
                it(eng)


def weave(*streams):
    live = [s if isinstance(s, tuple) else (s, 1) for s in streams]
    turn = 0
    while live:
        every = min(n for _, n in live)
        for s, n in list(live):
            if (n == every or turn % n == 0) and next(s, StopIteration) is StopIteration:
                live.remove((s, n))
        turn += 1


def run(stream):
    for _ in stream:
        pass


def chain(*streams):
    for s in streams:
        yield from s()


VECS = [
    ("c", 8), ("c_2", 8), ("mod_b0", 48), ("mod_b1", 48), ("kv_mod_b", 16), ("b_mod_2", 48),
    ("norm_mix_g0", 8), ("norm_mix_g1", 8), ("norm_mlp_g0", 8), ("norm_mlp_g1", 8),
    ("rw_mu", 48), ("rw_w0", 8), ("rw_a0", 8), ("rw_kk", 8), ("rw_ka", 8), ("rw_rk", 8),
    ("rw_lnw", 8), ("rw_lnb", 8), ("kv_norm_g", 8), ("kv_kg", 1), ("fx_qg", 1), ("final_g", 8),
    ("kv_fb", 16), ("g_mix_2", 8), ("conv_w_2", 120), ("a_log_2", 16), ("dt_bias_2", 16),
    ("dn_o_gain_2", 1), ("q_gain_2", 4), ("kv_gain_2", 2), ("g_ffn_2", 8), ("g_final_2", 8),
]
COL = {}
NCOL = 0
for _n, _w in VECS:
    COL[_n] = (NCOL, _w)
    NCOL += _w


def consts():
    j = np.arange(128)[:, None]
    i = np.arange(128)[None, :]
    out = {"ident": (i == j), "incl": (j <= i), "ones": np.ones((128, 128)),
           "onesB": np.ones((128, 128)), "onesC": np.ones((128, 128)),
           "blk": (i // 64 == j // 64), "strict": (j < i),
           "strictR": (j > i), "inclR": (j >= i),
           "neg": np.where(i <= j, 0.0, -1e30)}
    for n in range(7):
        s = 1 << n
        out[f"lv{n}"] = (j // (2 * s) == i // (2 * s)) & (j % (2 * s) < s) & (i % (2 * s) >= s)
    for n in range(7):
        out[f"lvR{n}"] = out[f"lv{n}"].T
    perm = np.zeros((128, 128))
    for m in range(32):
        perm[m + 32, m] = -1.0
        perm[m, m + 32] = 1.0
    out["perm"] = perm
    freq = (np.float32(10000.0) ** (-np.arange(32, dtype=np.float32) / np.float32(32))).astype(np.float32)
    f = np.tile(np.arange(128), (128, 1)).astype(np.float32)
    f[:, 64] = np.tile(freq, 4)
    f[:, 65] = np.arange(128) % 64
    out["iota"] = f
    half = np.zeros((128, 1024))
    for pr in range(8):
        for q in range(128):
            half[2 * pr + q // 64, pr * 128 + q] = 1.0
    names = list(out)
    arr = np.concatenate([out[n].astype(np.float32) for n in names], axis=1)
    return {n: k for k, n in enumerate(names)}, arr, half[:16].astype(np.float32)


CON, _CARR, _PAIR = consts()




def program(nc, a, out):
    ctx = ExitStack()
    with ctx:
        def sb(name, cols, dt=F32):
            return ctx.enter_context(nc.sbuf_tensor(name, [P, cols], dt))

        def new_sem(name):
            return ctx.enter_context(nc.semaphore(name))

        PE, SY = Queue(new_sem("pe")), Queue(new_sem("sp"))
        DV, AC, GP = (Queue(new_sem(n), serial=True) for n in ("dve", "act", "pool"))
        BK = [ctx.enter_context(nc.psum_tensor(f"bank{i}", [P, 512], F32)) for i in range(8)]
        bfree = [[] for _ in range(8)]

        X = sb("X", 4096)
        H = sb("H", 4096)
        NS = 5
        W = sb("W", NS * 2048)
        NCON = _CARR.shape[1]
        con = sb("con", NCON)
        cols = sb("cols", NCOL)
        mods = sb("mods", 48 * 3 + 16 + 64)
        ARENA = 27456
        A = sb("A", ARENA)
        SM = sb("SM", 3072)

        x3 = X[:, :].rearrange("p (k t) -> p k t", k=KT)
        h3 = H[:, :].rearrange("p (k t) -> p k t", k=KT)

        def C(name, n=128):
            k = CON[name] * 128
            return con[:, k:k + n]

        def col(name, k=0, n=1):
            o, w = COL[name]
            return cols[:, o + k:o + k + n]

        def now():
            return [(q.sem, q.n) for q in (PE, DV, AC, GP) if q.n]

        class Carve:
            def __init__(self):
                self.at = 0

            def __call__(self, n):
                self.at += n
                assert self.at <= ARENA, self.at
                return A[:, self.at - n:self.at]

        wsem = [new_sem(f"w{k}") for k in range(NS)]
        wcount = [0] * NS
        wfree = [[] for _ in range(NS)]
        wnext = [0]
        nring = [NS]

        def load(*parts):
            k = wnext[0] % nring[0]
            wnext[0] += 1
            views, mark = [], None
            for off, rows, shape, src in parts:
                n = 1
                for s in shape:
                    n *= s
                assert off + n <= 2048
                v = W[rows[0]:rows[1], k * 2048 + off:k * 2048 + off + n]
                if len(shape) == 2:
                    v = v.rearrange("p (a b) -> p a b", a=shape[0])
                views.append(v)
                wcount[k] += 16
                mark = SY.dma(wsem[k], wcount[k], lambda e, v=v, src=src: e.dma_start(v, src), *wfree[k])
            wfree[k] = []
            return k, views, mark

        def mms(items, *marks):
            PE.wait(*marks)
            for n, (o, l, r, s, e) in enumerate(items):
                f = lambda eng, o=o, l=l, r=r, s=s, e=e: eng.matmul(o, l, r, start=s, stop=e, skip_group_check=True)
                if n + 1 < len(items):
                    PE.silent(f)
                else:
                    return PE(f)

        def trs(items, *marks):
            PE.wait(*marks)
            for n, (o, i) in enumerate(items):
                f = lambda eng, o=o, i=i: eng.transpose(o, i, C("ident")[0:i.shape[0], 0:i.shape[0]])
                if n + 1 < len(items):
                    PE.silent(f)
                else:
                    return PE(f)

        def act(o, i, func, *marks, scale=1.0, bias=0.0, accum=None):
            if accum is not None:
                return AC(lambda e: e.activation(o, i, func, bias=bias, scale=scale, accum_out=accum), *marks)
            return AC(lambda e: e.activation(o, i, func, bias=bias, scale=scale), *marks)

        def tt(q, o, x, y, op, *marks):
            return q(lambda e: e.tensor_tensor(o, x, y, op), *marks)

        def ts(q, o, x, s1, s2, op0, op1, *marks):
            if op1 is None:
                return q(lambda e: e.tensor_scalar(o, x, s1, None, op0), *marks)
            return q(lambda e: e.tensor_scalar(o, x, s1, s2, op0, op1), *marks)

        def rroot(o, *marks):
            m = DV(lambda e: e.reciprocal(o, o), *marks)
            return act(o, o, ACT.Sqrt, m)

        def stt(o, x, s, y, op0, op1, *marks):
            return DV(lambda e: e.scalar_tensor_tensor(out=o, in0=x, scalar=s, in1=y, op0=op0, op1=op1), *marks)


        def body():
            s_in = new_sem("s_in")
            for n, (o, s) in enumerate([(con[:, :], a["const"]), (cols[:, :], a["cols"])]):
                m_in = SY.dma(s_in, 16 * (n + 1), lambda e, o=o, s=s: e.dma_start(o, s))
            ready = m_in
            xtok = A[:, 0:4096].rearrange("p (t d) -> p t d", t=4)
            s_x = new_sem("s_x")
            mx = SY.dma(s_x, 16, lambda e: e.dma_start(xtok, a["x"].rearrange("(t p) d -> p t d", p=P)))
            for q in (PE, DV, AC, GP):
                q.wait(ready)
            last = None
            for k in range(KT):
                b = k % 4
                t = trs([(BK[b][:, tk * 128:(tk + 1) * 128], xtok[:, tk, k * 128:(k + 1) * 128]) for tk in range(4)],
                        mx, *bfree[b])
                last = act(x3[:, k, :], BK[b][:, :], ACT.Copy, t)
                bfree[b] = [last]
            xdone = last

            def silu_cols(o, i, tmp):
                m = act(tmp, i, ACT.Sigmoid)
                return tt(DV, o, i, tmp, MUL, m)

            cact = sb("cact", 32)
            m_c = [silu_cols(cact[:, 0:8], col("c", 0, 8), cact[:, 16:24]),
                   silu_cols(cact[:, 8:16], col("c_2", 0, 8), cact[:, 24:32])]
            rowb = SM[:, 0:1024]
            rfree = [[], []]

            def mod_stream(o, w, n, cc, bias, bc):
                marks = list(bfree[bc])
                for g in range(n // 512):
                    acc = rowb[:, (g % 2) * 512:(g % 2) * 512 + 512]
                    m = None
                    for hf in range(2):
                        k, (v,), tk = load((0, (0, P), (4, 512), w[hf * 512:(hf + 1) * 512, g * 512:(g + 1) * 512].rearrange("(k p) n -> p k n", p=P)))
                        for j in range(4):
                            c = cact[:, cc + 4 * hf + j:cc + 4 * hf + j + 1]
                            if hf == 0 and j == 0:
                                m = ts(DV, acc, v[:, j, :], c, None, MUL, None, tk, m_c, *rfree[g % 2])
                            else:
                                m = stt(acc, v[:, j, :], c, acc, MUL, ADD, tk, m)
                        wfree[k] = [m]
                        yield
                    m = mms([(BK[bc][:, 4 * g + j:4 * g + j + 1], acc[:, j * 128:(j + 1) * 128], C("ones", 1), True, True)
                             for j in range(4)], m, *marks)
                    rfree[g % 2] = [m]
                    yield
                m = tt(DV, o, BK[bc][:, 0:n // 128], bias, ADD, m)
                bfree[bc] = [m]
                mod_mark.append(m)
                yield

            mod_mark = []
            mod0, mod1, mod2 = (mods[:, 48 * k:48 * k + 48] for k in range(3))
            modk = mods[:, 144:160]
            gs = mods[:, 160:168]
            g1 = mods[:, 168:176]

            def rsum_free(b):
                return bfree[b]

            sqb = SM[:, 1024:2048]
            sqf = [[], []]
            rstd = SM[:, 2048:2560]
            rstd_r = []

            def rms_rstd(src, nk, inv_n, eps, b, *marks, o=None):
                m = None
                for k in range(nk):
                    s = sqb[:, (k % 2) * 512:(k % 2) * 512 + 512]
                    m1 = act(s, src[:, k, :], ACT.Square, *marks, *sqf[k % 2])
                    m = mms([(BK[b][:, :], C("ones"), s, k == 0, k == nk - 1)], m1, *bfree[b])
                    sqf[k % 2] = [m]
                oo = rstd[:, :] if o is None else o
                m = ts(DV, oo, BK[b][:, :], inv_n, eps, MUL, ADD, m, *rstd_r)
                bfree[b] = [m]
                return rroot(oo, m)

            def norm_mod(o3, g, sc, sh, b, *marks):
                m = rms_rstd(x3, KT, 1.0 / D, 1e-6, b, *marks)
                if sc is not None:
                    mg = ts(DV, gs, sc, 1.0, None, ADD, None, *marks)
                    mg = tt(DV, gs, gs, g, MUL, mg)
                last = []
                for k in range(KT):
                    m1 = tt(DV, o3[:, k, :], x3[:, k, :], rstd[:, :], MUL, m, *marks)
                    if sc is not None:
                        last.append(act(o3[:, k, :], o3[:, k, :], ACT.Identity, m1, mg, *marks,
                                        scale=gs[:, k:k + 1], bias=sh[:, k:k + 1]))
                    else:
                        last.append(act(o3[:, k, :], o3[:, k, :], ACT.Copy, m1, scale=g[:, k:k + 1]))
                rstd_r[:] = [m1]
                return last

            def proj(w, src3, nk, n, banks, evac, *marks, width=256):
                j = 0
                for n0 in range(0, n, width):
                    wd = min(width, n - n0)
                    k, (v,), tk = load((0, (0, P), (nk, wd), w[:, n0:n0 + wd].rearrange("(k p) n -> p k n", p=P)))
                    for c in range(0, wd, 128):
                        cw = min(128, wd - c)
                        b = banks[j % len(banks)]
                        m = mms([(BK[b][0:cw, :], v[:, kk, c:c + cw], src3[:, kk, :], kk == 0, kk == nk - 1)
                                 for kk in range(nk)], tk, *bfree[b], *marks)
                        bfree[b] = [evac(j, b, m)]
                        j += 1
                        yield
                    wfree[k] = [m]

            run(mod_stream(mod0, a["mod_w0"], 6144, 0, col("mod_b0", 0, 48), 6))
            cv = Carve()
            XM = cv(3 * 4096)
            xm = [XM[:, 4096 * j:4096 * j + 4096].rearrange("p (k t) -> p k t", k=KT) for j in range(3)]
            LO = cv(512)
            ZG = cv(1024)
            XX = cv(4096)
            xx3 = XX.rearrange("p (k t) -> p k t", k=KT)
            MX = cv(1024)
            mh = norm_mod(h3, col("norm_mix_g0", 0, 8), mod0[:, 8:16], mod0[:, 0:8], 7, xdone, mod_mark[-1])
            start = now()
            xpark = nc.dram_tensor("xpark", (P, 4096), F32, kind="Internal").ap()
            s_park = new_sem("s_park")
            m_park = SY.dma(s_park, 16, lambda e: e.dma_start(xpark, X[:, :]), start)
            mxx = []
            for k in range(KT):
                m1 = tt(DV, xx3[:, k, 1:T], h3[:, k, 0:T - 1], h3[:, k, 1:T], SUB, start)
                mxx.append([m1, ts(DV, xx3[:, k, 0:1], h3[:, k, 0:1], -1.0, None, MUL, None)])

            def mix(o, j, k, *marks):
                return stt(o, xx3[:, k, :], col("rw_mu", 8 * j + k), h3[:, k, :], MUL, ADD, mxx[k], *marks)

            k1, (w1v, a1v, g1v), tk1 = load((0, (0, P), (8, 64), a["rw_w1"].rearrange("(k p) n -> p k n", p=P)),
                                            (512, (0, P), (8, 64), a["rw_a1"].rearrange("(k p) n -> p k n", p=P)),
                                            (1024, (0, P), (8, 96), a["rw_g1"][:, 0:96].rearrange("(k p) n -> p k n", p=P)))
            k2, (g1w,), tk2 = load((0, (0, P), (8, 64), a["rw_g1"][:, 96:160].rearrange("(k p) n -> p k n", p=P)))
            mfree = [[], []]
            n = 0
            for j in (1, 4, 5):
                for k in range(KT):
                    mb = MX[:, (n % 2) * 512:(n % 2) * 512 + 512]
                    m = mix(mb, j, k, *mfree[n % 2])
                    f, l = k == 0, k == KT - 1
                    if j == 1:
                        m = mms([(BK[0][0:64, :], w1v[:, k, :], mb, f, l)], m, tk1, *bfree[0])
                    elif j == 4:
                        m = mms([(BK[1][64:128, :], a1v[:, k, :], mb, f, l)], m, *bfree[1])
                    else:
                        m = mms([(BK[2][0:96, :], g1v[:, k, :], mb, f, l), (BK[3][0:64, :], g1w[:, k, :], mb, f, l)],
                                m, tk2, *bfree[2], *bfree[3])
                    mfree[n % 2] = [m]
                    n += 1
                if j == 1:
                    ml = [act(LO[0:64, :], BK[0][0:64, :], ACT.Tanh, m)]
                    bfree[0] = [ml[-1]]
                elif j == 4:
                    ml.append(act(LO[64:128, :], BK[1][64:128, :], ACT.Copy, m))
                    bfree[1] = [ml[-1]]
                else:
                    ml.append(act(ZG[0:96, 0:512], BK[2][0:96, :], ACT.Sigmoid, m))
                    ml.append(act(ZG[0:64, 512:1024], BK[3][0:64, :], ACT.Sigmoid, m))
                    bfree[2], bfree[3] = [ml[-2]], [ml[-1]]
            wfree[k1] = [m]
            wfree[k2] = [m]
            for d, j in ((0, 0), (1, 2), (2, 3)):
                for k in range(KT):
                    m = mix(xm[d][:, k, :], j, k)
                    ml.append(m)
            omka = mods[:, 176:184]
            ml.append(ts(DV, omka, col("rw_ka", 0, 8), -1.0, 1.0, MUL, ADD))
            start = now()

            cv.at = 3 * 4096 + 512 + 1024
            xa = [X[:, 512 * j:512 * j + 512] for j in range(8)]
            Rb, Kb, Lw, Ab, KKb, Lb, t0, t1 = xa
            nring[0] = NS - 1
            w4 = NS * 2048 - 2048
            spare = [W[:, w4 + 512 * j:w4 + 512 * j + 512] for j in range(4)] + [SM[:, 512 * j:512 * j + 512] for j in range(6)]
            start = [start, wfree[NS - 1]]
            sets = [[cv(1024)] + [cv(512) for _ in range(6)] for _ in range(2)]
            hw = [[cv(512) for _ in range(8)], spare[0:8]]
            BHt, Yb = cv(512), cv(512)
            KHt, Vt = spare[8:10]
            sm = cv(64)
            SS, SP = cv(64), cv(64)
            c4 = lambda v: v.rearrange("p (c t) -> p c t", c=4)
            yg = h3
            for w_ in hw:
                for z in (w_[0], w_[5], w_[6], w_[7]):
                    zm = GP(lambda e, z=z: e.memset(z, 0.0), start)
            for s_ in sets:
                for z in (s_[1][64:128, :], s_[2][0:64, :], s_[3][64:128, :], s_[4][0:64, :]):
                    zm = GP(lambda e, z=z: e.memset(z, 0.0), start)

            def prep(ct, since):
                AR, BHa, BHb, KHa, KHb, V, BO = sets[ct % 2]
                ar = AR.rearrange("p (c s t) -> p c s t", c=4, s=2)
                cs = slice(ct * 128, ct * 128 + 128)
                k1, (wr, wk), tk1 = load((0, (0, P), (8, 128), a["rw_wr"][:, cs].rearrange("(k p) n -> p k n", p=P)),
                                         (1024, (0, P), (8, 128), a["rw_wk"][:, cs].rearrange("(k p) n -> p k n", p=P)))
                k2, (wv, w2, a2), tk2 = load(
                    (0, (0, P), (8, 128), a["rw_wv"][:, cs].rearrange("(k p) n -> p k n", p=P)),
                    (1024, (0, 64), (128,), a["rw_w2"][:, cs]), (1024, (64, 128), (128,), a["rw_a2"][:, cs]))

                def big(b, w, src, tk):
                    for q in range(4):
                        m = mms([(BK[b][:, :], w[:, k, :], src[:, k, :], k == 0, k == 7) for k in (2 * q, 2 * q + 1)],
                                tk, *bfree[b], *since)
                        if q < 3:
                            yield
                    bigs.append(m)

                bigs = []
                yield from big(0, wk, xm[1], tk1)
                m = bigs[-1]
                mk = act(Kb, BK[0][:, :], ACT.Copy, m, *since)
                bfree[0] = [mk]
                m1 = ts(DV, KKb, Kb, col("rw_kk", ct), None, MUL, None, mk, *since)
                m2 = act(t0, KKb, ACT.Square, m1, *since)
                yield
                yield from big(1, wr, xm[0], tk1)
                m = bigs[-1]
                wfree[k1] = [m]
                mr = act(Rb, BK[1][:, :], ACT.Copy, m, *since)
                bfree[1] = [mr]
                yield
                m = mms([(BK[0][:, :], C("blk"), t0, True, True)], m2, *bfree[0])
                m = ts(DV, t0, BK[0][:, :], 1e-24, None, ALU.max, None, m)
                bfree[0] = [m]
                m = rroot(t0, m)
                mkk = tt(DV, KKb, KKb, t0, MUL, m)
                yield
                m = mms([(BK[0][:, :], w2[:, :], LO[0:64, :], True, True)], tk2, *bfree[0])
                m1 = act(Lw, BK[0][:, :], ACT.Sigmoid, m, *since, bias=col("rw_w0", ct))
                bfree[0] = [m1]
                m = mms([(BK[1][:, :], a2[:, :], LO[64:128, :], True, True)], *bfree[1])
                ma = act(Ab, BK[1][:, :], ACT.Sigmoid, m, *since, bias=col("rw_a0", ct))
                bfree[1] = [ma]
                mlw = ts(DV, Lw, Lw, -EXPM05, None, MUL, None, m1)
                yield
                for c in range(4):
                    s = slice(c * 128, c * 128 + 128)
                    mL = DV(lambda e, s=s: e.tensor_tensor_scan(Lb[:, s], C("ones"), Lw[:, s], 0.0, MUL, ADD), mlw, *since)
                yield from big(1, wv, xm[2], tk2)
                m = bigs[-1]
                wfree[k2] = [m]
                mv = act(V, BK[1][:, :], ACT.Copy, m, *since)
                bfree[1] = [mv]
                yield
                L3 = c4(Lb)
                eM, eE = sm[:, 16 * (ct % 2):16 * (ct % 2) + 4], sm[:, 16 * (ct % 2) + 4:16 * (ct % 2) + 8]
                mid = sm[:, 16 * (ct % 2) + 8:16 * (ct % 2) + 12]
                m1 = DV(lambda e: e.tensor_copy(mid, L3[:, :, 63]), mL, *since)
                m2 = tt(DV, eE, L3[:, :, 127], mid, SUB, m1)
                mE = act(eE, eE, ACT.Exp, m2)
                mM = act(eM, mid, ACT.Exp, m1)
                for c in range(4):
                    mL = ts(DV, L3[:, c, :], L3[:, c, :], mid[:, c:c + 1], None, SUB, None, m1)
                m = ts(DV, t0, Ab, col("rw_ka", ct), omka[:, ct:ct + 1], MUL, ADD, ma)
                mk2 = tt(DV, Kb, Kb, t0, MUL, m)
                yield
                m1 = act(t0, Lb, ACT.Exp, mL, mk2)
                mRh = tt(DV, ar[:, :, 1, :], c4(Rb), c4(t0), MUL, m1, mr, *since)
                m2 = tt(DV, t1, Lb, Lw, SUB, mL)
                m2 = act(t1, t1, ACT.Exp, m2)
                mAh = stt(ar[:, :, 0, :], c4(t1), -1.0, c4(KKb), MUL, MUL, m2, mkk)
                yield
                m1 = act(t0, Lb, ACT.Exp, mRh, scale=-1.0)
                mKh = [tt(DV, KHa[0:64, :], Kb[0:64, :], t0[0:64, :], MUL, m1, zm, *since),
                       tt(DV, KHb[64:128, :], Kb[64:128, :], t0[64:128, :], MUL)]
                m2 = tt(GP, t1, KKb, Ab, MUL, mAh, mkk)
                mBh = [tt(DV, BHa[0:64, :], t1[0:64, :], t0[0:64, :], MUL, m2, m1, *since),
                       tt(DV, BHb[64:128, :], t1[64:128, :], t0[64:128, :], MUL)]
                yield
                m = stt(t1, Rb, col("rw_rk", ct), Kb, MUL, MUL, mBh)
                m = mms([(BK[0][:, :], C("blk"), t1, True, True)], m, *bfree[0])
                mbo = tt(DV, BO, BK[0][:, :], V, MUL, m, mv, *since)
                bfree[0] = [mbo]
                prepared[ct] = [mRh, mAh, mKh, mBh, mbo, mv, mE, mM]
                used_tmp[ct] = now()
                yield

            def invert(NT, TT, TM, US, MT, R, banks, nb, sfree, m_nt):
                bu, bt, bm = banks
                c3 = lambda v: v.rearrange("p (c t) -> p c t", c=nb)
                bc = lambda name: C(name).unsqueeze(1).broadcast_to([P, nb, 128])
                lv = "lvR" if R else "lv"
                n3, t3, m3 = c3(NT), c3(TT), c3(TM)
                u3, k3 = c3(US), c3(MT)
                q = slice(0, nb * 128)
                m = tt(GP, k3, n3, bc(lv + "0"), MUL, m_nt, *sfree)
                mt_t = tt(GP, t3, k3, bc("ident"), ADD, m)
                m1 = mms([(BK[bu][:, c * 128:c * 128 + 128], k3[:, c, :], C("ident"), True, True) for c in range(nb)],
                         m, *bfree[bu])
                mt_m = tt(DV, m3, c3(BK[bu][:, q]), bc("ident"), ADD, m1, *sfree)
                bfree[bu] = [mt_m]
                mk_r = m1
                yield
                for lev in range(1, 7):
                    last = lev == 6
                    m = tt(GP, k3, n3, bc(lv + str(lev)), MUL, mk_r)
                    mu = mms([(BK[bu][:, c * 128:c * 128 + 128], k3[:, c, :], m3[:, c, :], True, True) for c in range(nb)],
                             m, mt_m, *bfree[bu])
                    mk_r = mu
                    me = act(US, BK[bu][:, q], ACT.Copy, mu)
                    bfree[bu] = [me]
                    yield
                    mA = mms([(BK[bt][:, c * 128:c * 128 + 128], u3[:, c, :], t3[:, c, :], True, True) for c in range(nb)],
                             me, mt_t, *bfree[bt])
                    if not last:
                        mB = mms([(BK[bm][:, c * 128:c * 128 + 128], t3[:, c, :], u3[:, c, :], True, True)
                                  for c in range(nb)], *bfree[bm])
                        mt_m = tt(DV, m3, m3, c3(BK[bm][:, q]), ADD, mB)
                        bfree[bm] = [mt_m]
                        mt_t = tt(DV, t3, t3, c3(BK[bt][:, q]), ADD, mB)
                    else:
                        mt_t = tt(DV, t3, t3, c3(BK[bt][:, q]), ADD, mA)
                    bfree[bt] = [mt_t]
                    yield
                inverse.append(mt_t)

            inverse = []
            prepared, used_tmp, chunked, headed = {}, {}, {}, {}

            def head(ct, hd, tok, mz):
                AR, BHa, BHb, KHa, KHb, V, BO = sets[ct % 2]
                NT, TT, TM, US, MT, AKT, RBT, RKT = hw[hd]
                XS, UU = MT[:, 0:64], MT[:, 64:128]
                ar = AR.rearrange("p (c s t) -> p c s t", c=4, s=2)
                eM, eE = sm[:, 16 * (ct % 2):16 * (ct % 2) + 4], sm[:, 16 * (ct % 2) + 4:16 * (ct % 2) + 8]
                hp = slice(64 * hd, 64 * hd + 64)
                pm = prepared[ct]
                ba, bb, bc = (2, 3, 4) if hd == 0 else (5, 6, 7)
                before = [headed[ct - 1]] if ct else []
                msc = []
                for n, (src, dA, dR, pr) in enumerate([(BHb if hd else BHa, NT, RBT, 0), (BHb if hd else BHa, NT, RBT, 1),
                                                       (KHb if hd else KHa, AKT, RKT, 0), (KHb if hd else KHa, AKT, RKT, 1)]):
                    b = (ba, bb, bc)[n % 3]
                    items = []
                    for cc in range(2):
                        c = 2 * pr + cc
                        o = BK[b][:, cc * 256:cc * 256 + 256].rearrange("p (s t) -> p s t", s=2)
                        items.append((o[0:64, :, :], src[:, c * 128:c * 128 + 64], ar[:, c, :, :], True, True))
                        items.append((o[64:128, :, 64:128], src[:, c * 128 + 64:c * 128 + 128],
                                      ar[:, c, :, 64:128], True, True))
                    m = mms(items, pm, *bfree[b])
                    o4 = BK[b][:, :].rearrange("p (c s t) -> p c s t", c=2, s=2)
                    for s, dst, mask in ((0, dA, "strict"), (1, dR, "incl")):
                        d3 = c4(dst)[:, 2 * pr:2 * pr + 2, :]
                        for rows, lo in ((slice(0, 64), 0), (slice(64, 128), 64)):
                            mk = C(mask)[rows, lo:128].unsqueeze(1).broadcast_to([64, 2, 128 - lo])
                            mm_ = tt(DV, d3[rows, :, lo:128], o4[rows, :, s, lo:128], mk, MUL, m, mz, *before)
                    msc.append(mm_)
                    bfree[b] = [mm_]
                    yield
                yield from invert(NT, TT, TM, US, MT, False, (ba, bb, bc), 4, before, msc)
                mt = inverse[-1]
                ms = GP(lambda e: e.memset(SS[hp, 0:64], 0.0), *before)
                my = None
                for c in range(4):
                    q = slice(c * 128, c * 128 + 128)
                    vt = Vt[:, c * 128 + 64 * hd:c * 128 + 64 * hd + 64]
                    msp = ts(DV, SP[hp, :], SS[hp, :], eM[hp, c:c + 1], None, MUL, None, ms, my)
                    m = mms([(BK[ba][:, 0:64], ar[hp, c, 0, :], SP[hp, :], True, False),
                             (BK[ba][:, 0:64], AKT[:, q], vt, False, True)], msp, tok, msc, *bfree[ba])
                    m = act(XS, BK[ba][:, 0:64], ACT.Copy, m)
                    bfree[ba] = [m]
                    yield
                    m = mms([(BK[bb][:, 0:64], TT[:, q], XS, True, True)], m, mt, *bfree[bb])
                    mu = act(UU, BK[bb][:, 0:64], ACT.Copy, m)
                    bfree[bb] = [mu]
                    yield
                    m = mms([(BK[ba][hp, 64:128], BHt[:, c * 128 + 64 * hd:c * 128 + 64 * hd + 64], UU, True, False),
                             (BK[ba][hp, 64:128], KHt[:, c * 128 + 64 * hd:c * 128 + 64 * hd + 64], vt, False, True)],
                            mu, *bfree[ba])
                    m = tt(DV, SS[hp, :], SP[hp, :], BK[ba][hp, 64:128], ADD, m)
                    bfree[ba] = [m]
                    ms = ts(DV, SS[hp, :], SS[hp, :], eE[hp, c:c + 1], None, MUL, None, m)
                    my = mms([(BK[bc][hp, q], SP[hp, :], ar[hp, c, 1, :], True, False),
                              (BK[bc][hp, q], UU, RBT[:, q], False, False),
                              (BK[bc][hp, q], vt, RKT[:, q], False, True)], *bfree[bc])
                    yield
                my = act(Yb[hp, :], BK[bc][hp, :], ACT.Copy, my, before, chunked.get(ct - 1))
                bfree[bc] = [my]
                ydone[hd] = my
                yield

            ydone = [None, None]

            def heads(ct, mz):
                AR, BHa, BHb, KHa, KHb, V, BO = sets[ct % 2]
                pm = prepared[ct]
                prev = [headed[ct - 1]] if ct else []
                tok = []
                for b, src, dst in ((2, (BHa, BHb), BHt), (5, (KHa, KHb), KHt), (3, (V,), Vt)):
                    m = mms([(BK[b][:, c * 128:c * 128 + 128], s_[:, c * 128:c * 128 + 128], C("ident"), i == 0, i == len(src) - 1)
                             for c in range(4) for i, s_ in enumerate(src)], pm, *bfree[b])
                    m = act(dst, BK[b][:, :], ACT.Copy, m, *prev)
                    bfree[b] = [m]
                    tok.append(m)
                yield
                fs = [head(ct, 0, tok, mz), head(ct, 1, tok, mz)]
                while fs:
                    for f in list(fs):
                        if next(f, StopIteration) is StopIteration:
                            fs.remove(f)
                    yield
                headed[ct] = now()

            def post(ct):
                AR, BHa, BHb, KHa, KHb, US, BO = sets[ct % 2]
                cs = slice(ct * 128, ct * 128 + 128)
                kg, (ga, gb), tkg = load((0, (0, 96), (128,), a["rw_g2"][0:96, cs]), (128, (0, 64), (128,), a["rw_g2"][96:160, cs]))
                m = mms([(BK[0][:, :], C("blk"), Yb, True, True)], ydone, *bfree[0])
                m = stt(Yb, BK[0][:, :], -1.0 / 64, Yb, MUL, ADD, m)
                bfree[0] = [m]
                yield
                m2 = act(US, Yb, ACT.Square, m, headed[ct])
                m2 = mms([(BK[1][:, :], C("blk"), US, True, True)], m2, *bfree[1])
                m2 = ts(DV, US, BK[1][:, :], 1.0 / 64, 64e-5, MUL, ADD, m2)
                bfree[1] = [m2]
                m2 = rroot(US, m2)
                yield
                m = tt(DV, Yb, Yb, US, MUL, m2)
                m = act(Yb, Yb, ACT.Identity, m, scale=col("rw_lnw", ct), bias=col("rw_lnb", ct))
                mg = mms([(BK[0][:, :], ga[:, :], ZG[0:96, 0:512], True, False),
                          (BK[0][:, :], gb[:, :], ZG[0:64, 512:1024], False, True)], tkg, *bfree[0])
                wfree[kg] = [mg]
                yield
                m = tt(DV, Yb, Yb, BO, ADD, m)
                m = tt(DV, yg[:, ct, :], Yb, BK[0][:, :], MUL, m, mg)
                bfree[0] = [m]
                chunked[ct] = [now(), m]
                yield

            start = [start, now(), m_park]
            run(prep(0, start))
            for ct in range(8):
                beside = [lambda ct=ct: post(ct - 1)] if ct else []
                if ct < 7:
                    beside.append(lambda ct=ct: prep(ct + 1, [used_tmp[ct]] + ([headed[ct - 1], chunked[ct - 1]] if ct else [])))
                weave(heads(ct, zm), chain(*beside))
            run(post(7))
            m_ret = SY.dma(s_park, 32, lambda e: e.dma_start(X[:, :], xpark), now())
            nring[0] = NS
            wfree[NS - 1] = now()
            mg1 = ts(DV, g1, mod0[:, 16:24], 1.0, None, ADD, None)

            def residual(gate, *marks):
                def evac(j, b, m):
                    return stt(x3[:, j, :], BK[b][:, :], gate[:, j:j + 1], x3[:, j, :], MUL, ADD, m, *marks)
                return evac

            run(proj(a["rw_wo"], h3, KT, D, (0, 1), residual(g1, mg1, m_ret), now()))
            def down(w, src3, nk, n, pairs, evac, *marks):
                for g in range(n // 256):
                    bs = pairs[g % len(pairs)]
                    for kg in range(nk // 8):
                        k, (v,), tk = load((0, (0, P), (8, 256), w[kg * 1024:kg * 1024 + 1024, g * 256:g * 256 + 256].rearrange("(k p) n -> p k n", p=P)))
                        for c in range(2):
                            m = mms([(BK[bs[c]][:, :], v[:, kk, c * 128:c * 128 + 128], src3[:, kg * 8 + kk, :],
                                      kg == 0 and kk == 0, kg == nk // 8 - 1 and kk == 7) for kk in range(8)],
                                    tk, *bfree[bs[c]], *marks)
                        wfree[k] = [m]
                        yield
                    for c in range(2):
                        bfree[bs[c]] = [evac(2 * g + c, bs[c], m)]

            def mlp(l, g, mod, *beside):
                mh = norm_mod(h3, g, mod[:, 32:40], mod[:, 24:32], 7, now())
                hid = A[:, 0:16384].rearrange("p (k t) -> p k t", k=32)
                mg = ts(DV, g1, mod[:, 40:48], 1.0, None, ADD, None, now())

                def evac(j, b, m):
                    m = act(hid[:, j, :], BK[b][:, :], ACT.Relu, m)
                    hm.append(tt(GP, hid[:, j, :], hid[:, j, :], hid[:, j, :], MUL, m))
                    return m

                hm = []
                def both():
                    yield from proj(a["mlp_up" + l], h3, KT, 4096, (0, 1, 2, 3), evac, mh)
                    yield from down(a["mlp_down" + l], hid, 32, D, ((0, 1), (2, 3)), residual(g1, mg), hm)

                weave(both(), *beside)

            mlp("0", col("norm_mlp_g0", 0, 8), mod0,
                chain(lambda: mod_stream(modk, a["kv_mod_w"], 2048, 0, col("kv_mod_b", 0, 16), 6),
                      lambda: mod_stream(mod1, a["mod_w1"], 6144, 0, col("mod_b1", 0, 48), 6)))

            cv = Carve()
            KK_, VV_, QQ_, GG_ = [cv(4096) for _ in range(4)]
            kT, qT, gT = [v.rearrange("p (k t) -> p k t", k=KT) for v in (KK_, QQ_, GG_)]
            vt = VV_.rearrange("p (t d) -> p t d", t=4)
            LF, FT, FA, FE = [cv(64) for _ in range(4)]
            lf3, ft3 = LF.rearrange("p (t h) -> p t h", t=4), FT.rearrange("p (t h) -> p t h", t=4)
            work = [[cv(512), cv(512), cv(2048), cv(16)] for _ in range(2)]
            nb_ = cv(512)
            start = now()

            def headnorm(dst, b, m, mask, inv_n, eps, gain, bn, o=None):
                m1 = act(dst, BK[b][:, :], ACT.Copy, m, start)
                m2 = act(nb_, dst, ACT.Square, m1, *nbf)
                m3 = mms([(BK[bn][:, :], C(mask), nb_, True, True)], m2, *bfree[bn])
                m4 = ts(DV, nb_, BK[bn][:, :], inv_n, eps, MUL, ADD, m3)
                bfree[bn] = [m4]
                m5 = rroot(nb_, m4)
                nbf[:] = [stt(dst, dst, gain, nb_, MUL, MUL, m5, m1)]
                return m1

            nbf = []
            mh = norm_mod(h3, col("kv_norm_g", 0, 8), modk[:, 8:16], modk[:, 0:8], 7, start)
            qgain = mods[:, 184:185]
            mq = ts(DV, qgain, col("fx_qg"), 0.125, None, MUL, None)
            run(proj(a["kv_w"][:, 0:1024], h3, KT, D, (0, 1, 2),
                     lambda j, b, m: headnorm(kT[:, j, :], b, m, "blk", 1.0 / 64, 1e-6, col("kv_kg"), 3), mh))

            def proj_tok(w, src3, n, banks, evac, *marks):
                for n0 in range(0, n, 512):
                    sl = [load((0, (0, P), (4, 512), w[hf * 512:hf * 512 + 512, n0:n0 + 512].rearrange("(k p) n -> p k n", p=P)))
                          for hf in range(2)]
                    for t in range(4):
                        b = banks[t % len(banks)]
                        m = mms([(BK[b][:, :], src3[:, k, t * 128:t * 128 + 128], sl[k // 4][1][0][:, k % 4, :], k == 0, k == 7)
                                 for k in range(8)], sl[0][2], sl[1][2], *bfree[b], *marks)
                        bfree[b] = [evac(t, n0, b, m)]
                        yield
                    wfree[sl[0][0]] = [m]
                    wfree[sl[1][0]] = [m]

            run(proj_tok(a["kv_w"][:, 1024:2048], h3, D, (0, 1, 2, 3),
                         lambda t, n0, b, m: act(vt[:, t, n0:n0 + 512], BK[b][:, :], ACT.Copy, m, start), mh))

            def small_tok(w, n, b, *marks):
                k, (v,), tk = load((0, (0, P), (8, n), w.rearrange("(k p) n -> p k n", p=P)))
                m = mms([(BK[b][:, t * n:t * n + n], h3[:, kk, t * 128:t * 128 + 128], v[:, kk, :], kk == 0, kk == 7)
                         for t in range(4) for kk in range(8)], tk, *bfree[b], *marks)
                wfree[k] = [m]
                return m

            def bc4(v):
                return v.unsqueeze(1).broadcast_to([P, 4, 16])

            v3 = lambda v: v.rearrange("p (t h) -> p t h", t=4)
            m = small_tok(a["kv_w"][:, 2048:2064], 16, 4, mh)
            m = tt(DV, v3(FA), v3(BK[4][:, 0:64]), bc4(col("kv_fb", 0, 16)), ADD, m, start)
            bfree[4] = [m]
            m1 = act(FE, FA, ACT.Abs, m, start)
            m1 = act(FE, FE, ACT.Exp, m1, scale=-1.0)
            m1 = act(FE, FE, ACT.Ln, m1, bias=1.0)
            m = ts(DV, FA, FA, 0.0, None, ALU.min, None, m1)
            mlf = tt(DV, LF, FA, FE, SUB, m, m1)
            m = mms([(BK[5][:, 16 * t:16 * t + 16], C("incl") if j == t else C("ones"), lf3[:, j, :], j == 0, j == t)
                     for t in range(4) for j in range(t + 1)], mlf, *bfree[5])
            mft = act(FT, BK[5][:, 0:64], ACT.Copy, m)
            bfree[5] = [mft]

            mh = norm_mod(h3, col("norm_mix_g1", 0, 8), mod1[:, 8:16], mod1[:, 0:8], 7, now())
            run(proj(a["fx_wqg"][:, 0:1024], h3, KT, D, (0, 1, 2),
                     lambda j, b, m: headnorm(qT[:, j, :], b, m, "blk", 1.0 / 64, 1e-6, qgain, 3), mh, mq))
            run(proj(a["fx_wqg"][:, 1024:2048], h3, KT, D, (0, 1, 2),
                     lambda j, b, m: act(gT[:, j, :], BK[b][:, :], ACT.Sigmoid, m), mh))
            cuml = con[:, CON["incl"] * 128:CON["incl"] * 128 + 512]

            def attention(banks, bufs, qk, causal, vcols, width, rows, evac, mr, scale=1.0, forget=None):
                bs, bt, bo = banks
                Fb, S, PT, sm_ = bufs
                p3 = PT.rearrange("p (k t) -> p k t", k=4)
                mo = None
                mF = None
                if forget is not None:
                    m = mms([(BK[bo][:, 128 * j:512], lf3[:, j, forget:forget + 1].broadcast_to([P, 128]), cuml[:, 0:512 - 128 * j],
                              j == 0, j == 3) for j in range(4)], mlf, *bfree[bo], mr)
                    mF = act(Fb, BK[bo][:, :], ACT.Copy, m, mr)
                    bfree[bo] = [mF]
                    yield
                for qt in range(4):
                    n = (qt + 1) * 128 if causal else 512
                    m = mms([(BK[bs][:, 0:n], q_(qt), k_(n), i == 0, i == len(qk) - 1) for i, (q_, k_) in enumerate(qk)],
                            *bfree[bs], mr)
                    if forget is not None:
                        m = DV(lambda e, qt=qt, n=n: e.scalar_tensor_tensor(
                            out=S[:, 0:n], in0=Fb[:, 0:n], scalar=ft3[:, qt, forget:forget + 1], in1=BK[bs][:, 0:n],
                            op0=SUB, op1=SUB, reverse1=True), m, mF, mft, mo)
                        bfree[bs] = [m]
                        m = tt(DV, S[:, n - 128:n], S[:, n - 128:n], C("neg"), ADD, m)
                        src = S
                    else:
                        src = BK[bs]
                    mx = DV(lambda e, n=n, src=src: e.tensor_reduce(sm_[:, 0:1], src[:, 0:n], AX, ALU.max), m, mo)
                    mx = ts(DV, sm_[:, 1:2], sm_[:, 0:1], -scale, None, MUL, None, mx)
                    yield
                    m = act(S[:, 0:n], src[:, 0:n], ACT.Exp, mx, mo, scale=scale, bias=sm_[:, 1:2], accum=sm_[:, 2:3])
                    if forget is None:
                        bfree[bs] = [m]
                    mr_ = DV(lambda e: e.reciprocal(sm_[:, 3:4], sm_[:, 2:3]), m)
                    m = ts(DV, S[:, 0:n], S[:, 0:n], sm_[:, 3:4], None, MUL, None, mr_)
                    yield
                    nk = n // 128
                    mo = trs([(BK[bt][:, k * 128:k * 128 + 128], S[:, k * 128:k * 128 + 128]) for k in range(nk)],
                             m, *bfree[bt])
                    m = act(p3[:, 0:nk, qt * 128:qt * 128 + 128], BK[bt][:, 0:n].rearrange("p (k t) -> p k t", k=nk),
                            ACT.Copy, mo, mr)
                    bfree[bt] = [m]
                    yield
                m = mms([(BK[bo][rows, (k * 128 if causal else 0):512], vcols(k), p3[:, k, (k * 128 if causal else 0):512],
                          k == 0, k == 3) for k in range(4)], m, *bfree[bo])
                m = evac(m)
                bfree[bo] = [m]
                yield

            def fox(par):
                for ct in range(8):
                    hd = 2 * ct + par
                    hp = slice(64 * par, 64 * par + 64)
                    bo = 4 * par + 2
                    yield from attention(
                        (4 * par, 4 * par + 1, bo), work[par],
                        [(lambda qt: qT[hp, ct, qt * 128:qt * 128 + 128], lambda n: kT[hp, ct, 0:n])], True,
                        lambda k: vt[:, k, hd * 64:hd * 64 + 64], 64, hp,
                        lambda m: tt(DV, gT[hp, ct, :], BK[bo][hp, :], gT[hp, ct, :], MUL, m), now(), forget=hd)

            weave(fox(0), fox(1))
            mg1 = ts(DV, g1, mod1[:, 16:24], 1.0, None, ADD, None)
            run(proj(a["fx_wo"], gT, KT, D, (0, 1), residual(g1, mg1), now()))
            mlp("1", col("norm_mlp_g1", 0, 8), mod1, mod_stream(mod2, a["w_mod_2"], 6144, 8, col("b_mod_2", 0, 48), 6))
            norm_mod(x3, col("final_g", 0, 8), None, None, 7, now())
            cv = Carve()
            OD = cv(4096)
            od3 = OD.rearrange("p (k t) -> p k t", k=KT)
            BE, GG2, GCs, EG, NEG, EGL, EKS, BEK, NBE, TA, TB = [cv(64) for _ in range(11)]
            win = a["w_in_2"]
            start = now()
            mh = norm_mod(h3, col("g_mix_2", 0, 8), mod2[:, 8:16], mod2[:, 0:8], 7, start)
            m = small_tok(win[:, 4096:4128], 32, 4, mh)
            ba = BK[4][:, 0:128].rearrange("p (t h) -> p t h", t=4)
            m1 = act(v3(BE), ba[:, :, 0:16], ACT.Sigmoid, m, start)
            m2 = tt(DV, v3(TA), ba[:, :, 16:32], bc4(col("dt_bias_2", 0, 16)), ADD, m1, start)
            bfree[4] = [m2]
            m = act(TB, TA, ACT.Abs, m2, start)
            m = act(TB, TB, ACT.Exp, m, scale=-1.0)
            m = act(TB, TB, ACT.Ln, m, bias=1.0)
            m = stt(TA, TA, 0.0, TB, ALU.max, ADD, m)
            ea = mods[:, 185:201]
            me = act(ea, col("a_log_2", 0, 16), ACT.Exp, start)
            m = tt(DV, v3(TA), v3(TA), bc4(ea), MUL, me, m)
            mg = ts(DV, GG2, TA, -1.0, None, MUL, None, m)
            g3 = v3(GG2)
            bk5 = BK[5][:, :].rearrange("p (s t h) -> p s t h", s=8, t=4)
            m = mms([(BK[5][:, 0:32], C("incl"), g3[:, :, 0:8], True, True),
                     (BK[5][:, 32:64], C("inclR"), g3[:, :, 8:16], True, True),
                     (BK[5][:, 64:128], C("ones"), GG2, True, True)], mg, *bfree[5])
            gc3 = v3(GCs)
            m1 = act(gc3[:, :, 0:8], BK[5][:, 0:32].rearrange("p (t h) -> p t h", t=4), ACT.Copy, m, start)
            m1 = act(gc3[:, :, 8:16], BK[5][:, 32:64].rearrange("p (t h) -> p t h", t=4), ACT.Copy, m)
            m2 = act(EGL, BK[5][:, 64:128], ACT.Exp, m)
            m3 = tt(DV, EKS, BK[5][:, 64:128], GCs, SUB, m1, m2)
            bfree[5] = [m3]
            m3 = act(EKS, EKS, ACT.Exp, m3)
            m1 = act(EG, GCs, ACT.Exp)
            m = ts(DV, NEG, EG, -1.0, None, MUL, None, m1)
            m = tt(DV, BEK, BE, EKS, MUL, m3)
            mcol = [ts(DV, NBE, BE, -1.0, None, MUL, None), m3, m2]

            dsets = [[cv(512) for _ in range(9)] for _ in range(2)]
            dwork = [[cv(512) for _ in range(8)] + [cv(128) for _ in range(4)] for _ in range(2)]
            PB, t0, t1 = cv(516), cv(512), cv(512)
            start = now()
            mz = GP(lambda e: e.memset(PB[:, 0:2], 0.0), start)
            mz = GP(lambda e: e.memset(PB[:, 514:516], 0.0), start)
            dprep, dused, ddone, dheaded = {}, {}, {}, {}
            dsm = cv(16)

            def dn_prep(hd, since):
                qT_, kT_, Z_, Kt_, Vt_, KF, KB, QF, QB = dsets[hd % 2]
                cw = col("conv_w_2", 0, 120).rearrange("p (c j) -> p c j", c=24)
                src = [win[:, b0 + hd * 128:b0 + hd * 128 + 128].rearrange("(k p) n -> p k n", p=P) for b0 in (0, 1024, 2048, 3072)]
                sl = [load((0, (0, P), (8, 128), src[2 * i]), (1024, (0, P), (8, 128), src[2 * i + 1])) for i in range(2)]
                mlast = None
                toks = []
                for i in range(4):
                    k, vs, tk = sl[i // 2]
                    b = i % 2
                    m = mms([(BK[b][:, :], vs[i % 2][:, kk, :], h3[:, kk, :], kk == 0, kk == 7) for kk in range(8)],
                            tk, *bfree[b], mh)
                    if i % 2:
                        wfree[k] = [m]
                    if i == 3:
                        mzz = act(Z_, BK[b][:, :], ACT.Silu, m, since)
                        bfree[b] = [mzz]
                        yield
                        break
                    m = act(PB[:, 2:514], BK[b][:, :], ACT.Copy, m, mlast, since)
                    bfree[b] = [m]
                    yield
                    ct = 8 * i + hd
                    m = ts(DV, t0, PB[:, 0:512], cw[:, ct, 0:1], None, MUL, None, m, mz, since)
                    for j in range(1, 5):
                        m = stt(t0, PB[:, j:j + 512], cw[:, ct, j:j + 1], t0, MUL, ADD, m)
                    mlast = m
                    yield
                    dst = (qT_, kT_, t1)[i]
                    m = act(dst, t0, ACT.Silu, m, since)
                    if i < 2:
                        m2 = act(t0, dst, ACT.Square, m)
                        m2 = mms([(BK[1 - b][:, :], C("ones"), t0, True, True)], m2, *bfree[1 - b])
                        m2 = ts(DV, t0, BK[1 - b][:, :], 1e-6, None, ADD, None, m2)
                        bfree[1 - b] = [m2]
                        m2 = rroot(t0, m2)
                        mlast = m = stt(dst, dst, (128 ** -0.5, 1.0)[i], t0, MUL, MUL, m, m2)
                    mlast = [mlast, m]
                    yield
                    if i:
                        m = trs([(BK[b][:, c * 128:c * 128 + 128], dst[:, c * 128:c * 128 + 128]) for c in range(4)],
                                m, *bfree[b])
                        m = act((None, Kt_, Vt_)[i], BK[b][:, :], ACT.Copy, m, since)
                        bfree[b] = [m]
                        toks.append(m)
                        mlast = [mlast, m]
                        yield
                q3 = lambda v: v.rearrange("p (c t) -> p c t", c=4)
                for lhs, rhs, df, db, mf, mb, b in ((kT_, kT_, KF, KB, "strict", "strictR", 0), (kT_, qT_, QF, QB, "incl", "inclR", 1)):
                    m = mms([(BK[b][:, c * 128:c * 128 + 128], lhs[:, c * 128:c * 128 + 128], rhs[:, c * 128:c * 128 + 128], True, True)
                             for c in range(4)], mlast, *bfree[b])
                    for d, mk in ((df, mf), (db, mb)):
                        m1 = tt(DV, q3(d), q3(BK[b][:, :]), C(mk).unsqueeze(1).broadcast_to([P, 4, 128]), MUL, m, since)
                    bfree[b] = [m1]
                    toks.append(m1)
                    yield
                dprep[hd] = [toks, mzz, mlast]
                dused[hd] = now()

            def dn_dir(hd, R):
                qT_, kT_, Z_, Kt_, Vt_, KF, KB, QF, QB = dsets[hd % 2]
                E_, NT, TT, TM, US, MT, RK, OO, SS, XS, VN, VS = dwork[R]
                KM, QM = (KB, QB) if R else (KF, QF)
                ba_, bb_, bc_ = (5, 6, 7) if R else (2, 3, 4)
                dh = 8 * R + hd
                c_ = lambda v, c: v3(v)[:, c, dh:dh + 1]
                q3 = lambda v: v.rearrange("p (c t) -> p c t", c=4)
                pm = [dprep[hd], mcol]
                before = [dheaded[hd - 1]] if hd else [start]
                m = mms([(BK[ba_][:, c * 128:c * 128 + 128], g3[:, c, dh:dh + 1].broadcast_to([P, 128]), C("inclR" if R else "incl"), True, True)
                         for c in range(4)], pm, *bfree[ba_])
                for c in range(4):
                    m1 = ts(DV, q3(E_)[:, c, :], BK[ba_][:, c * 128:c * 128 + 128], c_(GCs, c), 0.0, SUB, ALU.min, m, before)
                bfree[ba_] = [m1]
                m = act(E_, E_, ACT.Exp, m1)
                yield
                for c in range(4):
                    mn = stt(q3(NT)[:, c, :], q3(E_)[:, c, :], c_(NBE, c), q3(KM)[:, c, :], MUL, MUL, m, before)
                mrk = tt(GP, RK, QM, E_, MUL, m, before, mn)
                yield
                yield from invert(NT, TT, TM, US, MT, R, (ba_, bb_, bc_), 4, [before], mn)
                mt = inverse[-1]
                ms = GP(lambda e: e.memset(SS, 0.0), before)
                mvs = None
                for c in (range(3, -1, -1) if R else range(4)):
                    q = slice(c * 128, c * 128 + 128)
                    m = mms([(BK[ba_][:, 0:128], kT_[:, q], SS, True, True), (BK[ba_][:, 128:256], qT_[:, q], SS, True, True)],
                            ms, *bfree[ba_])
                    m1 = stt(XS, BK[ba_][:, 0:128], c_(NEG, c), Vt_[:, q], MUL, ADD, m, mvs)
                    mq = ts(DV, OO[:, q], BK[ba_][:, 128:256], c_(EG, c), None, MUL, None, m, before, ddone.get(hd - 1))
                    bfree[ba_] = [mq]
                    yield
                    m = mms([(BK[bb_][:, 0:128], TT[:, q], XS, True, True)], m1, mt, *bfree[bb_])
                    m2 = act(VN, BK[bb_][:, 0:128], ACT.Copy, m, mvs, scale=c_(BE, c))
                    m3 = act(VS, BK[bb_][:, 0:128], ACT.Copy, m, mvs, scale=c_(BEK, c))
                    bfree[bb_] = [m3]
                    yield
                    m = mms([(BK[bc_][:, 0:128], Kt_[:, q], VS, True, True)], m3, *bfree[bc_])
                    mvs = mms([(BK[bc_][:, 128:256], RK[:, q], VN, True, True)], m2, mrk)
                    ms = stt(SS, SS, c_(EGL, c), BK[bc_][:, 0:128], MUL, ADD, mvs)
                    mo = tt(DV, OO[:, q], OO[:, q], BK[bc_][:, 128:256], ADD, mvs, mq)
                    bfree[bc_] = [mo]
                    yield
                dout.append(mo)

            dout = []

            def dn_head(hd):
                qT_, kT_, Z_, Kt_, Vt_, KF, KB, QF, QB = dsets[hd % 2]
                fs = [dn_dir(hd, False), dn_dir(hd, True)]
                while fs:
                    for f in list(fs):
                        if next(f, StopIteration) is StopIteration:
                            fs.remove(f)
                    yield
                dheaded[hd] = now()

            def dn_post(hd):
                qT_, kT_, Z_, Kt_, Vt_, KF, KB, QF, QB = dsets[hd % 2]
                OO, OB = dwork[0][7], dwork[1][7]
                sq, sm_ = KF, dsm
                m = tt(GP, OO, OO, OB, ADD, dheaded[hd])
                for c in range(4):
                    m1 = act(sq[:, 0:128], OO[:, c * 128:c * 128 + 128], ACT.Square, m, accum=sm_[:, c:c + 1])
                m1 = ts(DV, sm_[:, 0:4], sm_[:, 0:4], 1.0 / 128, 1e-6, MUL, ADD, m1)
                m1 = rroot(sm_[:, 0:4], m1)
                for c in range(4):
                    m = ts(DV, OO[:, c * 128:c * 128 + 128], OO[:, c * 128:c * 128 + 128], sm_[:, c:c + 1], None, MUL, None, m1)
                yield
                m = trs([(BK[0][:, c * 128:c * 128 + 128], OO[:, c * 128:c * 128 + 128]) for c in range(4)], m, *bfree[0])
                m = stt(od3[:, hd, :], BK[0][:, :], col("dn_o_gain_2"), Z_, MUL, MUL, m)
                bfree[0] = [m]
                ddone[hd] = now()
                yield

            run(dn_prep(0, start))
            for hd in range(8):
                beside = [lambda hd=hd: dn_post(hd - 1)] if hd else []
                if hd < 7:
                    beside.append(lambda hd=hd: dn_prep(hd + 1, [dused[hd]] + ([dheaded[hd - 1], ddone[hd - 1]] if hd else [])))
                weave(dn_head(hd), chain(*beside))
            run(dn_post(7))
            cv = Carve()
            OD, ME, GA = cv(4096), cv(4096), cv(4096)
            me3, ga3 = [v.rearrange("p (k t) -> p k t", k=KT) for v in (ME, GA)]
            start = now()
            gm = []

            def gate(j, b, m):
                m = act(ga3[:, j, :], BK[b][:, :], ACT.Sigmoid, m, start)
                gm[:] = [m]
                return m

            run(proj(win[:, 4960:5984], h3, KT, D, (0, 1), gate, mh))
            run(proj(a["w_o_dn_2"], od3, KT, D, (2, 3),
                     lambda j, b, m: tt(DV, me3[:, j, :], BK[b][:, :], ga3[:, j, :], MUL, m, gm, start), start))

            OM = OD
            om3 = OM.rearrange("p (k t) -> p k t", k=KT)
            start = now()
            CQ, CK, KR, CO, SI, R0, R1 = cv(2048), cv(1024), cv(512), cv(512), cv(512), cv(512), cv(512)
            cq3, ck3 = CQ.rearrange("p (k t) -> p k t", k=4), CK.rearrange("p (k t) -> p k t", k=2)
            lw_ = []
            for _ in range(2):
                lw_.append([cv(512) for _ in range(4)] + [None, cv(512), cv(2048), cv(16)])
            s_pos = new_sem("s_pos")
            pi = R0[0:64, :].bitcast(I32)
            mp = SY.dma(s_pos, 16, lambda e: e.dma_start(pi, a["pos"].broadcast_to([64, 512])), start)
            ang, n_ = R1[0:64, :], SI[0:64, :]
            m = DV(lambda e: e.tensor_copy(ang, pi), mp, start)
            m = ts(DV, ang, ang, C("iota")[0:64, 64:65], None, MUL, None)
            MAGIC = 12582912.0
            m = ts(DV, n_, ang, float(1 / (2 * np.pi)), MAGIC, MUL, ADD)
            m = ts(DV, n_, n_, -MAGIC, None, ADD, None)
            c1 = 6.28125
            c2 = float(np.float32(int((2 * np.pi - c1) * 2 ** 20) / 2 ** 20))
            c3 = float(np.float32(2 * np.pi - c1 - c2))
            for c in (c1, c2, c3):
                m = stt(ang, n_, -c, ang, MUL, ADD)
            m = ts(DV, ang, ang, 3.1415925, -3.1415925, ALU.min, ALU.max)
            ms = act(SI[0:64, :], ang, ACT.Sin, m)
            mc = act(CO[0:64, :], ang, ACT.Sin, m, scale=0.5)
            m = tt(DV, CO[0:64, :], CO[0:64, :], CO[0:64, :], MUL, mc)
            mcs = [ts(DV, CO[0:64, :], CO[0:64, :], -2.0, 1.0, MUL, ADD), ms]

            run(proj(win[:, 4128:4640], h3, KT, 512, (0, 1), lambda j, b, m: act(cq3[:, j, :], BK[b][:, :], ACT.Copy, m, start), mh))
            run(proj(win[:, 4640:4896], h3, KT, 256, (0, 1), lambda j, b, m: act(ck3[:, j, :], BK[b][:, :], ACT.Copy, m, start), mh))

            def rope(dst, b, m, tmp, b2, *marks):
                m1 = act(tmp[0:64, :], BK[b][0:64, :], ACT.Copy, m, *marks)
                bfree[b] = [m1]
                m2 = mms([(BK[b2][0:64, :], C("perm")[0:64, 0:64], tmp[0:64, :], True, True)], m1, *bfree[b2])
                m3 = tt(DV, dst, BK[b2][0:64, :], SI[0:64, :], MUL, m2, mcs, *marks)
                bfree[b2] = [m3]
                m4 = tt(DV, tmp[0:64, :], tmp[0:64, :], CO[0:64, :], MUL, m2, m3)
                return tt(DV, dst, dst, tmp[0:64, :], ADD, m4)

            k, (v,), tk = load((0, (0, P), (8, 64), win[:, 4896:4960].rearrange("(k p) n -> p k n", p=P)))
            m = mms([(BK[2][0:64, :], v[:, kk, :], h3[:, kk, :], kk == 0, kk == 7) for kk in range(8)], tk, mh, *bfree[2])
            wfree[k] = [m]
            mkr = rope(KR[0:64, :], 2, m, R0, 3, mp, start, now())
            for src, nk, g, inv in ((cq3, 4, "q_gain_2", 1.0 / 512), (ck3, 2, "kv_gain_2", 1.0 / 256)):
                m = rms_rstd(src, nk, inv, 1e-6, 4, now(), o=R0)
                for j in range(nk):
                    m = stt(src[:, j, :], src[:, j, :], col(g, j), R0, MUL, MUL, m)
            mlat = m
            start = now()

            def mla(par):
                Qn, Qr, Kn, Vh, _, S, PT, sm_ = lw_[par]
                b0 = 4 * par
                for hh in range(4):
                    hd = 2 * hh + par
                    since = now()
                    k, (wq, wkv), tk = load(
                        (0, (0, P), (4, 192), a["w_uq_2"][:, hd * 192:hd * 192 + 192].rearrange("(k p) n -> p k n", p=P)),
                        (768, (0, P), (2, 256), a["w_ukv_2"][:, hd * 256:hd * 256 + 256].rearrange("(k p) n -> p k n", p=P)))
                    m = mms([(BK[b0][0:64, :], wq[:, kk, 128:192], cq3[:, kk, :], kk == 0, kk == 3) for kk in range(4)],
                            tk, mlat, *bfree[b0], start)
                    mr = rope(Qr[0:64, :], b0, m, S, b0 + 1, since)
                    yield
                    m = mms([(BK[b0 + 2][:, :], wq[:, kk, 0:128], cq3[:, kk, :], kk == 0, kk == 3) for kk in range(4)],
                            *bfree[b0 + 2])
                    m1 = act(Qn, BK[b0 + 2][:, :], ACT.Copy, m, since)
                    bfree[b0 + 2] = [m1]
                    yield
                    m = mms([(BK[b0 + 3][:, :], wkv[:, kk, 0:128], ck3[:, kk, :], kk == 0, kk == 1) for kk in range(2)],
                            *bfree[b0 + 3])
                    m2 = act(Kn, BK[b0 + 3][:, :], ACT.Copy, m, since)
                    bfree[b0 + 3] = [m2]
                    yield
                    m = mms([(BK[b0][:, t * 128:t * 128 + 128], ck3[:, kk, t * 128:t * 128 + 128], wkv[:, kk, 128:256], kk == 0, kk == 1)
                             for t in range(4) for kk in range(2)], *bfree[b0])
                    wfree[k] = [m]
                    m3 = act(Vh, BK[b0][:, :], ACT.Copy, m, since)
                    bfree[b0] = [m3]
                    yield
                    yield from attention(
                        (b0, b0 + 1, b0 + 2), (None, S, PT, sm_),
                        [(lambda qt: Qn[:, qt * 128:qt * 128 + 128], lambda n: Kn[:, 0:n]),
                         (lambda qt: Qr[0:64, qt * 128:qt * 128 + 128], lambda n: KR[0:64, 0:n])], False,
                        lambda kt: Vh[:, kt * 128:kt * 128 + 128], 128, slice(0, P),
                        lambda m: act(om3[:, hd, :], BK[b0 + 2][:, :], ACT.Copy, m), [mr, m1, m2, m3, mkr, since],
                        scale=192 ** -0.5)

            weave(mla(0), mla(1))
            start = now()
            run(proj(win[:, 5984:7008], h3, KT, D, (0, 1), gate, mh))
            TG = lw_[0][6]
            tgf = [[], []]

            def merge(j, b, m):
                t_ = TG[:, 512 * (j % 2):512 * (j % 2) + 512]
                m1 = tt(DV, t_, BK[b][:, :], ga3[:, j, :], MUL, m, gm, start, *tgf[j % 2])
                tgf[j % 2] = [tt(GP, me3[:, j, :], me3[:, j, :], t_, ADD, m1)]
                return m1

            run(proj(a["w_o_mla_2"], om3, KT, D, (2, 3), merge, start))
            run(proj(a["w_out_2"], me3, KT, D, (0, 1), residual(mod2[:, 16:24]), now()))
            cv = Carve()
            HT, SEL, XE, YE = cv(4096), cv(4096), cv(8192), cv(8192)
            RKs, AFT = cv(512), cv(512)
            AF, RT, s4, s8 = cv(64), cv(64), cv(16), cv(16)
            ht3 = HT.rearrange("p (t d) -> p t d", t=4)
            sel3 = SEL.rearrange("p (t s) -> p t s", t=4)
            xe3 = XE.rearrange("p (k s) -> p k s", k=KT)
            ye3 = YE.rearrange("p (e d) -> p e d", e=8)
            start = now()
            mh = norm_mod(h3, col("g_ffn_2", 0, 8), mod2[:, 32:40], mod2[:, 24:32], 7, start)
            WKb, SMb, PAIR = YE[0:16, 0:512], YE[0:16, 512:1024], YE[0:16, 1024:2048]
            s_pair = new_sem("s_pair")
            mpair = SY.dma(s_pair, 16, lambda e: e.dma_start(PAIR, a["pair"]), start)
            m = small_tok(a["w_router_2"], 16, 0, mh)
            lg, af3 = v3(BK[0][:, 0:64]), v3(AF)
            b16 = lambda v: v.unsqueeze(2).broadcast_to([P, 4, 16])
            m = DV(lambda e: e.tensor_reduce(s4[:, 0:4], lg, AX, ALU.max), m, start)
            m = tt(DV, af3, lg, b16(s4[:, 0:4]), SUB)
            bfree[0] = [m]
            m = act(AF, AF, ACT.Exp, m)
            m = DV(lambda e: e.tensor_reduce(s4[:, 4:8], af3, AX, ADD), m)
            m = DV(lambda e: e.reciprocal(s4[:, 4:8], s4[:, 4:8]))
            m = tt(DV, af3, af3, b16(s4[:, 4:8]), MUL)
            m = trs([(BK[1][0:16, t * 128:t * 128 + 128], af3[:, t, :]) for t in range(4)], m, *bfree[1])
            ma = act(AFT[0:16, :], BK[1][0:16, :], ACT.Copy, m, start)
            bfree[1] = [ma]
            m = act(WKb, AFT[0:16, :], ACT.Copy)
            DV.wait(m)
            for _ in range(8):
                DV(lambda e: e.max(s8[0:16, 0:8], WKb))
                m = DV(lambda e: e.match_replace(WKb, s8[0:16, 0:8], WKb, -1.0))
            ts(DV, SMb, WKb, 0.0, None, ALU.is_lt, None)
            DV(lambda e: e.tensor_tensor_scan(WKb, SMb, SMb, 0.0, ADD, ALU.max))
            tt(DV, WKb, WKb, SMb, MUL)
            mr = ts(DV, RKs[0:16, :], WKb, -1.0, None, ADD, None)
            m = trs([(BK[2][:, 16 * t:16 * t + 16], RKs[0:16, t * 128:t * 128 + 128]) for t in range(4)], mr, *bfree[2])
            m = act(RT, BK[2][:, 0:64], ACT.Copy, m, start)
            bfree[2] = [m]
            for t in range(4):
                ms = DV(lambda e, t=t: e.tensor_tensor(
                    sel3[:, t, :].rearrange("p (e s) -> p e s", e=16),
                    v3(RT)[:, t, :].unsqueeze(2).broadcast_to([P, 16, 64]),
                    C("iota", 64).unsqueeze(1).broadcast_to([P, 16, 64]), ALU.is_equal), m, start)
            for k in range(KT):
                for hf in range(2):
                    pass
                b = 3 + k % 2
                m = trs([(BK[b][:, t * 128:t * 128 + 128], h3[:, k, t * 128:t * 128 + 128]) for t in range(4)], mh, *bfree[b])
                mt = act(ht3[:, :, k * 128:k * 128 + 128], BK[b][:, :].rearrange("p (t d) -> p t d", t=4), ACT.Copy, m, start)
                bfree[b] = [mt]
            mx = []
            for k in range(KT):
                for hf in range(2):
                    b = (2 * k + hf) % 4
                    m = mms([(BK[b][:, :], ht3[:, t, k * 128:k * 128 + 128], sel3[:, t, hf * 512:hf * 512 + 512], t == 0, t == 3)
                             for t in range(4)], ms, mt, *bfree[b])
                    m = act(xe3[:, k, hf * 512:hf * 512 + 512], BK[b][:, :], ACT.Copy, m, start)
                    bfree[b] = [m]
                    mx.append(m)
            dist = SEL.rearrange("p (e t) -> p e t", e=8)
            AB = HT[:, 0:1024]
            mdist = []
            gathered = now()
            for pr in range(8):
                m = mms([(BK[4][:, :], PAIR[:, pr * 128:pr * 128 + 128], RKs[0:16, :], True, True)], mr, mpair, *bfree[4])
                m1 = mms([(BK[5][:, :], PAIR[:, pr * 128:pr * 128 + 128], AFT[0:16, :], True, True)], ma, *bfree[5])
                ab = AB[:, 512 * (pr % 2):512 * (pr % 2) + 512]
                m1 = act(ab, BK[5][:, :], ACT.Copy, m1, gathered, mdist[-2:])
                bfree[5] = [m1]
                m = stt(dist[:, pr, :], BK[4][:, :], C("iota")[:, 65:66], ab, ALU.is_equal, MUL, m, m1, gathered)
                bfree[4] = [m]
                mdist.append(m)
            ready_e = now()
            SG, HI, HIT = HT[:, 0:1024], HT[:, 1024:2048], HT[:, 2048:4096]
            st = {}

            def ffn(name, pr, banks, lhs, *marks):
                for g in range(4):
                    sl = [load((0, (0, P), (2, 1024), a[name][2 * pr + e, g * 256:g * 256 + 256, :].rearrange("(k p) n -> p k n", p=P)))
                          for e in range(2)]
                    m = mms([(BK[banks[hf]][64 * e:64 * e + 64, :], lhs(2 * g + j, e), sl[e][1][0][:, j, hf * 512:hf * 512 + 512],
                              g == 0 and j == 0, g == 3 and j == 1) for j in range(2) for hf in range(2) for e in range(2)],
                            sl[0][2], sl[1][2], *bfree[banks[0]], *bfree[banks[1]], *marks)
                    wfree[sl[0][0]] = [m]
                    wfree[sl[1][0]] = [m]
                return m

            def gate_of(pr):
                m = ffn("w_gate_2", pr, (0, 1), lambda k, e: xe3[:, k, (2 * pr + e) * 64:(2 * pr + e) * 64 + 64], mx)
                for hf in range(2):
                    m1 = act(SG[:, hf * 512:hf * 512 + 512], BK[hf][:, :], ACT.Silu, m, ready_e, st.get("hi"))
                    bfree[hf] = [m1]
                st["sg"] = m1

            def up_of(pr):
                m = ffn("w_up_2", pr, (2, 3), lambda k, e: xe3[:, k, (2 * pr + e) * 64:(2 * pr + e) * 64 + 64], mx)
                for hf in range(2):
                    m1 = tt(DV, HI[:, hf * 512:hf * 512 + 512], BK[2 + hf][:, :], SG[:, hf * 512:hf * 512 + 512], MUL,
                            m, st["sg"], ready_e, st.get("tr"))
                    bfree[2 + hf] = [m1]
                st["hi"] = m1

            def down_of(pr):
                hit = HIT[:, 0:1024].rearrange("p (f s) -> p f s", f=8)
                mm_ = []
                for hf in range(2):
                    b = 6 + hf
                    m = trs([(BK[b][:, f * 128:f * 128 + 128], HI[:, hf * 512 + f * 128:hf * 512 + f * 128 + 128]) for f in range(4)],
                            st["hi"], *bfree[b])
                    m1 = act(hit[:, 4 * hf:4 * hf + 4, :], BK[b][:, :].rearrange("p (f s) -> p f s", f=4), ACT.Copy, m, st.get("dn"))
                    bfree[b] = [m1]
                    mm_.append(m1)
                st["tr"] = m
                m = ffn("w_down_2", pr, (4, 5), lambda f, e: hit[:, f, 64 * e:64 * e + 64], mm_)
                st["dn"] = m
                for hf in range(2):
                    m1 = act(ye3[:, pr, hf * 512:hf * 512 + 512], BK[4 + hf][:, :], ACT.Copy, m)
                    bfree[4 + hf] = [m1]
                st["ye"] = m1

            gate_of(0)
            up_of(0)
            for pr in range(8):
                if pr < 7:
                    gate_of(pr + 1)
                down_of(pr)
                if pr < 7:
                    up_of(pr + 1)
            evac = residual(mod2[:, 40:48])
            for k in range(KT):
                b = k % 4
                m = mms([(BK[b][:, :], ye3[:, pr, k * 128:k * 128 + 128], dist[:, pr, :], pr == 0, pr == 7) for pr in range(8)],
                        st["ye"], mdist, *bfree[b])
                bfree[b] = [evac(k, b, m)]
            mf = norm_mod(x3, col("g_final_2", 0, 8), None, None, 7, now())
            ot = A[:, 0:4096].rearrange("p (t d) -> p t d", t=4)
            mo = now()
            for k in range(KT):
                b = k % 4
                m = trs([(BK[b][:, t * 128:t * 128 + 128], x3[:, k, t * 128:t * 128 + 128]) for t in range(4)], mf[k], *bfree[b])
                m = act(ot[:, :, k * 128:k * 128 + 128], BK[b][:, :].rearrange("p (t d) -> p t d", t=4), ACT.Copy, m, mo)
                bfree[b] = [m]
            s_out = new_sem("s_out")
            m = SY.dma(s_out, 16, lambda e: e.dma_start(out.rearrange("(t p) d -> p t d", p=P), ot), m)
            SY.wait(m)

        body()
        block = ctx.enter_context(nc.Block())

        @block.sync
        def _(eng):
            SY.play(eng)

        @block.scalar
        def _(eng):
            AC.play(eng)

        @block.vector
        def _(eng):
            DV.play(eng)

        @block.gpsimd
        def _(eng):
            GP.play(eng)

        @block.tensor
        def _(eng):
            PE.play(eng)


_WHOLE = ["kv_mod_w", "kv_w"]
_FIRST = ["rw_wr", "rw_wk", "rw_wv", "rw_wo", "rw_w1", "rw_w2", "rw_a1", "rw_a2", "rw_g1", "rw_g2", "fx_wqg", "fx_wo",
          "w_mod_2", "w_in_2", "w_uq_2", "w_ukv_2", "w_o_dn_2", "w_o_mla_2", "w_out_2", "w_router_2",
          "w_gate_2", "w_up_2", "w_down_2"]
_LAYERS = ["mod_w", "mlp_up", "mlp_down"]


def _columns(inputs):
    g = {k: np.asarray(v) for k, v in inputs.items()}

    def by128(v):
        return v.reshape(-1, 128).T

    def tiled(v, n):
        return np.tile(v.reshape(-1), n).reshape(-1, 128).T

    def rows(v):
        return np.tile(v.reshape(1, -1), (128, 1))

    out = []
    for name, w in VECS:
        if name in ("mod_b0", "mod_b1", "norm_mix_g0", "norm_mix_g1", "norm_mlp_g0", "norm_mlp_g1"):
            v = by128(g[name[:-1]][int(name[-1])])
        elif name == "conv_w_2":
            v = g[name][0].reshape(5, 24, 128).transpose(2, 1, 0).reshape(128, 120)
        elif name in ("kv_kg", "fx_qg"):
            v = tiled(g[name], 2)
        elif name in ("kv_fb", "a_log_2", "dt_bias_2"):
            v = rows(g[name])
        else:
            v = by128(g[name])
        assert v.shape == (128, w), (name, v.shape)
        out.append(v)
    return np.ascontiguousarray(np.concatenate(out, axis=1))


def arrays_of(inputs):
    g = {k: np.asarray(v) for k, v in inputs.items()}
    arr = {"x": g["x"][0], "pos": g["positions_2"], "const": _CARR, "pair": _PAIR, "cols": _columns(inputs)}
    for n in _WHOLE:
        arr[n] = g[n]
    for n in _FIRST:
        arr[n] = g[n][0]
    for n in _LAYERS:
        arr[n + "0"], arr[n + "1"] = g[n][0], g[n][1]
    return {f"in_{n}": np.ascontiguousarray(v) for n, v in arr.items()}


def kernel(**inputs):
    import concourse.bacc as _bacc
    from concourse.bass_utils import run_bass_kernel_spmd as _run

    nc = _bacc.Bacc("TRN2", target_bir_lowering=False, num_devices=1)
    arrays = arrays_of(inputs)
    a = {n[3:]: nc.dram_tensor(n, v.shape, mybir.dt.from_np(v.dtype), kind="ExternalInput").ap()
         for n, v in arrays.items()}
    out = nc.dram_tensor("out_0", (T, D), F32, kind="ExternalOutput").ap()
    program(nc, a, out)
    r = _run(nc, [arrays], core_ids=[0])
    return r.results[0]["out_0"].reshape(1, T, D)
```

```python
import numpy as np
from contextlib import ExitStack
import concourse.bass as bass
from concourse import mybir

F32 = mybir.dt.float32
I32 = mybir.dt.int32
ALU = mybir.AluOpType
ACT = mybir.ActivationFunctionType
AX = mybir.AxisListType.X
P = 128
T = 512
D = 1024
KT = 8
EXPM05 = float(np.exp(-0.5))
MUL, ADD, SUB = ALU.mult, ALU.add, ALU.subtract


class Queue:

    def __init__(self, sem, serial=False):
        self.sem, self.n, self.items, self.past, self.serial = sem, 0, [], {}, serial

    def wait(self, *marks):
        for m in marks:
            if m is None:
                continue
            if isinstance(m, list):
                self.wait(*m)
                continue
            sem, v = m
            if self.past.get(id(sem), 0) < v:
                self.past[id(sem)] = v
                self.items.append((sem, v))

    def __call__(self, fn, *marks):
        self.wait(*marks)
        if self.serial and self.n:
            self.wait((self.sem, self.n))
        self.n += 1
        sem = self.sem
        self.items.append(lambda e: fn(e).then_inc(sem, 1))
        return (sem, self.n)

    def silent(self, fn, *marks):
        self.wait(*marks)
        self.items.append(fn)

    def dma(self, sem, count, fn, *marks):
        self.wait(*marks)
        self.items.append(lambda e: fn(e).then_inc(sem, 16))
        return (sem, count)

    def play(self, eng):
        for it in self.items:
            if isinstance(it, tuple):
                eng.wait_ge(it[0], it[1])
            else:
                it(eng)


def weave(*streams):
    live = [s if isinstance(s, tuple) else (s, 1) for s in streams]
    turn = 0
    while live:
        every = min(n for _, n in live)
        for s, n in list(live):
            if (n == every or turn % n == 0) and next(s, StopIteration) is StopIteration:
                live.remove((s, n))
        turn += 1


def run(stream):
    for _ in stream:
        pass


def chain(*streams):
    for s in streams:
        yield from s()


VECS = [
    ("c", 8), ("c_2", 8), ("mod_b0", 48), ("mod_b1", 48), ("kv_mod_b", 16), ("b_mod_2", 48),
    ("norm_mix_g0", 8), ("norm_mix_g1", 8), ("norm_mlp_g0", 8), ("norm_mlp_g1", 8),
    ("rw_mu", 48), ("rw_w0", 8), ("rw_a0", 8), ("rw_kk", 8), ("rw_ka", 8), ("rw_rk", 8),
    ("rw_lnw", 8), ("rw_lnb", 8), ("kv_norm_g", 8), ("kv_kg", 1), ("fx_qg", 1), ("final_g", 8),
    ("kv_fb", 16), ("g_mix_2", 8), ("conv_w_2", 120), ("a_log_2", 16), ("dt_bias_2", 16),
    ("dn_o_gain_2", 1), ("q_gain_2", 4), ("kv_gain_2", 2), ("g_ffn_2", 8), ("g_final_2", 8),
]
COL = {}
NCOL = 0
for _n, _w in VECS:
    COL[_n] = (NCOL, _w)
    NCOL += _w


def consts():
    j = np.arange(128)[:, None]
    i = np.arange(128)[None, :]
    out = {"ident": (i == j), "strict": (j < i), "incl": (j <= i), "ones": np.ones((128, 128)),
           "onesB": np.ones((128, 128)), "onesC": np.ones((128, 128)),
           "blk": (i // 64 == j // 64),
           "strictR": (j > i), "inclR": (j >= i),
           "neg": np.where(i <= j, 0.0, -1e30)}
    for n in range(7):
        s = 1 << n
        out[f"lv{n}"] = (j // (2 * s) == i // (2 * s)) & (j % (2 * s) < s) & (i % (2 * s) >= s)
    for n in range(7):
        out[f"lvR{n}"] = out[f"lv{n}"].T
    perm = np.zeros((128, 128))
    for m in range(32):
        perm[m + 32, m] = -1.0
        perm[m, m + 32] = 1.0
    out["perm"] = perm
    freq = (np.float32(10000.0) ** (-np.arange(32, dtype=np.float32) / np.float32(32))).astype(np.float32)
    f = np.tile(np.arange(128), (128, 1)).astype(np.float32)
    f[:, 64] = np.tile(freq, 4)
    f[:, 65] = np.arange(128) % 64
    out["iota"] = f
    half = np.zeros((128, 1024))
    for pr in range(8):
        for q in range(128):
            half[2 * pr + q // 64, pr * 128 + q] = 1.0
    names = list(out)
    arr = np.concatenate([out[n].astype(np.float32) for n in names], axis=1)
    return {n: k for k, n in enumerate(names)}, arr, half[:16].astype(np.float32)


CON, _CARR, _PAIR = consts()




def program(nc, a, out):
    ctx = ExitStack()
    with ctx:
        def sb(name, cols, dt=F32):
            return ctx.enter_context(nc.sbuf_tensor(name, [P, cols], dt))

        def new_sem(name):
            return ctx.enter_context(nc.semaphore(name))

        PE, SY = Queue(new_sem("pe")), Queue(new_sem("sp"))
        DV, AC, GP = (Queue(new_sem(n), serial=True) for n in ("dve", "act", "pool"))
        BK = [ctx.enter_context(nc.psum_tensor(f"bank{i}", [P, 512], F32)) for i in range(8)]
        bfree = [[] for _ in range(8)]

        X = sb("X", 4096)
        H = sb("H", 4096)
        NS = 5
        W = sb("W", NS * 2048)
        NCON = _CARR.shape[1]
        con = sb("con", NCON)
        cols = sb("cols", NCOL)
        mods = sb("mods", 48 * 3 + 16 + 64)
        ARENA = 27456
        A = sb("A", ARENA)
        SM = sb("SM", 3072)

        x3 = X[:, :].rearrange("p (k t) -> p k t", k=KT)
        h3 = H[:, :].rearrange("p (k t) -> p k t", k=KT)

        def C(name, n=128):
            k = CON[name] * 128
            return con[:, k:k + n]

        def col(name, k=0, n=1):
            o, w = COL[name]
            return cols[:, o + k:o + k + n]

        def now():
            return [(q.sem, q.n) for q in (PE, DV, AC, GP) if q.n]

        class Carve:
            def __init__(self):
                self.at = 0

            def __call__(self, n):
                self.at += n
                assert self.at <= ARENA, self.at
                return A[:, self.at - n:self.at]

        wsem = [new_sem(f"w{k}") for k in range(NS)]
        wcount = [0] * NS
        wfree = [[] for _ in range(NS)]
        wnext = [0]
        nring = [NS]

        def load(*parts):
            k = wnext[0] % nring[0]
            wnext[0] += 1
            views, mark = [], None
            for off, rows, shape, src in parts:
                n = 1
                for s in shape:
                    n *= s
                assert off + n <= 2048
                v = W[rows[0]:rows[1], k * 2048 + off:k * 2048 + off + n]
                if len(shape) == 2:
                    v = v.rearrange("p (a b) -> p a b", a=shape[0])
                views.append(v)
                wcount[k] += 16
                mark = SY.dma(wsem[k], wcount[k], lambda e, v=v, src=src: e.dma_start(v, src), *wfree[k])
            wfree[k] = []
            return k, views, mark

        def mms(items, *marks):
            PE.wait(*marks)
            for n, (o, l, r, s, e) in enumerate(items):
                f = lambda eng, o=o, l=l, r=r, s=s, e=e: eng.matmul(o, l, r, start=s, stop=e, skip_group_check=True)
                if n + 1 < len(items):
                    PE.silent(f)
                else:
                    return PE(f)

        def trs(items, *marks):
            PE.wait(*marks)
            for n, (o, i) in enumerate(items):
                f = lambda eng, o=o, i=i: eng.transpose(o, i, C("ident")[0:i.shape[0], 0:i.shape[0]])
                if n + 1 < len(items):
                    PE.silent(f)
                else:
                    return PE(f)

        def act(o, i, func, *marks, scale=1.0, bias=0.0, accum=None):
            if accum is not None:
                return AC(lambda e: e.activation(o, i, func, bias=bias, scale=scale, accum_out=accum), *marks)
            return AC(lambda e: e.activation(o, i, func, bias=bias, scale=scale), *marks)

        def tt(q, o, x, y, op, *marks):
            return q(lambda e: e.tensor_tensor(o, x, y, op), *marks)

        def ts(q, o, x, s1, s2, op0, op1, *marks):
            if op1 is None:
                return q(lambda e: e.tensor_scalar(o, x, s1, None, op0), *marks)
            return q(lambda e: e.tensor_scalar(o, x, s1, s2, op0, op1), *marks)

        def rroot(o, *marks):
            act(o, o, ACT.Ln, *marks)
            return act(o, o, ACT.Exp, scale=-0.5)

        def stt(o, x, s, y, op0, op1, *marks):
            return DV(lambda e: e.scalar_tensor_tensor(out=o, in0=x, scalar=s, in1=y, op0=op0, op1=op1), *marks)


        def body():
            s_in = new_sem("s_in")
            for n, (o, s) in enumerate([(con[:, :], a["const"]), (cols[:, :], a["cols"])]):
                m_in = SY.dma(s_in, 16 * (n + 1), lambda e, o=o, s=s: e.dma_start(o, s))
            ready = m_in
            xtok = A[:, 0:4096].rearrange("p (t d) -> p t d", t=4)
            s_x = new_sem("s_x")
            mx = SY.dma(s_x, 16, lambda e: e.dma_start(xtok, a["x"].rearrange("(t p) d -> p t d", p=P)))
            for q in (PE, DV, AC, GP):
                q.wait(ready)
            last = None
            for k in range(KT):
                b = k % 4
                t = trs([(BK[b][:, tk * 128:(tk + 1) * 128], xtok[:, tk, k * 128:(k + 1) * 128]) for tk in range(4)],
                        mx, *bfree[b])
                last = act(x3[:, k, :], BK[b][:, :], ACT.Copy, t)
                bfree[b] = [last]
            xdone = last

            def silu_cols(o, i, tmp):
                m = act(tmp, i, ACT.Sigmoid)
                return tt(DV, o, i, tmp, MUL, m)

            cact = sb("cact", 32)
            m_c = [silu_cols(cact[:, 0:8], col("c", 0, 8), cact[:, 16:24]),
                   silu_cols(cact[:, 8:16], col("c_2", 0, 8), cact[:, 24:32])]
            rowb = SM[:, 0:1024]
            rfree = [[], []]

            def mod_stream(o, w, n, cc, bias, bc, on_pe=()):
                marks = list(bfree[bc])
                for g in range(n // 512):
                    acc = rowb[:, (g % 2) * 512:(g % 2) * 512 + 512]
                    m = None
                    for hf in range(2):
                        k, (v,), tk = load((0, (0, P), (4, 512), w[hf * 512:(hf + 1) * 512, g * 512:(g + 1) * 512].rearrange("(k p) n -> p k n", p=P)))
                        if g in on_pe:
                            b = 4 + g % 2
                            m = mms([(BK[b][0:1, :], cact[:, cc + 4 * hf + j:cc + 4 * hf + j + 1], v[:, j, :], hf == 0 and j == 0,
                                      hf == 1 and j == 3) for j in range(4)], tk, m_c, *bfree[b])
                            wfree[k] = [m]
                            continue
                        for j in range(4):
                            c = cact[:, cc + 4 * hf + j:cc + 4 * hf + j + 1]
                            if hf == 0 and j == 0:
                                m = ts(DV, acc, v[:, j, :], c, None, MUL, None, tk, m_c, *rfree[g % 2])
                            else:
                                m = stt(acc, v[:, j, :], c, acc, MUL, ADD, tk, m)
                        wfree[k] = [m]
                        yield
                    if g in on_pe:
                        m = act(rowp[0:1, :], BK[b][0:1, :], ACT.Copy, m, rowp_free)
                        bfree[b] = [m]
                        m = mms([(BK[bc][:, 4 * g + j:4 * g + j + 1], rowp[0:1, j * 128:(j + 1) * 128], C("ones")[0:1, 0:1], True, True)
                                 for j in range(4)], m, *marks)
                        rowp_free[:] = [m]
                        yield
                        continue
                    m = mms([(BK[bc][:, 4 * g + j:4 * g + j + 1], acc[:, j * 128:(j + 1) * 128], C("ones", 1), True, True)
                             for j in range(4)], m, *marks)
                    rfree[g % 2] = [m]
                    yield
                m = tt(DV, o, BK[bc][:, 0:n // 128], bias, ADD, m)
                bfree[bc] = [m]
                mod_mark.append(m)
                yield

            mod_mark = []
            rowp, rowp_free = SM[:, 2560:3072], []
            mod0, mod1, mod2 = (mods[:, 48 * k:48 * k + 48] for k in range(3))
            modk = mods[:, 144:160]
            gs = mods[:, 160:168]
            g1 = mods[:, 168:176]

            def rsum_free(b):
                return bfree[b]

            sqb = SM[:, 1024:2048]
            sqf = [[], []]
            rstd = SM[:, 2048:2560]
            rstd_r = []

            def rms_rstd(src, nk, inv_n, eps, b, *marks, o=None):
                m = None
                for k in range(nk):
                    s = sqb[:, (k % 2) * 512:(k % 2) * 512 + 512]
                    if k % 2:
                        m1 = tt(DV, s, src[:, k, :], src[:, k, :], MUL, *marks, *sqf[1])
                    else:
                        m1 = act(s, src[:, k, :], ACT.Square, *marks, *sqf[0])
                    m = mms([(BK[b][:, :], C("ones"), s, k == 0, k == nk - 1)], m1, *bfree[b])
                    sqf[k % 2] = [m]
                oo = rstd[:, :] if o is None else o
                m = ts(DV, oo, BK[b][:, :], inv_n, eps, MUL, ADD, m, *rstd_r)
                bfree[b] = [m]
                return rroot(oo, m)

            def norm_mod(o3, g, sc, sh, b, *marks):
                m = rms_rstd(x3, KT, 1.0 / D, 1e-6, b, *marks)
                if sc is not None:
                    mg = ts(DV, gs, sc, 1.0, None, ADD, None, *marks)
                    mg = tt(DV, gs, gs, g, MUL, mg)
                last = []
                for k in range(KT):
                    m1 = tt(DV, o3[:, k, :], x3[:, k, :], rstd[:, :], MUL, m, *marks)
                    if sc is not None:
                        last.append(act(o3[:, k, :], o3[:, k, :], ACT.Identity, m1, mg, *marks,
                                        scale=gs[:, k:k + 1], bias=sh[:, k:k + 1]))
                    else:
                        last.append(act(o3[:, k, :], o3[:, k, :], ACT.Copy, m1, scale=g[:, k:k + 1]))
                rstd_r[:] = [m1]
                return last

            def proj(w, src3, nk, n, banks, evac, *marks, width=256):
                j = 0
                for n0 in range(0, n, width):
                    wd = min(width, n - n0)
                    k, (v,), tk = load((0, (0, P), (nk, wd), w[:, n0:n0 + wd].rearrange("(k p) n -> p k n", p=P)))
                    for c in range(0, wd, 128):
                        cw = min(128, wd - c)
                        b = banks[j % len(banks)]
                        it = [(BK[b][0:cw, :], v[:, kk, c:c + cw], src3[:, kk, :], kk == 0, kk == nk - 1) for kk in range(nk)]
                        if j == 0 and marks and isinstance(marks[0], list) and len(marks[0]) == nk == 8:
                            PE.wait(*marks[1:])
                            for kk in range(nk):
                                m = mms(it[kk:kk + 1], tk, *bfree[b], marks[0][kk])
                        else:
                            m = mms(it, tk, *bfree[b], *marks)
                        bfree[b] = [evac(j, b, m)]
                        j += 1
                        yield
                    wfree[k] = [m]

            run(mod_stream(mod0, a["mod_w0"], 6144, 0, col("mod_b0", 0, 48), 6, on_pe=(1, 3, 5, 8, 10)))
            cv = Carve()
            XM = cv(3 * 4096)
            xm = [XM[:, 4096 * j:4096 * j + 4096].rearrange("p (k t) -> p k t", k=KT) for j in range(3)]
            LO = cv(512)
            ZG = cv(1024)
            XX = cv(4096)
            xx3 = XX.rearrange("p (k t) -> p k t", k=KT)
            MX = cv(1024)
            mh = norm_mod(h3, col("norm_mix_g0", 0, 8), mod0[:, 8:16], mod0[:, 0:8], 7, xdone, mod_mark[-1])
            start = now()
            xpark = nc.dram_tensor("xpark", (P, 4096), F32, kind="Internal").ap()
            s_park = new_sem("s_park")
            m_park = SY.dma(s_park, 16, lambda e: e.dma_start(xpark, X[:, :]), start)
            mxx = []
            for k in range(KT):
                m1 = tt(DV, xx3[:, k, 1:T], h3[:, k, 0:T - 1], h3[:, k, 1:T], SUB, start)
                mxx.append([m1, ts(DV, xx3[:, k, 0:1], h3[:, k, 0:1], -1.0, None, MUL, None)])

            def mix(o, j, k, *marks):
                return stt(o, xx3[:, k, :], col("rw_mu", 8 * j + k), h3[:, k, :], MUL, ADD, mxx[k], *marks)

            k1, (w1v, a1v, g1v), tk1 = load((0, (0, P), (8, 64), a["rw_w1"].rearrange("(k p) n -> p k n", p=P)),
                                            (512, (0, P), (8, 64), a["rw_a1"].rearrange("(k p) n -> p k n", p=P)),
                                            (1024, (0, P), (8, 96), a["rw_g1"][:, 0:96].rearrange("(k p) n -> p k n", p=P)))
            k2, (g1w,), tk2 = load((0, (0, P), (8, 64), a["rw_g1"][:, 96:160].rearrange("(k p) n -> p k n", p=P)))
            mfree = [[], []]
            n = 0
            for j in (1, 4, 5):
                for k in range(KT):
                    mb = MX[:, (n % 2) * 512:(n % 2) * 512 + 512]
                    m = mix(mb, j, k, *mfree[n % 2])
                    f, l = k == 0, k == KT - 1
                    if j == 1:
                        m = mms([(BK[0][0:64, :], w1v[:, k, :], mb, f, l)], m, tk1, *bfree[0])
                    elif j == 4:
                        m = mms([(BK[1][64:128, :], a1v[:, k, :], mb, f, l)], m, *bfree[1])
                    else:
                        m = mms([(BK[2][0:96, :], g1v[:, k, :], mb, f, l), (BK[3][0:64, :], g1w[:, k, :], mb, f, l)],
                                m, tk2, *bfree[2], *bfree[3])
                    mfree[n % 2] = [m]
                    n += 1
                if j == 1:
                    ml = [act(LO[0:64, :], BK[0][0:64, :], ACT.Tanh, m)]
                    bfree[0] = [ml[-1]]
                elif j == 4:
                    ml.append(act(LO[64:128, :], BK[1][64:128, :], ACT.Copy, m))
                    bfree[1] = [ml[-1]]
                else:
                    ml.append(act(ZG[0:96, 0:512], BK[2][0:96, :], ACT.Sigmoid, m))
                    ml.append(act(ZG[0:64, 512:1024], BK[3][0:64, :], ACT.Sigmoid, m))
                    bfree[2], bfree[3] = [ml[-2]], [ml[-1]]
            wfree[k1] = [m]
            wfree[k2] = [m]
            xmr = {}
            for d, j in ((1, 2), (0, 0), (2, 3)):
                for k in range(KT):
                    m = mix(xm[d][:, k, :], j, k)
                    ml.append(m)
                xmr[d] = m
            omka = mods[:, 176:184]
            ml.append(ts(DV, omka, col("rw_ka", 0, 8), -1.0, 1.0, MUL, ADD))
            halfw, halfa = mods[:, 201:209], modk[:, 0:8]
            ts(DV, halfw, col("rw_w0", 0, 8), 0.5, None, MUL, None)
            ts(DV, halfa, col("rw_a0", 0, 8), 0.5, None, MUL, None)
            start = now()

            cv.at = 3 * 4096 + 512 + 1024
            xa = [X[:, 512 * j:512 * j + 512] for j in range(8)]
            Rb, Kb, Lw, Ab, KKb, Lb, t0, t1 = xa
            nring[0] = NS - 1
            w4 = NS * 2048 - 2048
            spare = [W[:, w4 + 512 * j:w4 + 512 * j + 512] for j in range(4)] + [SM[:, 512 * j:512 * j + 512] for j in range(6)]
            start = [start, wfree[NS - 1]]
            sets = [[cv(1024)] + [cv(512) for _ in range(6)] for _ in range(2)]
            hw = [[cv(1024)] + [cv(512) for _ in range(4)] + [cv(1024)],
                  [W[:, w4:w4 + 1024], spare[2], spare[3], spare[6], spare[7], SM[:, 0:1024]]]
            BHt, Yb = cv(512), cv(512)
            KHt, Vt = spare[8:10]
            sm = cv(64)
            SS, SPs = cv(64), [cv(64), cv(64)]
            c4 = lambda v: v.rearrange("p (c t) -> p c t", c=4)
            yg = h3
            for w_ in hw:
                for z in (w_[0], w_[5]):
                    zm = GP(lambda e, z=z: e.memset(z, 0.0), start)
            for z in SPs:
                zm = GP(lambda e, z=z: e.memset(z, 0.0), start)
            for s_ in sets:
                for z in (s_[1][64:128, :], s_[2][0:64, :], s_[3][64:128, :], s_[4][0:64, :]):
                    zm = GP(lambda e, z=z: e.memset(z, 0.0), start)

            def fetch(ct, since, full=None):
                V = sets[ct % 2][5]
                cs = slice(ct * 128, ct * 128 + 128)
                k1, (wr, wk), tk1 = load((0, (0, P), (8, 128), a["rw_wr"][:, cs].rearrange("(k p) n -> p k n", p=P)),
                                         (1024, (0, P), (8, 128), a["rw_wk"][:, cs].rearrange("(k p) n -> p k n", p=P)))
                k2, (wv, w2, a2), tk2 = load(
                    (0, (0, P), (8, 128), a["rw_wv"][:, cs].rearrange("(k p) n -> p k n", p=P)),
                    (1024, (0, 64), (128,), a["rw_w2"][:, cs]), (1024, (64, 128), (128,), a["rw_a2"][:, cs]))

                def big(b, w, src, tk):
                    for q in range(4):
                        m = mms([(BK[b][:, :], w[:, k, :], src[:, k, :], k == 0, k == 7) for k in (2 * q, 2 * q + 1)],
                                tk, *bfree[b], *since, xmr[0 if src is xm[0] else 1 if src is xm[1] else 2])
                        if q < 3:
                            yield
                    bigs.append(m)

                bigs = []
                yield from big(0, wk, xm[1], tk1)
                mk = act(Kb, BK[0][:, :], ACT.Copy, bigs[-1], *since)
                bfree[0] = [mk]
                m1 = ts(DV, KKb, Kb, col("rw_kk", ct), None, MUL, None, mk, *since)
                m2 = act(t0, KKb, ACT.Square, m1, *since)
                yield
                yield from big(1, wr, xm[0], tk1)
                m = bigs[-1]
                wfree[k1] = [m]
                mr = act(Rb, BK[1][:, :], ACT.Copy, m, *since)
                bfree[1] = [mr]
                yield
                m = mms([(BK[0][:, :], C("blk"), t0, True, True)], m2, *bfree[0])
                m = ts(DV, t0, BK[0][:, :], 1e-24, None, ALU.max, None, m)
                bfree[0] = [m]
                yield from big(1, wv, xm[2], tk2)
                mv = act(V, BK[1][:, :], ACT.Copy, bigs[-1], *since, full)
                bfree[1] = [mv]
                fetched[ct] = [k2, w2, a2, tk2, m, mk, mr, mv]
                yield

            def prep(ct, since):
                AR, BHa, BHb, KHa, KHb, V, BO = sets[ct % 2]
                ar = AR.rearrange("p (c s t) -> p c s t", c=4, s=2)
                k2, w2, a2, tk2, m, mk, mr, mv = fetched[ct]
                m = rroot(t0, m)
                mkk = tt(DV, KKb, KKb, t0, MUL, m)
                m = mms([(BK[0][:, :], w2[:, :], LO[0:64, :], True, True)], tk2, *bfree[0])
                m1 = act(Lw, BK[0][:, :], ACT.Tanh, m, *since, bias=halfw[:, ct:ct + 1], scale=0.5)
                bfree[0] = [m1]
                m = mms([(BK[1][:, :], a2[:, :], LO[64:128, :], True, True)], *bfree[1])
                wfree[k2] = [m]
                ma = act(Ab, BK[1][:, :], ACT.Tanh, m, *since, bias=halfa[:, ct:ct + 1], scale=0.5)
                bfree[1] = [ma]
                mlw = ts(DV, Lw, Lw, -0.5 * EXPM05, -0.5 * EXPM05, MUL, ADD, m1)
                ma = ts(GP, Ab, Ab, 0.5, 0.5, MUL, ADD, ma)
                yield
                for c in range(4):
                    s = slice(c * 128, c * 128 + 128)
                    mL = DV(lambda e, s=s: e.tensor_tensor_scan(Lb[:, s], C("ones"), Lw[:, s], 0.0, MUL, ADD), mlw, *since)
                yield
                L3 = c4(Lb)
                eM, eE = sm[:, 16 * (ct % 2):16 * (ct % 2) + 4], sm[:, 16 * (ct % 2) + 4:16 * (ct % 2) + 8]
                mid = sm[:, 16 * (ct % 2) + 8:16 * (ct % 2) + 12]
                m1 = DV(lambda e: e.tensor_copy(mid, L3[:, :, 63]), mL, *since)
                m2 = tt(DV, eE, L3[:, :, 127], mid, SUB, m1)
                mE = act(eE, eE, ACT.Exp, m2)
                mM = act(eM, mid, ACT.Exp, m1)
                for c in range(4):
                    mL = ts(DV, L3[:, c, :], L3[:, c, :], mid[:, c:c + 1], None, SUB, None, m1)
                m = ts(DV, t0, Ab, col("rw_ka", ct), omka[:, ct:ct + 1], MUL, ADD, ma)
                mk2 = tt(DV, Kb, Kb, t0, MUL, m)
                yield
                m1 = act(t0, Lb, ACT.Exp, mL, mk2)
                mRh = tt(DV, ar[:, :, 1, :], c4(Rb), c4(t0), MUL, m1, mr, *since)
                m2 = tt(DV, t1, Lb, Lw, SUB, mL)
                m2 = act(t1, t1, ACT.Exp, m2)
                mAh = stt(ar[:, :, 0, :], c4(t1), -1.0, c4(KKb), MUL, MUL, m2, mkk)
                yield
                m1 = act(t0, Lb, ACT.Exp, mRh, scale=-1.0)
                mKh = [tt(DV, KHa[0:64, :], Kb[0:64, :], t0[0:64, :], MUL, m1, zm, *since),
                       tt(DV, KHb[64:128, :], Kb[64:128, :], t0[64:128, :], MUL)]
                m2 = tt(GP, t1, KKb, Ab, MUL, mAh, mkk)
                mBh = [tt(DV, BHa[0:64, :], t1[0:64, :], t0[0:64, :], MUL, m2, m1, *since),
                       tt(DV, BHb[64:128, :], t1[64:128, :], t0[64:128, :], MUL)]
                yield
                m = stt(t1, Rb, col("rw_rk", ct), Kb, MUL, MUL, mBh)
                m = mms([(BK[0][:, :], C("blk"), t1, True, True)], m, *bfree[0])
                mbo = tt(DV, BO, BK[0][:, :], V, MUL, m, mv, *since)
                bfree[0] = [mbo]
                prepared[ct] = [mRh, mAh, mKh, mBh, mbo, mv, mE, mM]
                used_tmp[ct] = now()
                yield

            def invert(NT, TT, TM, US, MT, R, banks, nb, sfree, m_nt, q0=None):
                bu, bt, bm = banks
                c3 = lambda v: v.rearrange("p (c t) -> p c t", c=nb)
                bc = lambda name: C(name).unsqueeze(1).broadcast_to([P, nb, 128])
                lv = "lvR" if R else "lv"
                n3, t3, m3 = c3(NT), c3(TT), c3(TM)
                u3, k3 = c3(US), c3(MT)
                q = slice(0, nb * 128)
                m = tt(q0 or GP, k3, n3, bc(lv + "0"), MUL, m_nt, *sfree)
                mt_t = tt(GP, t3, k3, bc("ident"), ADD, m, *sfree)
                m1 = mms([(BK[bu][:, c * 128:c * 128 + 128], k3[:, c, :], C("ident"), True, True) for c in range(nb)],
                         m, *bfree[bu])
                mt_m = tt(DV, m3, c3(BK[bu][:, q]), bc("ident"), ADD, m1, *sfree)
                bfree[bu] = [mt_m]
                mk_r = m1
                yield
                for lev in range(1, 7):
                    last = lev == 6
                    m = tt(GP, k3, n3, bc(lv + str(lev)), MUL, mk_r)
                    mu = mms([(BK[bu][:, c * 128:c * 128 + 128], k3[:, c, :], m3[:, c, :], True, True) for c in range(nb)],
                             m, mt_m, *bfree[bu])
                    mk_r = mu
                    me = act(US, BK[bu][:, q], ACT.Copy, mu)
                    bfree[bu] = [me]
                    yield
                    mA = mms([(BK[bt][:, c * 128:c * 128 + 128], u3[:, c, :], t3[:, c, :], True, True) for c in range(nb)],
                             me, mt_t, *bfree[bt])
                    if not last:
                        mB = mms([(BK[bm][:, c * 128:c * 128 + 128], t3[:, c, :], u3[:, c, :], True, True)
                                  for c in range(nb)], *bfree[bm])
                        mt_m = tt(DV, m3, m3, c3(BK[bm][:, q]), ADD, mB)
                        bfree[bm] = [mt_m]
                        mt_t = tt(DV, t3, t3, c3(BK[bt][:, q]), ADD, mB)
                    else:
                        mt_t = tt(DV, t3, t3, c3(BK[bt][:, q]), ADD, mA)
                    bfree[bt] = [mt_t]
                    yield
                inverse.append(mt_t)

            inverse = []
            prepared, used_tmp, chunked, headed, fetched, tokened = {}, {}, {}, {}, {}, {}

            def head(ct, hd, tok, mz):
                AR, BHa, BHb, KHa, KHb, V, BO = sets[ct % 2]
                NR, TT, TM, US, MT, AKRK = hw[hd]
                SP = SPs[hd]
                NT, RBT, AKT, RKT = NR[:, 0:512], NR[:, 512:1024], AKRK[:, 0:512], AKRK[:, 512:1024]
                XS, UU = MT[:, 0:64], MT[:, 64:128]
                ar = AR.rearrange("p (c s t) -> p c s t", c=4, s=2)
                eM, eE = sm[:, 16 * (ct % 2):16 * (ct % 2) + 4], sm[:, 16 * (ct % 2) + 4:16 * (ct % 2) + 8]
                hp = slice(64 * hd, 64 * hd + 64)
                pm = prepared[ct]
                ba, bb, bc = (2, 3, 4) if hd == 0 else (5, 6, 7)
                before = [headed[ct - 1]] if ct else []
                msc = []
                for n, (src, dd, pr) in enumerate([(BHb if hd else BHa, NR, 0), (BHb if hd else BHa, NR, 1),
                                                       (KHb if hd else KHa, AKRK, 0), (KHb if hd else KHa, AKRK, 1)]):
                    b = (ba, bb, bc)[n % 3]
                    items = []
                    for cc in range(2):
                        c = 2 * pr + cc
                        o = BK[b][:, cc * 256:cc * 256 + 256].rearrange("p (s t) -> p s t", s=2)
                        items.append((o[0:64, :, :], src[:, c * 128:c * 128 + 64], ar[:, c, :, :], True, True))
                        items.append((o[64:128, :, 64:128], src[:, c * 128 + 64:c * 128 + 128],
                                      ar[:, c, :, 64:128], True, True))
                    m = mms(items, pm, *bfree[b])
                    o4 = BK[b][:, :].rearrange("p (c s t) -> p c s t", c=2, s=2)
                    d4 = dd.rearrange("p (s c t) -> p c s t", s=2, c=4)[:, 2 * pr:2 * pr + 2, :, :]
                    mc = act(d4[0:64, :, :, 64:128], o4[0:64, :, :, 64:128], ACT.Copy, m, mz, *before)
                    for rows, q, mo in ((slice(64, 128), slice(64, 128), None), (slice(0, 64), slice(0, 64), mc)):
                        mk = C("strict", 256).rearrange("p (s t) -> p s t", s=2)[rows, :, q].unsqueeze(1).broadcast_to([64, 2, 2, 64])
                        mm_ = [tt(DV, d4[rows, :, :, q], o4[rows, :, :, q], mk, MUL, m, mz, mo, *before), mc]
                    msc.append(mm_)
                    bfree[b] = [mm_]
                    yield
                yield from invert(NT, TT, TM, US, MT, False, (ba, bb, bc), 4, before, msc)
                mt = inverse[-1]
                ms = GP(lambda e: e.memset(SS[hp, 0:64], 0.0), *before)
                my = None
                for c in range(4):
                    q = slice(c * 128, c * 128 + 128)
                    vt = Vt[:, c * 128 + 64 * hd:c * 128 + 64 * hd + 64]
                    msp = ts(DV, SP[hp, :], SS[hp, :], eM[hp, c:c + 1], None, MUL, None, ms, my, mz)
                    m = mms([(BK[ba][:, 0:64], ar[:, c, 0, :], SP, True, False),
                             (BK[ba][:, 0:64], AKT[:, q], vt, False, True)], msp, tok, msc, *bfree[ba])
                    m = act(XS, BK[ba][:, 0:64], ACT.Copy, m)
                    bfree[ba] = [m]
                    yield
                    m = mms([(BK[bb][:, 0:64], TT[:, q], XS, True, True)], m, mt, *bfree[bb])
                    mu = act(UU, BK[bb][:, 0:64], ACT.Copy, m)
                    bfree[bb] = [mu]
                    yield
                    m = mms([(BK[ba][hp, 64:128], BHt[:, c * 128 + 64 * hd:c * 128 + 64 * hd + 64], UU, True, False),
                             (BK[ba][hp, 64:128], KHt[:, c * 128 + 64 * hd:c * 128 + 64 * hd + 64], vt, False, True)],
                            mu, *bfree[ba])
                    m = tt(DV, SS[hp, :], SP[hp, :], BK[ba][hp, 64:128], ADD, m)
                    bfree[ba] = [m]
                    ms = ts(DV, SS[hp, :], SS[hp, :], eE[hp, c:c + 1], None, MUL, None, m)
                    my = mms([(BK[bc][hp, q], SP, ar[:, c, 1, :], True, False),
                              (BK[bc][hp, q], UU, RBT[:, q], False, False),
                              (BK[bc][hp, q], vt, RKT[:, q], False, True)], *bfree[bc])
                    yield
                my = act(Yb[hp, :], BK[bc][hp, :], ACT.Copy, my, before, chunked.get(ct - 1))
                bfree[bc] = [my]
                ydone[hd] = my
                yield

            ydone = [None, None]

            def heads(ct, mz):
                AR, BHa, BHb, KHa, KHb, V, BO = sets[ct % 2]
                pm = prepared[ct]
                prev = [headed[ct - 1]] if ct else []
                tok = []
                for b, src, dst in ((2, (BHa, BHb), BHt), (5, (KHa, KHb), KHt), (3, (V,), Vt)):
                    m = mms([(BK[b][:, c * 128:c * 128 + 128], s_[:, c * 128:c * 128 + 128], C("ident"), i == 0, i == len(src) - 1)
                             for c in range(4) for i, s_ in enumerate(src)], pm, *bfree[b])
                    m = act(dst, BK[b][:, :], ACT.Copy, m, *prev)
                    bfree[b] = [m]
                    tok.append(m)
                tokened[ct] = tok
                yield
                fs = [head(ct, 0, tok, mz), head(ct, 1, tok, mz)]
                while fs:
                    for f in list(fs):
                        if next(f, StopIteration) is StopIteration:
                            fs.remove(f)
                    yield
                headed[ct] = now()

            def post(ct):
                BO, US = sets[ct % 2][6], t1
                cs = slice(ct * 128, ct * 128 + 128)
                kg, (ga, gb), tkg = load((0, (0, 96), (128,), a["rw_g2"][0:96, cs]), (128, (0, 64), (128,), a["rw_g2"][96:160, cs]))
                m = mms([(BK[0][:, :], C("blk"), Yb, True, True)], ydone, *bfree[0])
                m = stt(Yb, BK[0][:, :], -1.0 / 64, Yb, MUL, ADD, m)
                bfree[0] = [m]
                yield
                m2 = act(US, Yb, ACT.Square, m, headed[ct], used_tmp.get(ct + 1))
                m2 = mms([(BK[1][:, :], C("blk"), US, True, True)], m2, *bfree[1])
                m2 = ts(DV, US, BK[1][:, :], 1.0 / 64, 64e-5, MUL, ADD, m2)
                bfree[1] = [m2]
                m2 = rroot(US, m2)
                yield
                m = tt(DV, Yb, Yb, US, MUL, m2)
                m = act(Yb, Yb, ACT.Identity, m, scale=col("rw_lnw", ct), bias=col("rw_lnb", ct))
                mg = mms([(BK[0][:, :], ga[:, :], ZG[0:96, 0:512], True, False),
                          (BK[0][:, :], gb[:, :], ZG[0:64, 512:1024], False, True)], tkg, *bfree[0])
                wfree[kg] = [mg]
                yield
                m = tt(DV, Yb, Yb, BO, ADD, m)
                m = tt(DV, yg[:, ct, :], Yb, BK[0][:, :], MUL, m, mg)
                bfree[0] = [m]
                chunked[ct] = [now(), m]
                yield

            start = [start, now(), m_park]
            run(fetch(0, [m_park], start))
            run(prep(0, start))
            run(fetch(1, [start, used_tmp[0]]))

            def idle(n):
                for _ in range(n):
                    yield

            for ct in range(8):
                beside = [lambda: idle(4), (lambda ct=ct: post(ct - 1)) if ct else (lambda: idle(4))]
                if ct < 7:
                    beside.append(lambda ct=ct: prep(ct + 1, [used_tmp[ct]] + ([headed[ct - 1], chunked[ct - 1]] if ct else [])))
                if ct < 6:
                    beside.append(lambda: idle(2))
                    beside.append(lambda ct=ct: fetch(ct + 2, [used_tmp[ct + 1], tokened[ct]]))
                weave(heads(ct, zm), chain(*beside))
            run(post(7))
            m_ret = SY.dma(s_park, 32, lambda e: e.dma_start(X[:, :], xpark), now())
            nring[0] = NS
            wfree[NS - 1] = now()
            mg1 = ts(DV, g1, mod0[:, 16:24], 1.0, None, ADD, None)

            def residual(gate, *marks):
                def evac(j, b, m):
                    return stt(x3[:, j, :], BK[b][:, :], gate[:, j:j + 1], x3[:, j, :], MUL, ADD, m, *marks)
                return evac

            run(proj(a["rw_wo"], h3, KT, D, (0, 1), residual(g1, mg1, m_ret), now()))
            def down(w, src3, nk, n, pairs, evac, *marks):
                for g in range(n // 256):
                    bs = pairs[g % len(pairs)]
                    for kg in range(nk // 8):
                        k, (v,), tk = load((0, (0, P), (8, 256), w[kg * 1024:kg * 1024 + 1024, g * 256:g * 256 + 256].rearrange("(k p) n -> p k n", p=P)))
                        for c in range(2):
                            m = mms([(BK[bs[c]][:, :], v[:, kk, c * 128:c * 128 + 128], src3[:, kg * 8 + kk, :],
                                      kg == 0 and kk == 0, kg == nk // 8 - 1 and kk == 7) for kk in range(8)],
                                    tk, *bfree[bs[c]], *marks)
                        wfree[k] = [m]
                        yield
                    for c in range(2):
                        bfree[bs[c]] = [evac(2 * g + c, bs[c], m)]

            def mlp(l, g, mod, *beside):
                mh = norm_mod(h3, g, mod[:, 32:40], mod[:, 24:32], 7, now())
                hid = A[:, 0:16384].rearrange("p (k t) -> p k t", k=32)
                mg = ts(DV, g1, mod[:, 40:48], 1.0, None, ADD, None, now())

                def evac(j, b, m):
                    m = act(hid[:, j, :], BK[b][:, :], ACT.Relu, m)
                    hm.append(tt(GP, hid[:, j, :], hid[:, j, :], hid[:, j, :], MUL, m))
                    return m

                hm = []
                def both():
                    yield from proj(a["mlp_up" + l], h3, KT, 4096, (0, 1, 2, 3), evac, mh)
                    yield from down(a["mlp_down" + l], hid, 32, D, ((0, 1), (2, 3)), residual(g1, mg), hm)

                weave(both(), *beside)

            mlp("0", col("norm_mlp_g0", 0, 8), mod0,
                chain(lambda: mod_stream(modk, a["kv_mod_w"], 2048, 0, col("kv_mod_b", 0, 16), 6),
                      lambda: mod_stream(mod1, a["mod_w1"], 6144, 0, col("mod_b1", 0, 48), 6)))

            cv = Carve()
            KK_, VV_, QQ_, GG_ = [cv(4096) for _ in range(4)]
            kT, qT, gT = [v.rearrange("p (k t) -> p k t", k=KT) for v in (KK_, QQ_, GG_)]
            vt = VV_.rearrange("p (t d) -> p t d", t=4)
            LF, FT, FA, FE = [cv(64) for _ in range(4)]
            lf3, ft3 = LF.rearrange("p (t h) -> p t h", t=4), FT.rearrange("p (t h) -> p t h", t=4)
            dg = [H[:, 2048 + 128 * n:2176 + 128 * n] for n in range(4)]
            work = [[cv(512), cv(512), cv(2048), cv(16), dg[n]] if n < 2 else
                    [SM[:, 1024 * n - 2048:1024 * n - 1536], SM[:, 1024 * n - 1536:1024 * n - 1024], cv(2048), cv(16), dg[n]] for n in range(4)]
            nb_ = cv(512)
            start = now()

            def headnorm(dst, b, m, mask, inv_n, eps, gain, bn, o=None):
                settle()
                z = hn[0] % 2
                hn[0] += 1
                nb = nbs[z]
                m1 = act(dst, BK[b][:, :], ACT.Copy, m, start)
                m2 = act(nb, dst, ACT.Square, m1, *nbf[z])

                def rest():
                    m3 = mms([(BK[bn][:, :], C(mask), nb, True, True)], m2, *bfree[bn])
                    m4 = ts(DV, nb, BK[bn][:, :], inv_n, eps, MUL, ADD, m3)
                    bfree[bn] = [m4]
                    m5 = rroot(nb, m4)
                    nbf[z] = [stt(dst, dst, gain, nb, MUL, MUL, m5, m1)]

                pend.append(rest)
                return m1

            def settle():
                while pend:
                    pend.pop()()

            nbs, pend, hn = [nb_, SM[:, 2560:3072]], [], [0]
            nbf = [[], []]
            mh = norm_mod(h3, col("kv_norm_g", 0, 8), modk[:, 8:16], modk[:, 0:8], 7, start)
            qgain = mods[:, 184:185]
            mq = ts(DV, qgain, col("fx_qg"), 0.125, None, MUL, None)
            run(proj(a["kv_w"][:, 0:1024], h3, KT, D, (0, 1, 2),
                     lambda j, b, m: headnorm(kT[:, j, :], b, m, "blk", 1.0 / 64, 1e-6, col("kv_kg"), 3), mh))

            settle()

            def proj_tok(w, src3, n, banks, evac, *marks):
                for n0 in range(0, n, 512):
                    sl = [load((0, (0, P), (4, 512), w[hf * 512:hf * 512 + 512, n0:n0 + 512].rearrange("(k p) n -> p k n", p=P)))
                          for hf in range(2)]
                    for t in range(4):
                        b = banks[t % len(banks)]
                        m = mms([(BK[b][:, :], src3[:, k, t * 128:t * 128 + 128], sl[k // 4][1][0][:, k % 4, :], k == 0, k == 7)
                                 for k in range(8)], sl[0][2], sl[1][2], *bfree[b], *marks)
                        bfree[b] = [evac(t, n0, b, m)]
                        yield
                    wfree[sl[0][0]] = [m]
                    wfree[sl[1][0]] = [m]

            run(proj_tok(a["kv_w"][:, 1024:2048], h3, D, (0, 1, 2, 3),
                         lambda t, n0, b, m: act(vt[:, t, n0:n0 + 512], BK[b][:, :], ACT.Copy, m, start), mh))

            def small_tok(w, n, b, *marks):
                k, (v,), tk = load((0, (0, P), (8, n), w.rearrange("(k p) n -> p k n", p=P)))
                m = mms([(BK[b][:, t * n:t * n + n], h3[:, kk, t * 128:t * 128 + 128], v[:, kk, :], kk == 0, kk == 7)
                         for t in range(4) for kk in range(8)], tk, *bfree[b], *marks)
                wfree[k] = [m]
                return m

            def bc4(v):
                return v.unsqueeze(1).broadcast_to([P, 4, 16])

            v3 = lambda v: v.rearrange("p (t h) -> p t h", t=4)
            m = small_tok(a["kv_w"][:, 2048:2064], 16, 4, mh)
            m = tt(DV, v3(FA), v3(BK[4][:, 0:64]), bc4(col("kv_fb", 0, 16)), ADD, m, start)
            bfree[4] = [m]
            m1 = act(FE, FA, ACT.Abs, m, start)
            m1 = act(FE, FE, ACT.Exp, m1, scale=-1.0)
            m1 = act(FE, FE, ACT.Ln, m1, bias=1.0)
            m = ts(DV, FA, FA, 0.0, None, ALU.min, None, m1)
            mlf = tt(DV, LF, FA, FE, SUB, m, m1)
            m = mms([(BK[5][:, 16 * t:16 * t + 16], C("incl") if j == t else C("ones"), lf3[:, j, :], j == 0, j == t)
                     for t in range(4) for j in range(t + 1)], mlf, *bfree[5])
            mft = act(FT, BK[5][:, 0:64], ACT.Copy, m)
            bfree[5] = [mft]

            mh = norm_mod(h3, col("norm_mix_g1", 0, 8), mod1[:, 8:16], mod1[:, 0:8], 7, now())
            run(proj(a["fx_wqg"][:, 0:1024], h3, KT, D, (0, 1, 2),
                     lambda j, b, m: headnorm(qT[:, j, :], b, m, "blk", 1.0 / 64, 1e-6, qgain, 3), mh, mq))
            settle()
            run(proj(a["fx_wqg"][:, 1024:2048], h3, KT, D, (0, 1, 2),
                     lambda j, b, m: act(gT[:, j, :], BK[b][:, :], ACT.Sigmoid, m), mh))
            cuml = con[:, CON["incl"] * 128:CON["incl"] * 128 + 512]

            def attention(banks, bufs, qk, causal, vcols, width, rows, evac, mr, scale=1.0, forget=None):
                bs, bt, bo = banks
                Fb, S, PT, sm_, DG = bufs
                p3 = PT.rearrange("p (k t) -> p k t", k=4)
                mo = None
                mF = None
                if forget is not None:
                    m = mms([(BK[bo][:, 128 * j:512], lf3[:, j, forget:forget + 1].broadcast_to([P, 128]), cuml[:, 0:512 - 128 * j],
                              j == 0, j == 3) for j in range(4)], mlf, *bfree[bo], mr)
                    mF = act(Fb, BK[bo][:, :], ACT.Copy, m, mr)
                    bfree[bo] = [mF]
                    yield
                for qt in range(4):
                    n = (qt + 1) * 128 if causal else 512
                    m = mms([(BK[bs][:, 0:n], q_(qt), k_(n), i == 0, i == len(qk) - 1) for i, (q_, k_) in enumerate(qk)] +
                            ([(BK[bs][:, n - 128:n], C("ident"), C("neg"), False, True)] if forget is not None else []),
                            *bfree[bs], mr)
                    if forget is not None:
                        m = DV(lambda e, qt=qt, n=n: e.scalar_tensor_tensor(
                            out=S[:, 0:n], in0=Fb[:, 0:n], scalar=ft3[:, qt, forget:forget + 1], in1=BK[bs][:, 0:n],
                            op0=SUB, op1=SUB, reverse1=True), m, mF, mft, mo)
                        bfree[bs] = [m]
                        src = S
                    else:
                        src = BK[bs]
                    mx = DV(lambda e, n=n, src=src: e.tensor_reduce(sm_[:, 1:2], src[:, 0:n], AX, ALU.max, negate=True), m, mo)
                    if scale != 1.0:
                        mx = ts(DV, sm_[:, 1:2], sm_[:, 1:2], scale, None, MUL, None, mx)
                    yield
                    m = act(S[:, 0:n], src[:, 0:n], ACT.Exp, mx, mo, scale=scale, bias=sm_[:, 1:2], accum=sm_[:, 2:3])
                    if forget is None:
                        bfree[bs] = [m]
                    mr_ = DV(lambda e: e.reciprocal(sm_[:, 3:4], sm_[:, 2:3]), m)
                    m = ts(DV, DG, C("ident"), sm_[:, 3:4], None, MUL, None, mr_, mo)
                    yield
                    nk = n // 128
                    mo = mms([(BK[bt][:, k * 128:k * 128 + 128], S[:, k * 128:k * 128 + 128], DG, True, True) for k in range(nk)],
                             m, *bfree[bt])
                    m = act(p3[:, 0:nk, qt * 128:qt * 128 + 128], BK[bt][:, 0:n].rearrange("p (k t) -> p k t", k=nk),
                            ACT.Copy, mo, mr)
                    bfree[bt] = [m]
                    yield
                m = mms([(BK[bo][rows, (k * 128 if causal else 0):512], vcols(k), p3[:, k, (k * 128 if causal else 0):512],
                          k == 0, k == 3) for k in range(4)], m, *bfree[bo])
                m = evac(m)
                bfree[bo] = [m]
                yield

            start = now()
            QZ = [H[:, 512 * n:512 * n + 512] for n in range(4)]
            mqz = [GP(lambda e, n=n: e.memset(QZ[n][64 - 64 * (n % 2):128 - 64 * (n % 2), :], 0.0), start) for n in range(4)]

            def fox(n):
                par, bs, bo = n % 2, 2 * n, 2 * n + 1
                qz, m = QZ[n], start
                for ct in range(n // 2, 8, 2):
                    hd = 2 * ct + par
                    hp = slice(64 * par, 64 * par + 64)
                    mc = DV(lambda e, ct=ct: e.tensor_copy(qz[hp, :], qT[hp, ct, :]), m)
                    done = []

                    def evac(m, ct=ct):
                        done.append(tt(DV, gT[hp, ct, :], BK[bo][hp, :], gT[hp, ct, :], MUL, m))
                        return done[-1]

                    yield from attention(
                        (bs, bo, bo), work[n],
                        [(lambda qt: qz[:, qt * 128:qt * 128 + 128], lambda n, ct=ct: kT[:, ct, 0:n])], True,
                        lambda k, hd=hd: vt[:, k, hd * 64:hd * 64 + 64], 64, hp, evac, [m, mc, mqz[n]], forget=hd)
                    m = done[-1]

            weave(fox(0), chain(lambda: idle(1), lambda: fox(1)), chain(lambda: idle(2), lambda: fox(2)), chain(lambda: idle(3), lambda: fox(3)))
            mg1 = ts(DV, g1, mod1[:, 16:24], 1.0, None, ADD, None)
            run(proj(a["fx_wo"], gT, KT, D, (0, 1), residual(g1, mg1), now()))
            mlp("1", col("norm_mlp_g1", 0, 8), mod1, mod_stream(mod2, a["w_mod_2"], 6144, 8, col("b_mod_2", 0, 48), 6))
            norm_mod(x3, col("final_g", 0, 8), None, None, 7, now())
            cv = Carve()
            OD = cv(4096)
            od3 = OD.rearrange("p (k t) -> p k t", k=KT)
            BE, GG2, GCs, EG, NEG, EGL, EKS, BEK, NBE, TA, TB = [cv(64) for _ in range(11)]
            win = a["w_in_2"]
            start = now()
            mh = norm_mod(h3, col("g_mix_2", 0, 8), mod2[:, 8:16], mod2[:, 0:8], 7, start)
            m = small_tok(win[:, 4096:4128], 32, 4, mh)
            ba = BK[4][:, 0:128].rearrange("p (t h) -> p t h", t=4)
            m1 = act(v3(BE), ba[:, :, 0:16], ACT.Sigmoid, m, start)
            m2 = tt(DV, v3(TA), ba[:, :, 16:32], bc4(col("dt_bias_2", 0, 16)), ADD, m1, start)
            bfree[4] = [m2]
            m = act(TB, TA, ACT.Abs, m2, start)
            m = act(TB, TB, ACT.Exp, m, scale=-1.0)
            m = act(TB, TB, ACT.Ln, m, bias=1.0)
            m = stt(TA, TA, 0.0, TB, ALU.max, ADD, m)
            ea = mods[:, 185:201]
            me = act(ea, col("a_log_2", 0, 16), ACT.Exp, start)
            m = tt(DV, v3(TA), v3(TA), bc4(ea), MUL, me, m)
            mg = ts(DV, GG2, TA, -1.0, None, MUL, None, m)
            g3 = v3(GG2)
            bk5 = BK[5][:, :].rearrange("p (s t h) -> p s t h", s=8, t=4)
            m = mms([(BK[5][:, 0:32], C("incl"), g3[:, :, 0:8], True, True),
                     (BK[5][:, 32:64], C("inclR"), g3[:, :, 8:16], True, True),
                     (BK[5][:, 64:128], C("ones"), GG2, True, True)], mg, *bfree[5])
            gc3 = v3(GCs)
            m1 = act(gc3[:, :, 0:8], BK[5][:, 0:32].rearrange("p (t h) -> p t h", t=4), ACT.Copy, m, start)
            m1 = act(gc3[:, :, 8:16], BK[5][:, 32:64].rearrange("p (t h) -> p t h", t=4), ACT.Copy, m)
            m2 = act(EGL, BK[5][:, 64:128], ACT.Exp, m)
            m3 = tt(DV, EKS, BK[5][:, 64:128], GCs, SUB, m1, m2)
            bfree[5] = [m3]
            m3 = act(EKS, EKS, ACT.Exp, m3)
            m1 = act(EG, GCs, ACT.Exp)
            m = ts(DV, NEG, EG, -1.0, None, MUL, None, m1)
            m = tt(DV, BEK, BE, EKS, MUL, m3)
            mcol = [ts(DV, NBE, BE, -1.0, None, MUL, None), m3, m2]

            dsets = [[cv(512) for _ in range(9)] for _ in range(2)]
            dwork = [[cv(512) for _ in range(8)] + [cv(128) for _ in range(4)] for _ in range(2)]
            PB, t1 = cv(516), cv(512)
            RW = [cv(512) for _ in range(4)]
            dfetched = {}
            start = now()
            mz = GP(lambda e: e.memset(PB[:, 0:2], 0.0), start)
            mz = GP(lambda e: e.memset(PB[:, 514:516], 0.0), start)
            dprep, dused, ddone, dheaded = {}, {}, {}, {}
            dsm = cv(16)

            def dn_fetch(hd, since):
                cw = col("conv_w_2", 0, 120).rearrange("p (c j) -> p c j", c=24)
                src = [win[:, b0 + hd * 128:b0 + hd * 128 + 128].rearrange("(k p) n -> p k n", p=P) for b0 in (0, 1024, 2048, 3072)]
                sl = [load((0, (0, P), (8, 128), src[2 * i]), (1024, (0, P), (8, 128), src[2 * i + 1])) for i in range(2)]
                mlast, raw = None, []
                for i in range(4):
                    k, vs, tk = sl[i // 2]
                    b = i % 2
                    for q in range(4):
                        m = mms([(BK[b][:, :], vs[i % 2][:, kk, :], h3[:, kk, :], kk == 0, kk == 7) for kk in (2 * q, 2 * q + 1)],
                                tk, *bfree[b], mh)
                        if q < 3:
                            yield
                    if i % 2:
                        wfree[k] = [m]
                    if i == 3:
                        m = act(RW[3], BK[b][:, :], ACT.Copy, m, since)
                        bfree[b] = [m]
                    else:
                        m = act(PB[:, 2:514], BK[b][:, :], ACT.Copy, m, mlast, since)
                        bfree[b] = [m]
                        m = ts(DV, RW[i], PB[:, 0:512], cw[:, 8 * i + hd, 0:1], None, MUL, None, m, mz, since)
                        for j in range(1, 5):
                            m = stt(RW[i], PB[:, j:j + 512], cw[:, 8 * i + hd, j:j + 1], RW[i], MUL, ADD, m)
                        mlast = m
                    raw.append(m)
                    yield
                dfetched[hd] = raw

            def dn_prep(hd, since):
                qT_, kT_, Z_, Kt_, Vt_, KF, KB, QF, QB = dsets[hd % 2]
                raw = dfetched[hd]
                toks = []
                mq = act(qT_, RW[0], ACT.Silu, raw[0], since)
                mk = act(kT_, RW[1], ACT.Silu, raw[1], since)
                mv = act(t1, RW[2], ACT.Silu, raw[2], since)
                mzz = act(Z_, RW[3], ACT.Silu, raw[3], since)
                mn = []
                yield
                for dst, sq, g, b, m in ((qT_, RW[0], 128 ** -0.5, 0, mq), (kT_, RW[1], 1.0, 1, mk)):
                    m2 = act(sq, dst, ACT.Square, m)
                    m2 = mms([(BK[b][:, :], C("ones"), sq, True, True)], m2, *bfree[b])
                    m2 = ts(DV, sq, BK[b][:, :], 1e-6, None, ADD, None, m2)
                    bfree[b] = [m2]
                    mn.append(m2)
                yield
                for dst, sq, g, b, m in ((qT_, RW[0], 128 ** -0.5, 0, mq), (kT_, RW[1], 1.0, 1, mk)):
                    act(sq, sq, ACT.Ln, mn[b])
                for dst, sq, g, b, m in ((qT_, RW[0], 128 ** -0.5, 0, mq), (kT_, RW[1], 1.0, 1, mk)):
                    m2 = act(sq, sq, ACT.Exp, scale=-0.5)
                    mn[b] = stt(dst, dst, g, sq, MUL, MUL, m, m2)
                m = trs([(BK[0][:, c * 128:c * 128 + 128], t1[:, c * 128:c * 128 + 128]) for c in range(4)], mv, *bfree[0])
                m = act(Vt_, BK[0][:, :], ACT.Copy, m, since)
                bfree[0] = [m]
                toks.append(m)
                yield
                m = trs([(BK[1][:, c * 128:c * 128 + 128], kT_[:, c * 128:c * 128 + 128]) for c in range(4)], mn[1], *bfree[1])
                m = act(Kt_, BK[1][:, :], ACT.Copy, m, since)
                bfree[1] = [m]
                toks.append(m)
                mlast = [mn, m]
                yield
                q3 = lambda v: v.rearrange("p (c t) -> p c t", c=4)
                for lhs, rhs, df, db, mf, mb, b in ((kT_, kT_, KF, KB, "strict", "strictR", 0), (kT_, qT_, QF, QB, "incl", "inclR", 1)):
                    m = mms([(BK[b][:, c * 128:c * 128 + 128], lhs[:, c * 128:c * 128 + 128], rhs[:, c * 128:c * 128 + 128], True, True)
                             for c in range(4)], mlast, *bfree[b])
                    for d, mk in ((df, mf), (db, mb)):
                        m1 = tt(DV, q3(d), q3(BK[b][:, :]), C(mk).unsqueeze(1).broadcast_to([P, 4, 128]), MUL, m, since)
                    bfree[b] = [m1]
                    toks.append(m1)
                    yield
                dprep[hd] = [toks, mzz, mlast]
                dused[hd] = now()

            def dn_dir(hd, R):
                qT_, kT_, Z_, Kt_, Vt_, KF, KB, QF, QB = dsets[hd % 2]
                E_, NT, TT, TM, US, MT, RK, OO, SS, XS, VN, VS = dwork[R]
                KM, QM = (KB, QB) if R else (KF, QF)
                ba_, bb_, bc_ = (5, 6, 7) if R else (2, 3, 4)
                dh = 8 * R + hd
                c_ = lambda v, c: v3(v)[:, c, dh:dh + 1]
                q3 = lambda v: v.rearrange("p (c t) -> p c t", c=4)
                pm = [dprep[hd], mcol]
                before = [dheaded[hd - 1]] if hd else [start]
                m = mms([(BK[ba_][:, c * 128:c * 128 + 128], g3[:, c, dh:dh + 1].broadcast_to([P, 128]), C("inclR" if R else "incl"), True, True)
                         for c in range(4)], pm, *bfree[ba_])
                for c in range(4):
                    m1 = ts(DV, q3(E_)[:, c, :], BK[ba_][:, c * 128:c * 128 + 128], c_(GCs, c), 0.0, SUB, ALU.min, m, before)
                bfree[ba_] = [m1]
                m = act(E_, E_, ACT.Exp, m1)
                yield
                for c in range(4):
                    mn = stt(q3(NT)[:, c, :], q3(E_)[:, c, :], c_(NBE, c), q3(KM)[:, c, :], MUL, MUL, m, before)
                yield
                inv = invert(NT, TT, TM, US, MT, R, (ba_, bb_, bc_), 4, [before], mn)
                for _ in range(4):
                    next(inv)
                    yield
                mrk = tt(GP, RK, QM, E_, MUL, m, before, mn)
                yield from inv
                mt = inverse[-1]
                ms = GP(lambda e: e.memset(SS, 0.0), before)
                mvs = None
                for c in (range(3, -1, -1) if R else range(4)):
                    q = slice(c * 128, c * 128 + 128)
                    m = mms([(BK[ba_][:, 0:128], kT_[:, q], SS, True, True), (BK[ba_][:, 128:256], qT_[:, q], SS, True, True)],
                            ms, *bfree[ba_])
                    m1 = stt(XS, BK[ba_][:, 0:128], c_(NEG, c), Vt_[:, q], MUL, ADD, m, mvs)
                    mq = ts(DV, OO[:, q], BK[ba_][:, 128:256], c_(EG, c), None, MUL, None, m, before, ddone.get(hd - 1))
                    bfree[ba_] = [mq]
                    yield
                    m = mms([(BK[bb_][:, 0:128], TT[:, q], XS, True, True)], m1, mt, *bfree[bb_])
                    m2 = act(VN, BK[bb_][:, 0:128], ACT.Copy, m, mvs, scale=c_(BE, c))
                    m3 = act(VS, BK[bb_][:, 0:128], ACT.Copy, m, mvs, scale=c_(BEK, c))
                    bfree[bb_] = [m3]
                    yield
                    m = mms([(BK[bc_][:, 0:128], Kt_[:, q], VS, True, True)], m3, *bfree[bc_])
                    mvs = mms([(BK[bc_][:, 128:256], RK[:, q], VN, True, True)], m2, mrk)
                    ms = stt(SS, SS, c_(EGL, c), BK[bc_][:, 0:128], MUL, ADD, mvs)
                    mo = tt(DV, OO[:, q], OO[:, q], BK[bc_][:, 128:256], ADD, mvs, mq)
                    bfree[bc_] = [mo]
                    yield
                dout.append(mo)

            dout = []

            def dn_head(hd):
                qT_, kT_, Z_, Kt_, Vt_, KF, KB, QF, QB = dsets[hd % 2]
                fs = [dn_dir(hd, False), dn_dir(hd, True)]
                while fs:
                    for f in list(fs):
                        if next(f, StopIteration) is StopIteration:
                            fs.remove(f)
                    yield
                dheaded[hd] = now()

            def dn_post(hd):
                qT_, kT_, Z_, Kt_, Vt_, KF, KB, QF, QB = dsets[hd % 2]
                OO, OB = dwork[0][7], dwork[1][7]
                sq, sm_ = KF, dsm
                m = tt(GP, OO, OO, OB, ADD, dheaded[hd])
                for c in range(4):
                    m1 = act(sq[:, 0:128], OO[:, c * 128:c * 128 + 128], ACT.Square, m, accum=sm_[:, c:c + 1])
                m1 = ts(DV, sm_[:, 0:4], sm_[:, 0:4], 1.0 / 128, 1e-6, MUL, ADD, m1)
                m1 = rroot(sm_[:, 0:4], m1)
                for c in range(4):
                    m = ts(DV, OO[:, c * 128:c * 128 + 128], OO[:, c * 128:c * 128 + 128], sm_[:, c:c + 1], None, MUL, None, m1)
                yield
                m = trs([(BK[0][:, c * 128:c * 128 + 128], OO[:, c * 128:c * 128 + 128]) for c in range(4)], m, *bfree[0])
                m = stt(od3[:, hd, :], BK[0][:, :], col("dn_o_gain_2"), Z_, MUL, MUL, m)
                bfree[0] = [m]
                ddone[hd] = now()
                yield

            run(dn_fetch(0, start))
            run(dn_prep(0, start))
            run(dn_fetch(1, [start, dused[0]]))
            for hd in range(8):
                beside = [lambda: idle(2), (lambda hd=hd: dn_post(hd - 1)) if hd else (lambda: idle(2))]
                if hd < 7:
                    beside.append(lambda hd=hd: dn_prep(hd + 1, [dused[hd]] + ([dheaded[hd - 1], ddone[hd - 1]] if hd else [])))
                if hd < 6:
                    beside.append(lambda: idle(0))
                    beside.append(lambda hd=hd: dn_fetch(hd + 2, [dused[hd + 1]]))
                weave(dn_head(hd), chain(*beside))
            run(dn_post(7))
            cv = Carve()
            OD, ME, GA = cv(4096), cv(4096), cv(4096)
            me3, ga3 = [v.rearrange("p (k t) -> p k t", k=KT) for v in (ME, GA)]
            start = now()
            gm = []

            def gate(j, b, m):
                m = act(ga3[:, j, :], BK[b][:, :], ACT.Sigmoid, m, start)
                gm[:] = [m]
                return m

            run(proj(win[:, 4960:5984], h3, KT, D, (0, 1), gate, mh))
            run(proj(a["w_o_dn_2"], od3, KT, D, (2, 3),
                     lambda j, b, m: tt(DV, me3[:, j, :], BK[b][:, :], ga3[:, j, :], MUL, m, gm, start), start))

            OM = OD
            om3 = OM.rearrange("p (k t) -> p k t", k=KT)
            start = now()
            CQ, CK, KR, CO, SI, R0, R1 = cv(2048), cv(1024), cv(512), cv(512), cv(512), cv(512), cv(512)
            cq3, ck3 = CQ.rearrange("p (k t) -> p k t", k=4), CK.rearrange("p (k t) -> p k t", k=2)
            lw_ = []
            for n in range(2):
                lw_.append([cv(512) for _ in range(4)] + [None, cv(512), cv(2048), cv(16), SM[:, 1024 + 128 * n:1152 + 128 * n]])
            s_pos = new_sem("s_pos")
            pi = R0[0:64, :].bitcast(I32)
            mp = SY.dma(s_pos, 16, lambda e: e.dma_start(pi, a["pos"].broadcast_to([64, 512])), start)
            ang, n_ = R1[0:64, :], SI[0:64, :]
            m = DV(lambda e: e.tensor_copy(ang, pi), mp, start)
            m = ts(DV, ang, ang, C("iota")[0:64, 64:65], None, MUL, None)
            MAGIC = 12582912.0
            m = ts(DV, n_, ang, float(1 / (2 * np.pi)), MAGIC, MUL, ADD)
            m = ts(DV, n_, n_, -MAGIC, None, ADD, None)
            c1 = 6.28125
            c2 = float(np.float32(int((2 * np.pi - c1) * 2 ** 20) / 2 ** 20))
            c3 = float(np.float32(2 * np.pi - c1 - c2))
            for c in (c1, c2, c3):
                m = stt(ang, n_, -c, ang, MUL, ADD)
            m = ts(DV, ang, ang, 3.1415925, -3.1415925, ALU.min, ALU.max)
            ms = act(SI[0:64, :], ang, ACT.Sin, m)
            mc = act(CO[0:64, :], ang, ACT.Sin, m, scale=0.5)
            m = tt(DV, CO[0:64, :], CO[0:64, :], CO[0:64, :], MUL, mc)
            mcs = [ts(DV, CO[0:64, :], CO[0:64, :], -2.0, 1.0, MUL, ADD), ms]

            run(proj(win[:, 4128:4640], h3, KT, 512, (0, 1), lambda j, b, m: act(cq3[:, j, :], BK[b][:, :], ACT.Copy, m, start), mh))
            run(proj(win[:, 4640:4896], h3, KT, 256, (0, 1), lambda j, b, m: act(ck3[:, j, :], BK[b][:, :], ACT.Copy, m, start), mh))

            def rope(dst, b, m, tmp, b2, *marks):
                m1 = act(tmp[0:64, :], BK[b][0:64, :], ACT.Copy, m, *marks)
                bfree[b] = [m1]
                m2 = mms([(BK[b2][0:64, :], C("perm")[0:64, 0:64], tmp[0:64, :], True, True)], m1, *bfree[b2])
                m3 = tt(DV, dst, BK[b2][0:64, :], SI[0:64, :], MUL, m2, mcs, *marks)
                bfree[b2] = [m3]
                m4 = tt(DV, tmp[0:64, :], tmp[0:64, :], CO[0:64, :], MUL, m2, m3)
                return tt(DV, dst, dst, tmp[0:64, :], ADD, m4)

            k, (v,), tk = load((0, (0, P), (8, 64), win[:, 4896:4960].rearrange("(k p) n -> p k n", p=P)))
            m = mms([(BK[2][0:64, :], v[:, kk, :], h3[:, kk, :], kk == 0, kk == 7) for kk in range(8)], tk, mh, *bfree[2])
            wfree[k] = [m]
            mkr = rope(KR[0:64, :], 2, m, R0, 3, mp, start, now())
            for src, nk, g, inv in ((cq3, 4, "q_gain_2", 1.0 / 512), (ck3, 2, "kv_gain_2", 1.0 / 256)):
                m = rms_rstd(src, nk, inv, 1e-6, 4, now(), o=R0)
                for j in range(nk):
                    m = stt(src[:, j, :], src[:, j, :], col(g, j), R0, MUL, MUL, m)
            mlat = m
            start = now()

            mzr = [GP(lambda e, z=z: e.memset(z[64:128, :], 0.0), start) for z in (KR, lw_[0][1], lw_[1][1])]

            def mla(par):
                Qn, Qr, Kn, Vh, _, S, PT, sm_, DG = lw_[par]
                b0 = 4 * par
                for hh in range(4):
                    hd = 2 * hh + par
                    since = now()
                    k, (wq, wkv), tk = load(
                        (0, (0, P), (4, 192), a["w_uq_2"][:, hd * 192:hd * 192 + 192].rearrange("(k p) n -> p k n", p=P)),
                        (768, (0, P), (2, 256), a["w_ukv_2"][:, hd * 256:hd * 256 + 256].rearrange("(k p) n -> p k n", p=P)))
                    m = mms([(BK[b0][0:64, :], wq[:, kk, 128:192], cq3[:, kk, :], kk == 0, kk == 3) for kk in range(4)],
                            tk, mlat, *bfree[b0], start)
                    mr = rope(Qr[0:64, :], b0, m, S, b0 + 1, since)
                    yield
                    m = mms([(BK[b0 + 2][:, :], wq[:, kk, 0:128], cq3[:, kk, :], kk == 0, kk == 3) for kk in range(4)],
                            *bfree[b0 + 2])
                    m1 = act(Qn, BK[b0 + 2][:, :], ACT.Copy, m, since)
                    bfree[b0 + 2] = [m1]
                    yield
                    m = mms([(BK[b0 + 3][:, :], wkv[:, kk, 0:128], ck3[:, kk, :], kk == 0, kk == 1) for kk in range(2)],
                            *bfree[b0 + 3])
                    m2 = act(Kn, BK[b0 + 3][:, :], ACT.Copy, m, since)
                    bfree[b0 + 3] = [m2]
                    yield
                    m = mms([(BK[b0][:, t * 128:t * 128 + 128], ck3[:, kk, t * 128:t * 128 + 128], wkv[:, kk, 128:256], kk == 0, kk == 1)
                             for t in range(4) for kk in range(2)], *bfree[b0])
                    wfree[k] = [m]
                    m3 = act(Vh, BK[b0][:, :], ACT.Copy, m, since)
                    bfree[b0] = [m3]
                    yield
                    yield from attention(
                        (b0, b0 + 1, b0 + 2), (None, S, PT, sm_, DG),
                        [(lambda qt: Qn[:, qt * 128:qt * 128 + 128], lambda n: Kn[:, 0:n]),
                         (lambda qt: Qr[:, qt * 128:qt * 128 + 128], lambda n: KR[:, 0:n])], False,
                        lambda kt: Vh[:, kt * 128:kt * 128 + 128], 128, slice(0, P),
                        lambda m: act(om3[:, hd, :], BK[b0 + 2][:, :], ACT.Copy, m), [mr, m1, m2, m3, mkr, mzr, since],
                        scale=192 ** -0.5)

            weave(mla(0), chain(lambda: idle(4), lambda: mla(1)))
            start = now()
            run(proj(win[:, 5984:7008], h3, KT, D, (0, 1), gate, mh))
            TG = lw_[0][6]
            tgf = [[], []]

            def merge(j, b, m):
                t_ = TG[:, 512 * (j % 2):512 * (j % 2) + 512]
                m1 = tt(DV, t_, BK[b][:, :], ga3[:, j, :], MUL, m, gm, start, *tgf[j % 2])
                tgf[j % 2] = [tt(GP, me3[:, j, :], me3[:, j, :], t_, ADD, m1)]
                return m1

            run(proj(a["w_o_mla_2"], om3, KT, D, (2, 3), merge, start))
            run(proj(a["w_out_2"], me3, KT, D, (0, 1), residual(mod2[:, 16:24]), now()))
            cv = Carve()
            HT, SEL, XE, YE = cv(4096), cv(4096), cv(8192), cv(8192)
            RKs, AFT = cv(512), cv(512)
            AF, RT, s4, s8 = cv(64), cv(64), cv(16), cv(16)
            ht3 = HT.rearrange("p (t d) -> p t d", t=4)
            sel3 = SEL.rearrange("p (t s) -> p t s", t=4)
            xe3 = XE.rearrange("p (k s) -> p k s", k=KT)
            ye3 = YE.rearrange("p (e d) -> p e d", e=8)
            start = now()
            mh = norm_mod(h3, col("g_ffn_2", 0, 8), mod2[:, 32:40], mod2[:, 24:32], 7, start)
            WKb, SMb, PAIR = YE[0:16, 0:512], YE[0:16, 512:1024], YE[0:16, 1024:2048]
            s_pair = new_sem("s_pair")
            mpair = SY.dma(s_pair, 16, lambda e: e.dma_start(PAIR, a["pair"]), start)
            m = small_tok(a["w_router_2"], 16, 0, mh)
            lg, af3 = v3(BK[0][:, 0:64]), v3(AF)
            b16 = lambda v: v.unsqueeze(2).broadcast_to([P, 4, 16])
            m = DV(lambda e: e.tensor_reduce(s4[:, 0:4], lg, AX, ALU.max), m, start)
            m = tt(DV, af3, lg, b16(s4[:, 0:4]), SUB)
            bfree[0] = [m]
            m = act(AF, AF, ACT.Exp, m)
            m = DV(lambda e: e.tensor_reduce(s4[:, 4:8], af3, AX, ADD), m)
            m = DV(lambda e: e.reciprocal(s4[:, 4:8], s4[:, 4:8]))
            m = tt(DV, af3, af3, b16(s4[:, 4:8]), MUL)
            m = trs([(BK[1][0:16, t * 128:t * 128 + 128], af3[:, t, :]) for t in range(4)], m, *bfree[1])
            ma = act(AFT[0:16, :], BK[1][0:16, :], ACT.Copy, m, start)
            bfree[1] = [ma]
            mwk = act(WKb, AFT[0:16, :], ACT.Copy)
            for k in range(KT):
                b = 3 + k % 2
                m = trs([(BK[b][:, t * 128:t * 128 + 128], h3[:, k, t * 128:t * 128 + 128]) for t in range(4)], mh, *bfree[b])
                mt = act(ht3[:, :, k * 128:k * 128 + 128], BK[b][:, :].rearrange("p (t d) -> p t d", t=4), ACT.Copy, m, start)
                bfree[b] = [mt]
            DV.wait(mwk)
            for _ in range(8):
                DV(lambda e: e.max(s8[0:16, 0:8], WKb))
                m = DV(lambda e: e.match_replace(WKb, s8[0:16, 0:8], WKb, -1.0))
            ts(DV, SMb, WKb, 0.0, None, ALU.is_lt, None)
            DV(lambda e: e.tensor_tensor_scan(WKb, SMb, SMb, 0.0, ADD, ALU.max))
            tt(DV, WKb, WKb, SMb, MUL)
            mr = ts(DV, RKs[0:16, :], WKb, -1.0, None, ADD, None)
            m = trs([(BK[2][:, 16 * t:16 * t + 16], RKs[0:16, t * 128:t * 128 + 128]) for t in range(4)], mr, *bfree[2])
            m = act(RT, BK[2][:, 0:64], ACT.Copy, m, start)
            bfree[2] = [m]
            for t in range(4):
                ms = DV(lambda e, t=t: e.tensor_tensor(
                    sel3[:, t, :].rearrange("p (e s) -> p e s", e=16),
                    v3(RT)[:, t, :].unsqueeze(2).broadcast_to([P, 16, 64]),
                    C("iota", 64).unsqueeze(1).broadcast_to([P, 16, 64]), ALU.is_equal), m, start)
            mx = []
            for k in range(KT):
                for hf in range(2):
                    b = (2 * k + hf) % 4
                    m = mms([(BK[b][:, :], ht3[:, t, k * 128:k * 128 + 128], sel3[:, t, hf * 512:hf * 512 + 512], t == 0, t == 3)
                             for t in range(4)], ms, mt, *bfree[b])
                    m = act(xe3[:, k, hf * 512:hf * 512 + 512], BK[b][:, :], ACT.Copy, m, start)
                    bfree[b] = [m]
                    mx.append(m)
            dist = SEL.rearrange("p (e t) -> p e t", e=8)
            AB = HT[:, 0:1024]
            mdist = []
            gathered = now()
            for pr in range(8):
                m = mms([(BK[4][:, :], PAIR[:, pr * 128:pr * 128 + 128], RKs[0:16, :], True, True)], mr, mpair, *bfree[4])
                m1 = mms([(BK[5][:, :], PAIR[:, pr * 128:pr * 128 + 128], AFT[0:16, :], True, True)], ma, *bfree[5])
                ab = AB[:, 512 * (pr % 2):512 * (pr % 2) + 512]
                m1 = act(ab, BK[5][:, :], ACT.Copy, m1, gathered, mdist[-2:])
                bfree[5] = [m1]
                m = stt(dist[:, pr, :], BK[4][:, :], C("iota")[:, 65:66], ab, ALU.is_equal, MUL, m, m1, gathered)
                bfree[4] = [m]
                mdist.append(m)
            ready_e = now()
            SG, HI, HIT = HT[:, 0:1024], HT[:, 1024:2048], HT[:, 2048:4096]
            st = {}

            def ffn(name, pr, banks, lhs, *marks):
                for g in range(4):
                    sl = [load((0, (0, P), (2, 1024), a[name][2 * pr + e, g * 256:g * 256 + 256, :].rearrange("(k p) n -> p k n", p=P)))
                          for e in range(2)]
                    m = mms([(BK[banks[hf]][64 * e:64 * e + 64, :], lhs(2 * g + j, e), sl[e][1][0][:, j, hf * 512:hf * 512 + 512],
                              g == 0 and j == 0, g == 3 and j == 1) for j in range(2) for hf in range(2) for e in range(2)],
                            sl[0][2], sl[1][2], *bfree[banks[0]], *bfree[banks[1]], *marks)
                    wfree[sl[0][0]] = [m]
                    wfree[sl[1][0]] = [m]
                return m

            def gate_of(pr):
                m = ffn("w_gate_2", pr, (0, 1), lambda k, e: xe3[:, k, (2 * pr + e) * 64:(2 * pr + e) * 64 + 64], mx)
                for hf in range(2):
                    m1 = act(SG[:, hf * 512:hf * 512 + 512], BK[hf][:, :], ACT.Silu, m, ready_e, st.get("hi"))
                    bfree[hf] = [m1]
                st["sg"] = m1

            def up_of(pr):
                m = ffn("w_up_2", pr, (2, 3), lambda k, e: xe3[:, k, (2 * pr + e) * 64:(2 * pr + e) * 64 + 64], mx)
                for hf in range(2):
                    m1 = tt(DV, HI[:, hf * 512:hf * 512 + 512], BK[2 + hf][:, :], SG[:, hf * 512:hf * 512 + 512], MUL,
                            m, st["sg"], ready_e, st.get("tr"))
                    bfree[2 + hf] = [m1]
                st["hi"] = m1

            def down_of(pr):
                hit = HIT[:, 0:1024].rearrange("p (f s) -> p f s", f=8)
                mm_ = []
                for hf in range(2):
                    b = 6 + hf
                    m = trs([(BK[b][:, f * 128:f * 128 + 128], HI[:, hf * 512 + f * 128:hf * 512 + f * 128 + 128]) for f in range(4)],
                            st["hi"], *bfree[b])
                    m1 = act(hit[:, 4 * hf:4 * hf + 4, :], BK[b][:, :].rearrange("p (f s) -> p f s", f=4), ACT.Copy, m, st.get("dn"))
                    bfree[b] = [m1]
                    mm_.append(m1)
                st["tr"] = m
                m = ffn("w_down_2", pr, (4, 5), lambda f, e: hit[:, f, 64 * e:64 * e + 64], mm_)
                st["dn"] = m
                for hf in range(2):
                    m1 = act(ye3[:, pr, hf * 512:hf * 512 + 512], BK[4 + hf][:, :], ACT.Copy, m)
                    bfree[4 + hf] = [m1]
                st["ye"] = m1

            gate_of(0)
            up_of(0)
            for pr in range(8):
                if pr < 7:
                    gate_of(pr + 1)
                down_of(pr)
                if pr < 7:
                    up_of(pr + 1)
            evac = residual(mod2[:, 40:48])
            for k in range(KT):
                b = k % 4
                m = mms([(BK[b][:, :], ye3[:, pr, k * 128:k * 128 + 128], dist[:, pr, :], pr == 0, pr == 7) for pr in range(8)],
                        st["ye"], mdist, *bfree[b])
                bfree[b] = [evac(k, b, m)]
            mf = norm_mod(x3, col("g_final_2", 0, 8), None, None, 7, now())
            ot = A[:, 0:4096].rearrange("p (t d) -> p t d", t=4)
            mo = now()
            for k in range(KT):
                b = k % 4
                m = trs([(BK[b][:, t * 128:t * 128 + 128], x3[:, k, t * 128:t * 128 + 128]) for t in range(4)], mf[k], *bfree[b])
                m = act(ot[:, :, k * 128:k * 128 + 128], BK[b][:, :].rearrange("p (t d) -> p t d", t=4), ACT.Copy, m, mo)
                bfree[b] = [m]
            s_out = new_sem("s_out")
            m = SY.dma(s_out, 16, lambda e: e.dma_start(out.rearrange("(t p) d -> p t d", p=P), ot), m)
            SY.wait(m)

        body()
        block = ctx.enter_context(nc.Block())

        @block.sync
        def _(eng):
            SY.play(eng)

        @block.scalar
        def _(eng):
            AC.play(eng)

        @block.vector
        def _(eng):
            DV.play(eng)

        @block.gpsimd
        def _(eng):
            GP.play(eng)

        @block.tensor
        def _(eng):
            PE.play(eng)


_WHOLE = ["kv_mod_w", "kv_w"]
_FIRST = ["rw_wr", "rw_wk", "rw_wv", "rw_wo", "rw_w1", "rw_w2", "rw_a1", "rw_a2", "rw_g1", "rw_g2", "fx_wqg", "fx_wo",
          "w_mod_2", "w_in_2", "w_uq_2", "w_ukv_2", "w_o_dn_2", "w_o_mla_2", "w_out_2", "w_router_2",
          "w_gate_2", "w_up_2", "w_down_2"]
_LAYERS = ["mod_w", "mlp_up", "mlp_down"]


def _columns(inputs):
    g = {k: np.asarray(v) for k, v in inputs.items()}

    def by128(v):
        return v.reshape(-1, 128).T

    def tiled(v, n):
        return np.tile(v.reshape(-1), n).reshape(-1, 128).T

    def rows(v):
        return np.tile(v.reshape(1, -1), (128, 1))

    out = []
    for name, w in VECS:
        if name in ("mod_b0", "mod_b1", "norm_mix_g0", "norm_mix_g1", "norm_mlp_g0", "norm_mlp_g1"):
            v = by128(g[name[:-1]][int(name[-1])])
        elif name == "conv_w_2":
            v = g[name][0].reshape(5, 24, 128).transpose(2, 1, 0).reshape(128, 120)
        elif name in ("kv_kg", "fx_qg"):
            v = tiled(g[name], 2)
        elif name in ("kv_fb", "a_log_2", "dt_bias_2"):
            v = rows(g[name])
        else:
            v = by128(g[name])
        assert v.shape == (128, w), (name, v.shape)
        out.append(v)
    return np.ascontiguousarray(np.concatenate(out, axis=1))


def arrays_of(inputs):
    g = {k: np.asarray(v) for k, v in inputs.items()}
    arr = {"x": g["x"][0], "pos": g["positions_2"], "const": _CARR, "pair": _PAIR, "cols": _columns(inputs)}
    for n in _WHOLE:
        arr[n] = g[n]
    for n in _FIRST:
        arr[n] = g[n][0]
    for n in _LAYERS:
        arr[n + "0"], arr[n + "1"] = g[n][0], g[n][1]
    return {f"in_{n}": np.ascontiguousarray(v) for n, v in arr.items()}


def kernel(**inputs):
    import concourse.bacc as _bacc
    from concourse.bass_utils import run_bass_kernel_spmd as _run

    nc = _bacc.Bacc("TRN2", target_bir_lowering=False, num_devices=1)
    arrays = arrays_of(inputs)
    a = {n[3:]: nc.dram_tensor(n, v.shape, mybir.dt.from_np(v.dtype), kind="ExternalInput").ap()
         for n, v in arrays.items()}
    out = nc.dram_tensor("out_0", (T, D), F32, kind="ExternalOutput").ap()
    program(nc, a, out)
    r = _run(nc, [arrays], core_ids=[0])
    return r.results[0]["out_0"].reshape(1, T, D)
```
